# Optimizing a Trainium2 kernel written in Bass

```python
import math
import jax
import jax.numpy as jnp
from jax import lax
import numpy as np

D_MODEL = 1024
BATCH = 1
SEQ = 128
DEPTH = 2
DEC_BATCH = 1
DEC_SEQ = 512
PAST_LEN = 128

GRID_W = 64
Q_BLOCK = 128
EPS = 1e-6
ROPE_THETA = 10000.0
H_A = 4
DH_A = 32
H_B = 4
DH_B = 64
WIN_R = 8
WIN_C = 16
H_C = 4
Q_LORA = 256
KV_LORA = 128
NOPE_C = 32
ROPE_C = 32
DV_C = 64
CONV_CH = 256
CONV_K = 31
N_BRANCH = 4
N_GROUPS = 4
EXPERTS_PER_GROUP = 4
N_EXPERTS = 16
TOP_K = 2
D_EXPERT = 256

A_QK = H_A * 2 * DH_A
A_V = H_A * 2 * DH_A
B_W = H_B * DH_B
IN_SIZES = (A_QK, A_QK, A_V, B_W, B_W, B_W, Q_LORA, KV_LORA, ROPE_C, 2 * CONV_CH)
IN_COLS = 2 * A_QK + A_V + 3 * B_W + Q_LORA + KV_LORA + ROPE_C + 2 * CONV_CH

kernel_name = 'hybrid_diffusion_prefix_step'

def _in_split_points():
    pts, acc = [], 0
    for sz in IN_SIZES[:-1]:
        acc += sz
        pts.append(acc)
    return pts

def rms_norm(x, g):
    xf = x.astype(jnp.float32)
    y = xf * lax.rsqrt(jnp.mean(xf * xf, axis=-1, keepdims=True) + EPS)
    return (y * g.astype(jnp.float32)).astype(x.dtype)

def layer_norm(x, g, b):
    xf = x.astype(jnp.float32)
    mu = jnp.mean(xf, axis=-1, keepdims=True)
    var = jnp.mean(jnp.square(xf - mu), axis=-1, keepdims=True)
    y = (xf - mu) * lax.rsqrt(var + EPS)
    return (y * g.astype(jnp.float32) + b.astype(jnp.float32)).astype(x.dtype)

def rope2d_tables(n_tok, dim):
    h = dim // 4
    t = jnp.arange(n_tok, dtype=jnp.int32)
    rows = (t // GRID_W).astype(jnp.float32)
    cols = (t % GRID_W).astype(jnp.float32)
    inv = ROPE_THETA ** (-jnp.arange(h, dtype=jnp.float32) / h)
    ar = rows[:, None] * inv[None, :]
    ac = cols[:, None] * inv[None, :]
    ang = jnp.concatenate([ar, ar, ac, ac], axis=-1)
    return jnp.cos(ang), jnp.sin(ang)

def apply_rope2d(x, cos, sin):
    h = x.shape[-1] // 4
    xs = x.reshape(x.shape[:-1] + (2, 2, h))
    rot = jnp.stack([-xs[..., 1, :], xs[..., 0, :]], axis=-2).reshape(x.shape)
    out = x.astype(jnp.float32) * cos[:, None, :] + rot.astype(jnp.float32) * sin[:, None, :]
    return out.astype(x.dtype)

def map_query_blocks(fn, q):
    b, s = q.shape[:2]
    nb = s // Q_BLOCK
    qb = jnp.moveaxis(q.reshape((b, nb, Q_BLOCK) + q.shape[2:]), 1, 0)
    out = jnp.moveaxis(lax.map(fn, qb), 0, 1)
    return out.reshape((b, s) + out.shape[3:])

def softmax_attn(q, k, v, scale):
    s = jnp.einsum('bqhd,bkhd->bhqk', q, k).astype(jnp.float32) * scale
    p = jax.nn.softmax(s, axis=-1).astype(v.dtype)
    return jnp.einsum('bhqk,bkhe->bqhe', p, v)

def diff_attn(q, k, v, lam, scale):
    s = jnp.einsum('bqhmd,bkhmd->bhmqk', q, k).astype(jnp.float32) * scale
    p = jax.nn.softmax(s, axis=-1)
    w = (p[:, :, 0] - lam * p[:, :, 1]).astype(v.dtype)
    return jnp.einsum('bhqk,bkhe->bqhe', w, v)

def diff_lambda(lam_vecs, layer):
    lam_init = 0.8 - 0.6 * math.exp(-0.3 * layer)
    lv = lam_vecs.astype(jnp.float32)
    lam = jnp.exp(jnp.sum(lv[0] * lv[1])) - jnp.exp(jnp.sum(lv[2] * lv[3])) + lam_init
    return lam, lam_init

def neighborhood_attn(q, k, v, ck, cv, rpb):
    b, s, nh, d = q.shape
    rows = s // GRID_W
    kr = min(WIN_R, rows)
    n_cb = GRID_W // WIN_C
    kb_w = 2 * WIN_C
    qcol = np.arange(GRID_W).reshape(n_cb, WIN_C)
    kstart = np.clip(np.arange(n_cb) * WIN_C - WIN_C // 2, 0, GRID_W - kb_w)
    kcols = (kstart[:, None] + np.arange(kb_w)).astype(np.int32)
    cstart = np.clip(qcol - WIN_C // 2, 0, GRID_W - WIN_C)
    kc = kcols[:, None, :]
    col_mask = (kc >= cstart[..., None]) & (kc < cstart[..., None] + WIN_C)
    col_idx = np.clip(kc - qcol[..., None] + WIN_C - 1, 0, 2 * WIN_C - 2).astype(np.int32)
    mask = jnp.asarray(np.broadcast_to(col_mask[:, :, None, :], (n_cb, WIN_C, kr, kb_w)).reshape(n_cb, WIN_C, kr * kb_w))
    qg = q.reshape(b, rows, GRID_W, nh, d)
    kg = k.reshape(b, rows, GRID_W, nh, d)
    vg = v.reshape(b, rows, GRID_W, nh, d)
    n_ctx = ck.shape[1]
    scale = d ** -0.5

    def row_fn(r):
        rs = jnp.clip(r - kr // 2, 0, rows - kr)
        qr = lax.dynamic_index_in_dim(qg, r, axis=1, keepdims=False).reshape(b, n_cb, WIN_C, nh, d)
        kw = lax.dynamic_slice_in_dim(kg, rs, kr, axis=1)[:, :, kcols]
        vw = lax.dynamic_slice_in_dim(vg, rs, kr, axis=1)[:, :, kcols]
        kw = jnp.moveaxis(kw, 2, 1).reshape(b, n_cb, kr * kb_w, nh, d)
        vw = jnp.moveaxis(vw, 2, 1).reshape(b, n_cb, kr * kb_w, nh, d)
        row_idx = rs + jnp.arange(kr) - r + WIN_R - 1
        bias = rpb[:, row_idx[None, None, :, None], col_idx[:, :, None, :]]
        bias = bias.reshape(nh, n_cb, WIN_C, kr * kb_w).astype(jnp.float32)
        s_w = jnp.einsum('bjqhd,bjkhd->bhjqk', qr, kw).astype(jnp.float32) * scale + bias
        s_w = jnp.where(mask, s_w, -jnp.inf)
        s_c = jnp.einsum('bjqhd,bkhd->bhjqk', qr, ck).astype(jnp.float32) * scale
        p = jax.nn.softmax(jnp.concatenate([s_c, s_w], axis=-1), axis=-1).astype(v.dtype)
        o = (jnp.einsum('bhjqk,bkhd->bjqhd', p[..., :n_ctx], cv)
             + jnp.einsum('bhjqk,bjkhd->bjqhd', p[..., n_ctx:], vw))
        return o.reshape(b, GRID_W, nh, d)

    out = lax.map(row_fn, jnp.arange(rows))
    return jnp.moveaxis(out, 0, 1).reshape(b, s, nh, d)

def mla_keys(ckv_n, krope, wukv):
    b, t, _ = ckv_n.shape
    kv = (ckv_n @ wukv).reshape(b, t, H_C, NOPE_C + DV_C)
    k = jnp.concatenate([kv[..., :NOPE_C], jnp.broadcast_to(krope[:, :, None, :], (b, t, H_C, ROPE_C))], axis=-1)
    return k, kv[..., NOPE_C:]

def conformer_conv(u, lp):
    a, g = jnp.split(u, 2, axis=-1)
    z = a * jax.nn.sigmoid(g)
    w = lp['d_conv_w'].astype(z.dtype)[:, None, :]
    z = lax.conv_general_dilated(z, w, (1,), [(CONV_K // 2, CONV_K // 2)],
                                 dimension_numbers=('NWC', 'WIO', 'NWC'),
                                 feature_group_count=CONV_CH) + lp['d_conv_b']
    z = jax.nn.silu(layer_norm(z, lp['d_ln_g'], lp['d_ln_b']))
    return z @ lp['d_wo']

def hier_moe(h, lp):
    b, s, _ = h.shape
    lg = (h @ lp['moe_w_group'] + lp['moe_b_group']).astype(jnp.float32)
    pg = jax.nn.softmax(lg, axis=-1)
    gi = jnp.argmax(lg, axis=-1)
    gw = jnp.max(pg, axis=-1, keepdims=True)
    le = (h @ lp['moe_w_expert'] + lp['moe_b_expert']).astype(jnp.float32)
    le = le.reshape(b, s, N_GROUPS, EXPERTS_PER_GROUP)
    le_sel = jnp.einsum('bsg,bsge->bse', jax.nn.one_hot(gi, N_GROUPS, dtype=jnp.float32), le)
    tv, ti = lax.top_k(le_sel, TOP_K)
    tw = jax.nn.softmax(tv, axis=-1) * gw
    eid = gi[..., None] * EXPERTS_PER_GROUP + ti
    dense_w = jnp.sum(jax.nn.one_hot(eid, N_EXPERTS, dtype=jnp.float32) * tw[..., None], axis=-2)
    hid = jnp.einsum('bsd,edf->bsef', h, lp['moe_w1'])
    gate, up = jnp.split(hid, 2, axis=-1)
    act = jax.nn.silu(gate) * up * dense_w[..., None].astype(h.dtype)
    return jnp.einsum('bsef,efd->bsd', act, lp['moe_w2'])

def mixers(h, lp, layer, ctx):
    b, s, _ = h.shape
    aq, ak, av, bq, bk, bv, cq, ckv, ckr, du = jnp.split(h @ lp['w_in'], _in_split_points(), axis=-1)
    aq = aq.reshape(b, s, H_A, 2, DH_A)
    ak = ak.reshape(b, s, H_A, 2 * DH_A)
    av = av.reshape(b, s, H_A, 2 * DH_A)
    bq = bq.reshape(b, s, H_B, DH_B)
    bk = bk.reshape(b, s, H_B, DH_B)
    bv = bv.reshape(b, s, H_B, DH_B)
    qc = (rms_norm(cq, lp['c_q_norm_g']) @ lp['c_wuq']).reshape(b, s, H_C, NOPE_C + ROPE_C)
    ckv = rms_norm(ckv, lp['c_kv_norm_g'])
    own = (ak, av, bk, bv, ckv, ckr)
    lam, lam_init = diff_lambda(lp['a_lambda'], layer)
    sa = DH_A ** -0.5
    sb = DH_B ** -0.5
    sc = (NOPE_C + ROPE_C) ** -0.5
    if ctx is None:
        ka = ak.reshape(b, s, H_A, 2, DH_A)
        va = av
        ob = map_query_blocks(lambda q: softmax_attn(q, bk, bv, sb), bq)
        kc, vc = mla_keys(ckv, ckr, lp['c_wukv'])
    else:
        a_k_c, a_v_c, b_k_c, b_v_c, c_kv_c, c_kr_c = ctx
        cos_a, sin_a = rope2d_tables(s, DH_A)
        aq = apply_rope2d(aq.reshape(b, s, 2 * H_A, DH_A), cos_a, sin_a).reshape(b, s, H_A, 2, DH_A)
        ak_rot = apply_rope2d(ak.reshape(b, s, 2 * H_A, DH_A), cos_a, sin_a).reshape(b, s, H_A, 2 * DH_A)
        ka = jnp.concatenate([a_k_c, ak_rot], axis=1).reshape(b, -1, H_A, 2, DH_A)
        va = jnp.concatenate([a_v_c, av], axis=1)
        ob = neighborhood_attn(bq, bk, bv, b_k_c, b_v_c, lp['b_rpb'])
        cos_c, sin_c = rope2d_tables(s, ROPE_C)
        qc = jnp.concatenate([qc[..., :NOPE_C], apply_rope2d(qc[..., NOPE_C:], cos_c, sin_c)], axis=-1)
        kr_lat = apply_rope2d(ckr[:, :, None, :], cos_c, sin_c)[:, :, 0, :]
        kc_ctx, vc_ctx = mla_keys(c_kv_c, c_kr_c, lp['c_wukv'])
        kc_lat, vc_lat = mla_keys(ckv, kr_lat, lp['c_wukv'])
        kc = jnp.concatenate([kc_ctx, kc_lat], axis=1)
        vc = jnp.concatenate([vc_ctx, vc_lat], axis=1)
    oa = map_query_blocks(lambda q: diff_attn(q, ka, va, lam, sa), aq)
    oc = map_query_blocks(lambda q: softmax_attn(q, kc, vc, sc), qc)
    oa = (rms_norm(oa, lp['a_subln_g']) * (1.0 - lam_init)).reshape(b, s, A_V) @ lp['a_wo']
    ob = ob.reshape(b, s, B_W) @ lp['b_wo']
    oc = oc.reshape(b, s, H_C * DV_C) @ lp['c_wo']
    od = conformer_conv(du, lp)
    g = jax.nn.sigmoid(h @ lp['w_gate'] + lp['b_gate']).reshape(b, s, N_BRANCH, D_MODEL)
    merged = g[:, :, 0] * oa + g[:, :, 1] * ob + g[:, :, 2] * oc + g[:, :, 3] * od
    return merged @ lp['w_out'], own

def adaln(cond, w_ada, b_ada):
    m = jax.nn.silu(cond) @ w_ada + b_ada
    return jnp.split(m[:, None, :], 6, axis=-1)

def trunk_layer(x, cond, lp, layer, ctx):
    shift1, scale1, gate1, shift2, scale2, gate2 = adaln(cond, lp['w_ada'], lp['b_ada'])
    h = rms_norm(x, lp['norm1_g']) * (1 + scale1) + shift1
    y, own = mixers(h, lp, layer, ctx)
    x = x + gate1 * y
    h2 = rms_norm(x, lp['norm2_g']) * (1 + scale2) + shift2
    x = x + gate2 * hier_moe(h2, lp)
    return x, own

def setup_inputs(seed: int = 0) -> dict:
    key = jax.random.key(seed)
    keys = jax.random.split(key, 48)
    counter = [0]

    def nrm(shape, scale):
        k = keys[counter[0]]
        counter[0] += 1
        return jax.random.normal(k, shape, jnp.float32) * scale

    def gain(shape):
        return 1.0 + nrm(shape, 0.02)

    L = DEPTH
    D = D_MODEL
    return {
        'x_prompt': nrm((BATCH, SEQ, D), 1.0),
        'x_sample': nrm((DEC_BATCH, DEC_SEQ, D), 1.0),
        'cache_a_k': nrm((DEC_BATCH, DEPTH, PAST_LEN, H_A, 2 * DH_A), 1.0),
        'cache_a_v': nrm((DEC_BATCH, DEPTH, PAST_LEN, H_A, 2 * DH_A), 1.0),
        'cache_b_k': nrm((DEC_BATCH, DEPTH, PAST_LEN, H_B, DH_B), 1.0),
        'cache_b_v': nrm((DEC_BATCH, DEPTH, PAST_LEN, H_B, DH_B), 1.0),
        'cache_c_kv': nrm((DEC_BATCH, DEPTH, PAST_LEN, KV_LORA), 1.0),
        'cache_c_krope': nrm((DEC_BATCH, DEPTH, PAST_LEN, ROPE_C), 1.0),
        'c': nrm((DEC_BATCH, D), 1.0),
        'c_ctx': nrm((D,), 1.0),
        'norm1_g': gain((L, D)),
        'norm2_g': gain((L, D)),
        'w_ada': nrm((L, D, 6 * D), 0.5 * D ** -0.5),
        'b_ada': nrm((L, 6 * D), 0.02),
        'w_in': nrm((L, D, IN_COLS), D ** -0.5),
        'a_lambda': nrm((L, 4, DH_A), 0.1),
        'a_subln_g': gain((L, 2 * DH_A)),
        'a_wo': nrm((L, A_V, D), A_V ** -0.5),
        'b_rpb': nrm((L, H_B, 2 * WIN_R - 1, 2 * WIN_C - 1), 0.1),
        'b_wo': nrm((L, B_W, D), B_W ** -0.5),
        'c_q_norm_g': gain((L, Q_LORA)),
        'c_kv_norm_g': gain((L, KV_LORA)),
        'c_wuq': nrm((L, Q_LORA, H_C * (NOPE_C + ROPE_C)), Q_LORA ** -0.5),
        'c_wukv': nrm((L, KV_LORA, H_C * (NOPE_C + DV_C)), KV_LORA ** -0.5),
        'c_wo': nrm((L, H_C * DV_C, D), (H_C * DV_C) ** -0.5),
        'd_conv_w': nrm((L, CONV_K, CONV_CH), CONV_K ** -0.5),
        'd_conv_b': nrm((L, CONV_CH), 0.02),
        'd_ln_g': gain((L, CONV_CH)),
        'd_ln_b': nrm((L, CONV_CH), 0.02),
        'd_wo': nrm((L, CONV_CH, D), CONV_CH ** -0.5),
        'w_gate': nrm((L, D, N_BRANCH * D), D ** -0.5),
        'b_gate': nrm((L, N_BRANCH * D), 0.02),
        'w_out': nrm((L, D, D), D ** -0.5),
        'moe_w_group': nrm((L, D, N_GROUPS), D ** -0.5),
        'moe_b_group': nrm((L, N_GROUPS), 0.01),
        'moe_w_expert': nrm((L, D, N_EXPERTS), D ** -0.5),
        'moe_b_expert': nrm((L, N_EXPERTS), 0.01),
        'moe_w1': nrm((L, N_EXPERTS, D, 2 * D_EXPERT), D ** -0.5),
        'moe_w2': nrm((L, N_EXPERTS, D_EXPERT, D), D_EXPERT ** -0.5),
        'final_norm_g': gain((D,)),
    }

def reference(x_prompt, x_sample, cache_a_k, cache_a_v, cache_b_k, cache_b_v, cache_c_kv, cache_c_krope,
              c, c_ctx, norm1_g, norm2_g, w_ada, b_ada, w_in, a_lambda, a_subln_g, a_wo, b_rpb, b_wo,
              c_q_norm_g, c_kv_norm_g, c_wuq, c_wukv, c_wo, d_conv_w, d_conv_b, d_ln_g, d_ln_b, d_wo,
              w_gate, b_gate, w_out, moe_w_group, moe_b_group, moe_w_expert, moe_b_expert, moe_w1, moe_w2,
              final_norm_g):
    lps = [dict(norm1_g=norm1_g[l], norm2_g=norm2_g[l], w_ada=w_ada[l], b_ada=b_ada[l], w_in=w_in[l],
                a_lambda=a_lambda[l], a_subln_g=a_subln_g[l], a_wo=a_wo[l], b_rpb=b_rpb[l], b_wo=b_wo[l],
                c_q_norm_g=c_q_norm_g[l], c_kv_norm_g=c_kv_norm_g[l], c_wuq=c_wuq[l], c_wukv=c_wukv[l],
                c_wo=c_wo[l], d_conv_w=d_conv_w[l], d_conv_b=d_conv_b[l], d_ln_g=d_ln_g[l], d_ln_b=d_ln_b[l],
                d_wo=d_wo[l], w_gate=w_gate[l], b_gate=b_gate[l], w_out=w_out[l],
                moe_w_group=moe_w_group[l], moe_b_group=moe_b_group[l], moe_w_expert=moe_w_expert[l],
                moe_b_expert=moe_b_expert[l], moe_w1=moe_w1[l], moe_w2=moe_w2[l])
           for l in range(DEPTH)]

    xp = x_prompt
    states = []
    for l in range(DEPTH):
        xp, st = trunk_layer(xp, c_ctx[None, :], lps[l], l, None)
        states.append(st)
    y_prompt = rms_norm(xp, final_norm_g)

    xs = x_sample
    for l in range(DEPTH):
        ctx = (cache_a_k[:, l], cache_a_v[:, l], cache_b_k[:, l], cache_b_v[:, l],
               cache_c_kv[:, l], cache_c_krope[:, l])
        xs, _ = trunk_layer(xs, c, lps[l], l, ctx)
    y_sample = rms_norm(xs, final_norm_g)

    new_a_k = jnp.stack([st[0] for st in states], axis=1)
    new_a_v = jnp.stack([st[1] for st in states], axis=1)
    new_b_k = jnp.stack([st[2] for st in states], axis=1)
    new_b_v = jnp.stack([st[3] for st in states], axis=1)
    new_c_kv = jnp.stack([st[4] for st in states], axis=1)
    new_c_krope = jnp.stack([st[5] for st in states], axis=1)
    return (y_prompt, y_sample, new_a_k, new_a_v, new_b_k, new_b_v, new_c_kv, new_c_krope)


_drawn_inputs = setup_inputs


def setup_inputs(seed=0):
    import zlib

    import numpy as np

    out = dict(_drawn_inputs(seed))
    spreads = {}
    factors = {'cache_b_k': 3.12,
     'cache_c_kv': 6.866,
     'cache_c_krope': 8.0,
     'norm1_g': 2.913,
     'norm2_g': 4.342,
     'a_subln_g': 8.0,
     'b_rpb': 8.0,
     'c_q_norm_g': 8.0,
     'c_kv_norm_g': 2.884,
     'd_conv_b': 7.354,
     'd_ln_g': 7.979,
     'd_ln_b': 8.0,
     'b_gate': 8.0,
     'moe_b_group': 8.0,
     'moe_b_expert': 8.0,
     'final_norm_g': 7.366,
     'cache_a_k': 8.0,
     'cache_a_v': 8.0}
    for name, (base, spread) in spreads.items():
        noise = np.random.default_rng([zlib.crc32(name.encode()), seed]).standard_normal(out[name].shape)
        drawn = base * np.exp(spread * noise) if base else spread * noise
        out[name] = jnp.asarray(drawn.astype(out[name].dtype))
    for name, factor in factors.items():
        out[name] = (out[name] * factor).astype(out[name].dtype)
    return out
```

```python
import math
from contextlib import ExitStack

import concourse.bass as bass
import numpy as np
from concourse import mybir

F32 = mybir.dt.float32
BF16 = mybir.dt.bfloat16
ALU = mybir.AluOpType
ACT = mybir.ActivationFunctionType
AX_X = mybir.AxisListType.X
ds = bass.ds

P = 128
LAYERS = 2
D = 1024
KC = D // P
CTX, LAT = 128, 512
TOK = CTX + LAT
TILES = TOK // P
EPS = 1e-6
GRID_W = 64
CONV_K, CONV_CH = 31, 256
PAD = CONV_K // 2
IN_COLS = 2464
HEADS = 4
EXPERTS, F_EXP = 16, 256
N_GROUPS = 4
NEG = -1e30

C_AQ, C_AV, C_BQ, C_BV, C_CQ, C_CKV, C_CKR, C_DU = 0, 512, 768, 1280, 1536, 1792, 1920, 1952
TOKCOLS = C_DU

ADA_UNITS = 6 * D // 256
IN_UNITS = 10
WO_UNITS = 4
GATE_UNITS = 16
OUT_UNITS = 4
M1_UNITS = 2 * EXPERTS
M2_UNITS = 16
V_IN = ADA_UNITS
V_WO = V_IN + IN_UNITS
V_GATE = V_WO + WO_UNITS
V_OUT = V_GATE + GATE_UNITS
V_M1 = V_OUT + OUT_UNITS
V_M2 = V_M1 + M1_UNITS
V_ALL = V_M2 + M2_UNITS
S_ALL = V_ALL - WO_UNITS

PC_ADA, PC_G1, PC_G2, PC_BG, PC_CB, PC_LG, PC_LB, PC_N = 0, 48, 56, 64, 96, 98, 100, 102

MAPS = 16
HDS = 12


class Signal:

    def __init__(self, sem, per_layer, before=0):
        self.sem, self.per_layer, self.before = sem, per_layer, before

    def __call__(self, layer, n):
        return self.sem, layer * self.per_layer + (self.before + n)


def build(nc, t):
    ctx = ExitStack()
    with ctx:
        def sb(name, shape, dt=F32):
            return ctx.enter_context(nc.sbuf_tensor(name, shape, dt))

        def sig(name, per_layer=0, before=0):
            return Signal(ctx.enter_context(nc.semaphore(name)), per_layer, before)

        xT = sb("xT", [P, KC, TOK])
        hhi = sb("hhi", [P, KC, TOK], BF16)
        hlo = sb("hlo", [P, KC, TOK], BF16)
        wf = [sb(f"wf{j}", [P, 2048]) for j in range(2)]
        whi = [sb(f"whi{j}", [P, 2048], BF16) for j in range(2)]
        wlo = [sb(f"wlo{j}", [P, 2048], BF16) for j in range(2)]
        arena = sb("arena", [P, 23072])
        scratch = sb("scratch", [P, 4100])
        bias = sb("bias", [P, HEADS, 14, GRID_W])
        rsb = sb("rsb", [P, TOK])
        zhi = rsb[:, :].bitcast(BF16).rearrange("p (c n) -> p c n", c=2)
        zlo = sb("zlo", [P, 2, TOK], BF16)
        ident = sb("ident", [P, P])
        ones = sb("ones", [P, P])
        cosb = sb("cosb", [P, TILES - 1, 32])
        sinb = sb("sinb", [P, TILES - 1, 32])
        band = sb("band", [31, 207], BF16)
        prow = scratch[0:PC_N, 1152:1280]
        pcol = sb("pcol", [P, PC_N])
        cwrow = scratch[0:CONV_K, 896:1152]
        cw = sb("cw", [P, 2, CONV_K])
        rowg = sb("rowg", [P, 64 + 256 + 128])
        lamc = sb("lamc", [P, 2])
        lamt = sb("lamt", [P, 72])
        wr = sb("wr", [P, KC, 20])
        rbias = sb("rbias", [20, 1])
        gfin = sb("gfin", [P, KC])
        scf = sb("scf", [P, KC, 2])
        schi = sb("schi", [P, KC, 2], BF16)
        sclo = sb("sclo", [P, KC, 2], BF16)
        ada = sb("ada", [P, 6 * KC, 2])
        gs = sb("gs", [P, 2, KC, 2])
        stat = sb("stat", [P, 3, MAPS])
        cfa = sb("cfa", [P, 2, 4])
        cstat = sb("cstat", [P, 3, 10])
        ostat = sb("ostat", [P, 3, 4])
        wuf = scratch[:, 0:896]
        lamv = scratch[:, 1280:1408].rearrange("p (a n) -> p a n", a=4)
        rprow = scratch[0:60, 1408:1439]
        rpf = scratch[0:31, 1440:1500]
        rpd = scratch[0:31, 1500:1560]
        rp = scratch[0:31, 1560:1650].bitcast(BF16).rearrange("p (a n) -> p a n", a=3)
        maskb = scratch[:, 2040:2104]
        bandf = scratch[0:31, 1700:1907]
        crow = scratch[0:3 * KC, 1910:2038]
        wuhi = sb("wuhi", [P, 2 * 256 + 384], BF16)
        wulo = sb("wulo", [P, 2 * 256 + 384], BF16)
        PS = ctx.enter_context(nc.psum_tensor("PS", [P, 4, 1024], F32))

        proj = arena[:, 0:TILES * TOKCOLS].rearrange("p (t n) -> p t n", t=TILES)
        AR = TILES * TOKCOLS * 2
        ab = arena[:, :].bitcast(BF16)
        kThi = ab[:, AR:AR + 4608].rearrange("p (c k) -> p c k", c=6)
        kTlo = ab[:, AR + 4608:AR + 9216].rearrange("p (c k) -> p c k", c=6)
        vhi = ab[:, AR + 9216:AR + 13824].rearrange("p (c k) -> p c k", c=6)
        vlo = ab[:, AR + 13824:AR + 18432].rearrange("p (c k) -> p c k", c=6)
        qThi = ab[:, AR + 18432:AR + 22272].rearrange("p (c k) -> p c k", c=6)
        qTlo = ab[:, AR + 22272:AR + 26112].rearrange("p (c k) -> p c k", c=6)
        oThi = ab[:, 0:3840].rearrange("p (c k) -> p c k", c=6)
        oTlo = ab[:, 3840:7680].rearrange("p (c k) -> p c k", c=6)
        pthi = ab[:, 7680:8960].rearrange("p (s k) -> p s k", s=2)
        ptlo = ab[:, 8960:10240].rearrange("p (s k) -> p s k", s=2)
        otok = arena[:, 5120:5888]
        wohi = ab[:, AR:AR + 8192].rearrange("p (b c n) -> p b c n", b=4, c=2)
        wolo = ab[:, AR + 8192:AR + 16384].rearrange("p (b c n) -> p b c n", b=4, c=2)
        mhi = ab[:, AR + 16384:AR + 21504].rearrange("p (c k) -> p c k", c=KC)
        mlo = ab[:, AR + 21504:AR + 26624].rearrange("p (c k) -> p c k", c=KC)
        acthi = ab[:, 0:20480].rearrange("p (c k) -> p c k", c=32)
        actlo = ab[:, 20480:40960].rearrange("p (c k) -> p c k", c=32)
        xtok = arena[:, 0:TILES * D].rearrange("p (t n) -> p t n", t=TILES)
        ytok = arena[:, 0:TILES * D].rearrange("p (t n) -> p t n", t=TILES)

        xsq = scratch[:, 0:1280].rearrange("p (s n) -> p s n", s=2)
        tmp = scratch[:, 1280:2560].rearrange("p (s n) -> p s n", s=2)
        hf = scratch[:, 2560:3840].rearrange("p (s n) -> p s n", s=2)
        zpad = scratch[:, 0:1370].rearrange("p (c n) -> p c n", c=2)
        zacc = scratch[:, 1370:2680].rearrange("p (c n) -> p c n", c=2)
        zsg = scratch[:, 2680:3960].rearrange("p (c n) -> p c n", c=2)
        zc = scratch[:, 0:1280].rearrange("p (c n) -> p c n", c=2)
        zs = scratch[:, 1370:2650].rearrange("p (c n) -> p c n", c=2)
        csq = scratch[:, 0:1920]
        rope1 = scratch[:, 0:512]
        rope2 = scratch[:, 512:1024]
        roped = scratch[:, 1024:1536]
        qkc = scratch[:, 1536:2048]
        cn = scratch[:, 2048:2432]
        cThi = scratch[:, 2432:2624].bitcast(BF16)
        cTlo = scratch[:, 2624:2816].bitcast(BF16)
        cache = scratch[:, 2816:4000]
        ex = scratch[:, 0:2560].rearrange("p (s n) -> p s n", s=4)
        wmix = scratch[:, 2560:3840].rearrange("p (s n) -> p s n", s=2)
        osq = scratch[:, 3840:4096]
        sg = scratch[:, 0:1280].rearrange("p (s n) -> p s n", s=2)
        mt = scratch[:, 1280:2560].rearrange("p (s n) -> p s n", s=2)
        macc = scratch[:, 2560:3840].rearrange("p (s n) -> p s n", s=2)
        dwb = [scratch[:, 2560:3200], scratch[:, 3200:3840]]
        lgT = scratch[0:20, 3200:3840]
        dwT = scratch[0:16, 3200:3840]
        wuf32 = wuhi[:, :].bitcast(F32)
        route = wuf32[:, 0:100].rearrange("p (t n) -> p t n", t=5)
        rw = wuf32[:, 100:300].rearrange("p (t n) -> p t n", t=5)
        rcol = wuf32[:, 300:340].rearrange("p (q t) -> p q t", t=5)
        ex5 = wuf32[:, 340:365].rearrange("p (t n) -> p t n", t=5)
        tie = sb("tie", [P, 4])

        def pr(pair):
            return PS[:, pair, 384:1024]

        SEG = [(0, CTX), (CTX, TOK)]

        def bank(n, w=512):
            return PS[:, n // 2, 512 * (n % 2):512 * (n % 2) + w]

        consts_in = sig("consts_in")
        params_in = sig("params_in", 21 * 16)
        cache_in = sig("cache_in", 9 * 16)
        w_in = [sig(f"w_in{j}", V_ALL // 2 * 16) for j in range(2)]
        w_hi = sig("w_hi", V_ALL)
        w_lo = sig("w_lo", V_ALL)
        w_lo_dve = sig("w_lo_dve", ADA_UNITS)
        ada_used = sig("ada_used", ADA_UNITS, 2)
        half_used = sig("half_used", 8)
        set_ready = sig("set_ready")
        xt_done = sig("xt_done")
        x_even = sig("x_even")
        x_odd = sig("x_odd")
        cond_t = sig("cond_t")
        cond_f = sig("cond_f")
        cond_ready = sig("cond_ready")
        par_t = sig("par_t", 1)
        par_ready = sig("par_ready", 1)
        rp_ready = sig("rp_ready", 1)
        band_done = sig("band_done", 8)
        bias_ready = sig("bias_ready", 8)
        wu_hi = sig("wu_hi", 1)
        wu_ready = sig("wu_ready", 1)
        lam_sum = sig("lam_sum", 1)
        lam_exp = sig("lam_exp", 1)
        ada_ready = sig("ada_ready", 1)
        sq_ready = sig("sq_ready", 16)
        sq_used = sig("sq_used", 16)
        var_ready = sig("var_ready", 2)
        std_ready = sig("std_ready", 2)
        tmp_ready = sig("tmp_ready", 16)
        hf_ready = sig("hf_ready", 16)
        hhi_ready = sig("hhi_ready", 16)
        h_ready = sig("h_ready", 16)
        hf_used = sig("hf_used", 8)
        du_done = sig("du_done", 4)
        sig_ready = sig("sig_ready", 2)
        z_ready = sig("z_ready", 2)
        proj_done = sig("proj_done", 40)
        proj_ready = sig("proj_ready", 40)
        cv_ready = sig("cv_ready", 1)
        mu_done = sig("mu_done", 1)
        zc_ready = sig("zc_ready", 2)
        zsq_ready = sig("zsq_ready", 2)
        zv_done = sig("zv_done", 1)
        zvar_ready = sig("zvar_ready", 1)
        zstd_ready = sig("zstd_ready", 1)
        zn_ready = sig("zn_ready", 2)
        zs_ready = sig("zs_ready", 2)
        zhi_ready = sig("zhi_ready", 2)
        z_split = sig("z_split", 1)
        cs_ready = sig("cs_ready", 1)
        cv_var = sig("cv_var", 1)
        cv_std = sig("cv_std", 1)
        roped_ready = sig("roped_ready", 5)
        ab_t = sig("ab_t", 11)
        ab_hi = sig("ab_hi", 11)
        ab_ready = sig("ab_ready", 11)
        cn_ready = sig("cn_ready", 6)
        cn_t = sig("cn_t", 6)
        cT_hi = sig("cT_hi", 6)
        cT_ready = sig("cT_ready", 6)
        up_done = sig("up_done", 6)
        qkc_raw = sig("qkc_raw", 6)
        up_free = sig("up_free", 6)
        qkc_ready = sig("qkc_ready", 6)
        c_t = sig("c_t", 6)
        c_hi = sig("c_hi", 6)
        c_ready = sig("c_ready", 6)
        v_hi = sig("v_hi", 1)
        v_ready = sig("v_ready", 1)
        own_out = sig("own_out", 6 * 16)
        s_done = sig("s_done", TILES * MAPS)
        mx_ready = sig("mx_ready", TILES * MAPS)
        ex_ready = sig("ex_ready", TILES * MAPS)
        mix_ready = sig("mix_ready", TILES * 4)
        pt_done = sig("pt_done", TILES * HDS)
        pt_hi = sig("pt_hi", TILES * HDS)
        pt_ready = sig("pt_ready", TILES * HDS)
        pv_done = sig("pv_done", TILES * HDS)
        rec_ready = sig("rec_ready", TILES * HDS)
        o_ready = sig("o_ready", TILES * HDS)
        ovar_ready = sig("ovar_ready", TILES)
        ostd_ready = sig("ostd_ready", TILES)
        on_ready = sig("on_ready", TILES)
        ot_done = sig("ot_done", TILES)
        ot_hi = sig("ot_hi", TILES)
        ot_ready = sig("ot_ready", TILES)
        g_done = sig("g_done", 32)
        g_ready = sig("g_ready", 32, 2)
        b_done = sig("b_done", 32)
        m_used = sig("m_used", 32, 2)
        m_ready = sig("m_ready", 8)
        m_hi = sig("m_hi", 8)
        m_split = sig("m_split", 8)
        y_done = sig("y_done", 8)
        x1_ready = sig("x1_ready", 8, 4)
        lg_ready = sig("lg_ready", 1)
        lgt_done = sig("lgt_done", 1)
        rmax_ready = sig("rmax_ready", 1)
        rexp_ready = sig("rexp_ready", 1)
        dw_ready = sig("dw_ready", 1)
        dwt_done = sig("dwt_done", 1)
        dwT_ready = sig("dwT_ready", 1)
        dw_out = sig("dw_out", 16)
        dw_in = [sig(f"dw_in{j}", 8 * 16) for j in range(2)]
        gu_done = sig("gu_done", 4 * EXPERTS)
        silu_ready = sig("silu_ready", 2 * EXPERTS)
        gu_mul = sig("gu_mul", 2 * EXPERTS)
        a_ready = sig("a_ready", 2 * EXPERTS, 4)
        a_hi = sig("a_hi", 2 * EXPERTS)
        a_split = sig("a_split", 2 * EXPERTS)
        y2_done = sig("y2_done", 8)
        x2_ready = sig("x2_ready", 8, 2)
        fin_ready = sig("fin_ready")
        fin_t = sig("fin_t")
        fin_out = sig("fin_out")
        fin_saved = sig("fin_saved")

        block = ctx.enter_context(nc.Block())

        def passes(pe, out, st_hi, st_lo, mv_hi, mv_lo, first, last):
            for n, (st, mv) in enumerate(((st_hi, mv_hi), (st_hi, mv_lo), (st_lo, mv_hi))):
                ins = pe.matmul(out, st, mv, start=first and n == 0, stop=last and n == 2)
            return ins

        def passes640(pe, pair, st_hi, st_lo, mv_hi, mv_lo, first, last):
            for n, (st, mv) in enumerate(((st_hi, mv_hi), (st_hi, mv_lo), (st_lo, mv_hi))):
                for a, b in SEG:
                    ins = pe.matmul(pr(pair)[:, a:b], st, mv[:, a:b], start=first and n == 0, stop=last and n == 2)
            return ins

        def keytile(tile):
            return tile if tile else 5

        @block.sync
        def _(sp):
            for dst, src in ((ident, t["k_ident"]),
                             (bandf, t["k_band"]), (crow[0:KC, :], t["c_ctx"].rearrange("(k p) -> k p", p=P)),
                             (crow[KC:2 * KC, :], t["c"].rearrange("b (k p) -> (b k) p", p=P)),
                             (crow[2 * KC:3 * KC, :], t["final_norm_g"].rearrange("(k p) -> k p", p=P)),
                             (xtok[:, 0, :], t["x_prompt"].rearrange("b s d -> (b s) d")),
                             (xtok[:, 1:TILES, :], t["x_sample"].rearrange("b (t p) d -> p (b t) d", p=P))):
                sp.dma_start(dst[:] if not isinstance(dst, bass.AP) else dst, src).then_inc(consts_in.sem, 16)
            with sp.Fori(0, LAYERS) as l:
                def free(v):
                    sp.wait_ge(*w_lo(l, v - 1))

                def wcols(w, off, n=256):
                    return w[ds(l, 1), :, off:off + n].rearrange("o (k p) n -> p (o k) n", p=P)

                sp.wait_ge(*x2_ready(l, 0))
                small = [
                    (prow[PC_ADA:PC_G1, :], t["b_ada"][ds(l, 1), :].rearrange("o (k p) -> (o k) p", p=P)),
                    (prow[PC_G1:PC_G2, :], t["norm1_g"][ds(l, 1), :].rearrange("o (k p) -> (o k) p", p=P)),
                    (prow[PC_G2:PC_BG, :], t["norm2_g"][ds(l, 1), :].rearrange("o (k p) -> (o k) p", p=P)),
                    (prow[PC_BG:PC_CB, :], t["b_gate"][ds(l, 1), :].rearrange("o (k p) -> (o k) p", p=P)),
                    (prow[PC_CB:PC_LG, :], t["d_conv_b"][ds(l, 1), :].rearrange("o (k p) -> (o k) p", p=P)),
                    (prow[PC_LG:PC_LB, :], t["d_ln_g"][ds(l, 1), :].rearrange("o (k p) -> (o k) p", p=P)),
                    (prow[PC_LB:PC_N, :], t["d_ln_b"][ds(l, 1), :].rearrange("o (k p) -> (o k) p", p=P)),
                    (cwrow[:, :], t["d_conv_w"][ds(l, 1)].rearrange("o k c -> (o k) c")),
                    (rprow[:, :], t["b_rpb"][ds(l, 1)].rearrange("o h r c -> (o h r) c")),
                    (rowg[:, 0:64], t["a_subln_g"][ds(l, 1), :].partition_broadcast(P)),
                    (rowg[:, 64:320], t["c_q_norm_g"][ds(l, 1), :].partition_broadcast(P)),
                    (rowg[:, 320:448], t["c_kv_norm_g"][ds(l, 1), :].partition_broadcast(P)),
                    (lamv[:, :, :], t["a_lambda"][ds(l, 1)].partition_broadcast(P)),
                    (lamc[:, :], t["k_lam"][ds(l, 1), :].partition_broadcast(P)),
                    (wuf[:, 0:512].rearrange("p (k n) -> p k n", k=2),
                     t["c_wuq"][ds(l, 1)].rearrange("o (k p) n -> p (o k) n", p=P)),
                    (wuf[:, 512:896], t["c_wukv"][ds(l, 1)].rearrange("o p n -> (o p) n")),
                    (rbias[0:4, :], t["moe_b_group"][ds(l, 1), :].rearrange("o n -> n o")),
                    (rbias[4:20, :], t["moe_b_expert"][ds(l, 1), :].rearrange("o n -> n o")),
                    (wr[:, :, 0:4], t["moe_w_group"][ds(l, 1)].rearrange("o (k p) n -> p (o k) n", p=P)),
                    (wr[:, :, 4:20], t["moe_w_expert"][ds(l, 1)].rearrange("o (k p) n -> p (o k) n", p=P)),
                ]
                small.append((maskb, t["k_mask"]))
                for dst, src in small:
                    sp.dma_start(dst, src).then_inc(params_in.sem, 16)
                with sp.Fori(0, ADA_UNITS // 2) as i:
                    for j in range(2):
                        sp.wait_ge(w_lo.sem, l * V_ALL + i * 2)
                        sp.wait_ge(w_lo_dve.sem, l * ADA_UNITS + i * 2)
                        sp.dma_start(wf[j][:, :].rearrange("p (k n) -> p k n", k=KC),
                                     t["w_ada"][ds(l, 1), :, ds(i * 512 + j * 256, 256)]
                                     .rearrange("o (k p) n -> p (o k) n", p=P)).then_inc(w_in[j].sem, 16)
                for u in range(IN_UNITS):
                    off = C_DU + 256 * u if u < 2 else 256 * (u - 2)
                    n = 256 if u < IN_UNITS - 1 else 160
                    free(V_IN + u)
                    if u == 0:
                        sp.dma_start(tie[:, :], t["k_tie"]).then_inc(cache_in.sem, 16)
                        sp.wait_ge(*w_lo_dve(l, ADA_UNITS))
                        sp.dma_start(cosb[:, :, :], t["k_cos"]).then_inc(cache_in.sem, 16)
                    if u == 2:
                        sp.dma_start(sinb[:, :, :], t["k_sin"]).then_inc(cache_in.sem, 16)
                    sp.dma_start(wf[u % 2][:, 0:KC * n].rearrange("p (k n) -> p k n", k=KC),
                                 wcols(t["w_in"], off, n)).then_inc(w_in[u % 2].sem, 16)
                sp.wait_ge(*z_split(l, 1))
                for c, (name, w) in enumerate((("cache_a_k", 256), ("cache_b_k", 256), ("cache_a_v", 256),
                                               ("cache_b_v", 256), ("cache_c_kv", 128), ("cache_c_krope", 32))):
                    src = t[name][:, ds(l, 1)]
                    src = src.rearrange("b o s h d -> (b o s) (h d)" if c < 4 else "b o s d -> (b o s) d")
                    off = 256 * c if c < 4 else (1024 if c == 4 else 1152)
                    sp.dma_start(cache[:, off:off + w], src).then_inc(cache_in.sem, 16)
                sp.wait_ge(*cn_ready(l, 1))
                for name, a, n in (("new_a_k", 256, 256), ("new_a_v", C_AV, 256), ("new_b_k", 1024, 256),
                                   ("new_b_v", C_BV, 256), ("new_c_krope", C_CKR, 32)):
                    dst = t[name][:, ds(l, 1)]
                    dst = dst.rearrange("b o s h d -> (b o s) (h d)" if n == 256 else "b o s d -> (b o s) d")
                    sp.dma_start(dst, proj[:, 0, a:a + n]).then_inc(own_out.sem, 16)
                sp.dma_start(t["new_c_kv"][:, ds(l, 1)].rearrange("b o s d -> (b o s) d"), proj[:, 0, C_CKV:C_CKR]
                             ).then_inc(own_out.sem, 16)
                for b, name in enumerate(("a_wo", "b_wo", "c_wo", "d_wo")):
                    free(V_WO + b)
                    sp.dma_start(wf[b % 2][:, :].rearrange("p (k n) -> p k n", k=2),
                                 t[name][ds(l, 1)].rearrange("o (k p) n -> p (o k) n", p=P)
                                 ).then_inc(w_in[b % 2].sem, 16)
                with sp.Fori(0, KC // 2) as d2:
                    for b in range(4):
                        sp.wait_ge(w_lo.sem, l * V_ALL + d2 * 4 + (V_GATE + b - 1))
                        sp.dma_start(wf[b % 2][:, :].rearrange("p (k n) -> p k n", k=KC),
                                     t["w_gate"][ds(l, 1), :, ds(d2 * 256 + b * D, 256)]
                                     .rearrange("o (k p) n -> p (o k) n", p=P)).then_inc(w_in[b % 2].sem, 16)
                with sp.Fori(0, 2) as i:
                    for j in range(2):
                        sp.wait_ge(w_lo.sem, l * V_ALL + i * 2 + (V_OUT + j - 1))
                        sp.dma_start(wf[j][:, :].rearrange("p (k n) -> p k n", k=KC),
                                     t["w_out"][ds(l, 1), :, ds(i * 512 + j * 256, 256)]
                                     .rearrange("o (k p) n -> p (o k) n", p=P)).then_inc(w_in[j].sem, 16)
                with sp.Fori(0, EXPERTS // 2) as e2:
                    for je in range(2):
                        for j in range(2):
                            sp.wait_ge(w_lo.sem, l * V_ALL + e2 * 4 + (V_M1 + 2 * je + j - 1))
                            sp.dma_start(wf[j][:, :].rearrange("p (k n) -> p k n", k=KC),
                                         t["moe_w1"][ds(l, 1), ds(e2 * 2 + je, 1), :, 256 * j:256 * j + 256]
                                         .rearrange("o e (k p) n -> p (o e k) n", p=P)).then_inc(w_in[j].sem, 16)
                        sp.wait_ge(*dw_out(l, 16))
                        sp.wait_ge(*a_ready(l, e2 * 4 + 2 * je))
                        sp.dma_start(dwb[je], t["dw_rows"][ds(e2 * 2 + je, 1), :].partition_broadcast(P)
                                     .rearrange("p o n -> p (o n)")).then_inc(dw_in[je].sem, 16)
                with sp.Fori(0, 8) as d:
                    for j in range(2):
                        sp.wait_ge(w_lo.sem, l * V_ALL + d * 2 + (V_M2 + j - 1))
                        sp.dma_start(wf[j][:, :].rearrange("p (c n) -> p c n", c=16),
                                     t["moe_w2"][ds(l, 1), 8 * j:8 * j + 8, :, ds(d * P, P)]
                                     .rearrange("o e (c p) n -> p (o e c) n", p=P)).then_inc(w_in[j].sem, 16)

            sp.wait_ge(*own_out(LAYERS - 1, 6 * 16))
            for n, (name, a, b) in enumerate((("y_prompt", 0, 1), ("y_sample", 1, TILES))):
                sp.wait_ge(*fin_out(0, KC))
                dst = t[name].rearrange("b (t p) d -> p (b t) d", p=P)
                sp.dma_start(dst, ytok[:, a:b, :]).then_inc(fin_saved.sem, 16)
            sp.wait_ge(*fin_saved(0, 32))

        @block.tensor
        def _(pe):
            pe.wait_ge(*consts_in(0, 7 * 16))
            for tile in range(TILES):
                if tile == 4:
                    pe.wait_ge(*x_even(0, 1))
                for k in range(KC):
                    ins = pe.transpose(PS[:, tile % 4, k * P:(k + 1) * P], xtok[:, tile, k * P:(k + 1) * P], ident[:, :])
                ins.then_inc(xt_done.sem, 1)
            pe.wait_ge(*x_odd(0, 1))
            pe.transpose(PS[:, 1, 0:3 * KC], crow[:, :], ident[0:3 * KC, 0:3 * KC]).then_inc(cond_t.sem, 1)
            pe.wait_ge(*set_ready(0, 2))
            pe.wait_ge(*cond_ready(0, 1))

            def sums(l, n):
                for k in range(KC):
                    pe.wait_ge(*sq_ready(l, KC * n + k + 1))
                    for a, b in SEG:
                        ins = pe.matmul(pr(2)[:, a:b], ones[:, :], xsq[:, k % 2, a:b], start=k == 0, stop=k == KC - 1)
                    ins.then_inc(sq_used.sem, 1)

            with pe.Fori(0, LAYERS) as l:
                pe.wait_ge(*x2_ready(l, 0))
                pe.wait_ge(*params_in(l, 21 * 16))
                pe.transpose(bank(6)[:, 0:PC_N], prow[:, :], ident[0:PC_N, 0:PC_N])
                for c in range(2):
                    pe.transpose(bank(6)[:, 104 + 32 * c:104 + 32 * c + CONV_K], cwrow[:, c * P:(c + 1) * P],
                                 ident[0:CONV_K, 0:CONV_K])
                pe.transpose(bank(6)[0:31, 168:228], rprow[:, :], ident[0:60, 0:60]).then_inc(par_t.sem, 1)
                pe.wait_ge(*rp_ready(l, 1))
                for g in range(8):
                    if g >= 4:
                        pe.wait_ge(*bias_ready(l, g - 3))
                    for kl in range(8):
                        kc = 8 * g + kl
                        for part in range(3):
                            ins = pe.matmul(bank(g % 4)[:, kl * 60:(kl + 1) * 60], band[:, 79 - kc:207 - kc],
                                            rp[:, part, :], start=part == 0, stop=part == 2)
                    ins.then_inc(band_done.sem, 1)
                with pe.Fori(0, ADA_UNITS // 2) as i:
                    for j in range(2):
                        pe.wait_ge(w_lo.sem, l * V_ALL + i * 2 + (j + 1))
                        pe.wait_ge(w_lo_dve.sem, l * ADA_UNITS + i * 2 + (j + 1))
                        for c in range(2):
                            for k in range(KC):
                                w = slice(k * 256 + c * P, k * 256 + (c + 1) * P)
                                ins = passes(pe, PS[:, 3, ds(i * 8 + (512 + 4 * j + 2 * c), 2)], whi[j][:, w],
                                             wlo[j][:, w], schi[:, k, :], sclo[:, k, :], k == 0, k == KC - 1)
                        ins.then_inc(ada_used.sem, 1)
                sums(l, 0)
                for u in range(2):
                    pe.wait_ge(*w_lo(l, V_IN + u + 1))
                    for c in range(2):
                        for k in range(KC):
                            if u == 0 and c == 0:
                                pe.wait_ge(*h_ready(l, k + 1))
                            w = slice(k * 256 + c * P, k * 256 + (c + 1) * P)
                            ins = passes640(pe, 2 * u + c, whi[u][:, w], wlo[u][:, w], hhi[:, k, :], hlo[:, k, :],
                                            k == 0, k == KC - 1)
                        ins.then_inc(du_done.sem, 1)
                for u in range(2, IN_UNITS):
                    n = 256 if u < IN_UNITS - 1 else 160
                    pe.wait_ge(*w_lo(l, V_IN + u + 1))
                    for tile in range(TILES):
                        g = (u - 2) * TILES + tile
                        if g < 8:
                            pe.wait_ge(*z_ready(l, 2))
                        else:
                            pe.wait_ge(*proj_ready(l, g - 7))
                        for k in range(KC):
                            ins = passes(pe, bank(g % 8, n), hhi[:, k, tile * P:(tile + 1) * P],
                                         hlo[:, k, tile * P:(tile + 1) * P], whi[u % 2][:, k * n:(k + 1) * n],
                                         wlo[u % 2][:, k * n:(k + 1) * n], k == 0, k == KC - 1)
                        ins.then_inc(proj_done.sem, 1)
                pe.wait_ge(*proj_ready(l, 40))
                pe.wait_ge(*cv_ready(l, 1))
                for (a, b), z0 in zip(SEG, (0, CTX + PAD)):
                    for c in range(2):
                        ins = pe.matmul(pr(0)[:, a:b], ones[:, :], zacc[:, c, z0:z0 + b - a], start=c == 0, stop=c == 1)
                ins.then_inc(mu_done.sem, 1)
                for c in range(2):
                    pe.wait_ge(*zsq_ready(l, c + 1))
                    for a, b in SEG:
                        ins = pe.matmul(pr(1)[:, a:b], ones[:, :], zsg[:, c, a:b], start=c == 0, stop=c == 1)
                ins.then_inc(zv_done.sem, 1)
                pe.wait_ge(*wu_ready(l, 1))
                pe.wait_ge(*cache_in(l, 9 * 16))
                pe.wait_ge(*zvar_ready(l, 1))
                for n in range(TILES + 1):
                    own = n < TILES
                    src = cache[:, 0:512] if not own else (roped if n else proj[:, 0, 0:512])
                    if own and n:
                        pe.wait_ge(*roped_ready(l, n + 1))
                    if n >= 2:
                        pe.wait_ge(*ab_ready(l, 2 * n - 3))
                    for c in range(4):
                        ins = pe.transpose(bank(4 + 2 * (n % 2))[:, c * P:(c + 1) * P], src[:, c * P:(c + 1) * P], ident[:, :])
                    ins.then_inc(ab_t.sem, 1)
                    if own:
                        if n >= 2:
                            pe.wait_ge(*ab_ready(l, 2 * n - 2))
                        for c in range(4):
                            ins = pe.transpose(bank(5 + 2 * (n % 2))[:, c * P:(c + 1) * P],
                                               proj[:, n, C_BQ + c * P:C_BQ + (c + 1) * P], ident[:, :])
                        ins.then_inc(ab_t.sem, 1)
                    pe.wait_ge(*cn_ready(l, n + 1))
                    if n:
                        pe.wait_ge(*cT_ready(l, n))
                    for c in range(0 if own else 2, 3):
                        src = cn[:, c * P:(c + 1) * P] if own else cache[:, 1024:1152]
                        ins = pe.transpose(bank(0)[:, c * P:(c + 1) * P], src, ident[:, :])
                    ins.then_inc(cn_t.sem, 1)
                    pe.wait_ge(*cT_ready(l, n + 1))
                    if n:
                        pe.wait_ge(*up_free(l, n))
                    if own:
                        for c in range(2):
                            passes(pe, bank(1, 256), cThi[:, c * P:(c + 1) * P], cTlo[:, c * P:(c + 1) * P],
                                   wuhi[:, c * 256:(c + 1) * 256], wulo[:, c * 256:(c + 1) * 256], c == 0, c == 1)
                    passes(pe, bank(2, 384), cThi[:, 256:384], cTlo[:, 256:384], wuhi[:, 512:896], wulo[:, 512:896],
                           True, True).then_inc(up_done.sem, 1)
                    pe.wait_ge(*qkc_ready(l, n + 1))
                    if n:
                        pe.wait_ge(*c_ready(l, n))
                    for c in range(0 if own else 2, 4):
                        ins = pe.transpose(bank(3)[:, c * P:(c + 1) * P], qkc[:, c * P:(c + 1) * P], ident[:, :])
                    ins.then_inc(c_t.sem, 1)
                pe.wait_ge(*ab_ready(l, 11))
                pe.wait_ge(*c_ready(l, 6))
                pe.wait_ge(*v_ready(l, 1))

                def score(ti, tile, m):
                    if ti or m >= 2:
                        pe.wait_ge(*ex_ready(l, ti * MAPS + m - 1))
                    if m < 8:
                        lo, n, c = 32 * (m % 4), 32, m // 4
                    else:
                        lo, n, c = 64 * (m % 2), 64, (m - 8) // 2 + 2
                    q = (slice(lo, lo + n), c, slice(tile * P, (tile + 1) * P))
                    for a, b in SEG if tile else SEG[:1]:
                        k = (slice(lo, lo + n), c, slice(a, b) if tile else slice(TOK, TOK + P))
                        ins = passes(pe, pr(m % 2)[:, a:b], qThi[q], qTlo[q], kThi[k], kTlo[k], True, True)
                    ins.then_inc(s_done.sem, 1)

                def maps(hd):
                    return (2 * hd, 2 * hd + 1) if hd < 4 else (hd + 4,)

                def turn(ti, tile, hd):
                    if hd < 4:
                        pe.wait_ge(*mix_ready(l, ti * 4 + hd + 1))
                        src = wmix[:, hd % 2, :]
                    else:
                        pe.wait_ge(*ex_ready(l, ti * MAPS + hd + 5))
                        src = ex[:, hd % 4, :]
                    pe.wait_ge(*pt_ready(l, ti * HDS + hd))
                    if hd == 0:
                        pe.wait_ge(*ot_ready(l, ti))
                    for c in range(TILES if tile else 1):
                        ins = pe.transpose(pr(2)[:, c * P:(c + 1) * P], src[:, c * P:(c + 1) * P], ident[:, :])
                    ins.then_inc(pt_done.sem, 1)

                def values(ti, tile, hd):
                    pe.wait_ge(*pt_ready(l, ti * HDS + hd + 1))
                    if ti or hd >= 2:
                        pe.wait_ge(*o_ready(l, ti * HDS + hd - 1))
                    kts = range(TILES) if tile else (5,)
                    for c, kt in enumerate(kts):
                        ins = passes(pe, bank(6 + hd % 2, 64), pthi[:, hd % 2, c * P:(c + 1) * P],
                                     ptlo[:, hd % 2, c * P:(c + 1) * P], vhi[:, kt, hd * 64:(hd + 1) * 64],
                                     vlo[:, kt, hd * 64:(hd + 1) * 64], c == 0, c == len(kts) - 1)
                    ins.then_inc(pv_done.sem, 1)

                for ti, tile in enumerate((1, 2, 3, 4, 0)):
                    for step in range(HDS + 2):
                        if step < HDS:
                            for m in maps(step):
                                score(ti, tile, m)
                        if 1 <= step <= HDS:
                            turn(ti, tile, step - 1)
                        if step >= 2:
                            values(ti, tile, step - 2)
                    pe.wait_ge(*on_ready(l, ti + 1))
                    pe.wait_ge(*pt_ready(l, (ti + 1) * HDS))
                    for c in range(6):
                        ins = pe.transpose(PS[:, 2, c * P:(c + 1) * P], otok[:, c * P:(c + 1) * P], ident[:, :])
                    ins.then_inc(ot_done.sem, 1)
                with pe.Fori(0, KC // 2) as d2:
                    pe.wait_ge(*ot_ready(l, TILES))
                    pe.wait_ge(*z_split(l, 1))
                    for b in range(4):
                        pe.wait_ge(w_lo.sem, l * V_ALL + d2 * 4 + (V_GATE + b + 1))
                        bhi = [oThi[:, 2 * b + k, :] if b < 3 else zhi[:, k, :] for k in range(2)]
                        blo = [oTlo[:, 2 * b + k, :] if b < 3 else zlo[:, k, :] for k in range(2)]
                        for c in range(2):
                            pe.wait_ge(*m_used(l, d2 * 8 + (2 * b + c - 1)))
                            for k in range(2):
                                w = ds(d2 * 256 + c * P, P)
                                ins = passes640(pe, 2 + c, wohi[:, b, k, w], wolo[:, b, k, w], bhi[k], blo[k],
                                                k == 0, k == 1)
                            ins.then_inc(b_done.sem, 1)
                            pe.wait_ge(*g_ready(l, d2 * 8 + (2 * b + c - 1)))
                            for k in range(KC):
                                w = slice(k * 256 + c * P, k * 256 + (c + 1) * P)
                                ins = passes640(pe, c, whi[b % 2][:, w], wlo[b % 2][:, w], hhi[:, k, :], hlo[:, k, :],
                                                k == 0, k == KC - 1)
                            ins.then_inc(g_done.sem, 1)
                with pe.Fori(0, 2) as i:
                    pe.wait_ge(*m_split(l, KC))
                    for j in range(2):
                        pe.wait_ge(w_lo.sem, l * V_ALL + i * 2 + (V_OUT + j + 1))
                        for c in range(2):
                            pe.wait_ge(x1_ready.sem, l * 8 + i * 4 + (2 * j + c + 1))
                            for k in range(KC):
                                w = slice(k * 256 + c * P, k * 256 + (c + 1) * P)
                                ins = passes640(pe, 2 * j + c, whi[j][:, w], wlo[j][:, w], mhi[:, k, :], mlo[:, k, :],
                                                k == 0, k == KC - 1)
                            ins.then_inc(y_done.sem, 1)
                sums(l, 1)
                for k in range(KC):
                    pe.wait_ge(*hf_ready(l, KC + k + 1))
                    for a, b in SEG:
                        ins = pe.matmul(pr(3)[0:20, a:b], wr[:, k, :], hf[:, k % 2, a:b], start=k == 0, stop=k == KC - 1)
                    ins.then_inc(hf_used.sem, 1)
                pe.wait_ge(*lg_ready(l, 1))
                for tile in range(TILES):
                    ins = pe.matmul(bank(4)[:, tile * 20:(tile + 1) * 20], lgT[:, tile * P:(tile + 1) * P],
                                    ident[0:20, 0:20], start=True, stop=True)
                ins.then_inc(lgt_done.sem, 1)
                pe.wait_ge(*dw_ready(l, 1))
                for tile in range(TILES):
                    ins = pe.transpose(pr(2)[0:16, tile * P:(tile + 1) * P], rw[:, tile, 0:16], ident[:, :])
                ins.then_inc(dwt_done.sem, 1)
                with pe.Fori(0, EXPERTS) as e:
                    pe.wait_ge(*dwT_ready(l, 1))
                    pe.wait_ge(*h_ready(l, 2 * KC))
                    for j in range(2):
                        pe.wait_ge(w_lo.sem, l * V_ALL + e * 2 + (V_M1 + j + 1))
                        if j == 0:
                            pe.wait_ge(silu_ready.sem, l * 32 + e * 2)
                        else:
                            pe.wait_ge(gu_mul.sem, l * 32 + e * 2)
                        for c in range(2):
                            for k in range(KC):
                                w = slice(k * 256 + c * P, k * 256 + (c + 1) * P)
                                ins = passes640(pe, 2 * j + c, whi[j][:, w], wlo[j][:, w], hhi[:, k, :], hlo[:, k, :],
                                                k == 0, k == KC - 1)
                            ins.then_inc(gu_done.sem, 1)
                with pe.Fori(0, KC // 2) as d2:
                    pe.wait_ge(*a_split(l, 2 * EXPERTS))
                    for jd in range(2):
                        pe.wait_ge(x2_ready.sem, l * 8 + d2 * 2 + (jd + 1))
                        for j in range(2):
                            pe.wait_ge(w_lo.sem, l * V_ALL + d2 * 4 + (V_M2 + 2 * jd + j + 1))
                            for c in range(16):
                                w = slice(c * P, (c + 1) * P)
                                k = 16 * j + c
                                ins = passes640(pe, jd, whi[j][:, w], wlo[j][:, w], acthi[:, k, :], actlo[:, k, :],
                                                k == 0, k == 31)
                            ins.then_inc((y2_done if j else half_used).sem, 1)
            pe.wait_ge(*x2_ready(LAYERS - 1, 8))
            sums(LAYERS, 0)
            for k in range(KC):
                pe.wait_ge(*fin_ready(0, k + 1))
                if k >= 2:
                    pe.wait_ge(*fin_out(0, k - 1))
                for tile in range(TILES):
                    ins = pe.transpose(pr(k % 2)[:, tile * P:(tile + 1) * P], tmp[:, k % 2, tile * P:(tile + 1) * P],
                                       ident[:, :])
                ins.then_inc(fin_t.sem, 1)

        @block.scalar
        def _(act):
            for tile in (0, 2, 4):
                act.wait_ge(*xt_done(0, tile + 1))
                ins = act.copy(xT[:, :, tile * P:(tile + 1) * P], PS[:, tile % 4, :].rearrange("p (k n) -> p k n", k=KC))
                ins.then_inc(x_even.sem, 1)
            act.wait_ge(*cond_t(0, 1))
            act.activation(scf[:, :, :], PS[:, 1, 0:2 * KC].rearrange("p (s k) -> p k s", s=2), ACT.Silu
                           ).then_inc(cond_f.sem, 1)
            act.wait_ge(*cond_f(0, 1))
            act.copy(schi[:, :, :], scf[:, :, :]).then_inc(cond_f.sem, 1)
            act.wait_ge(*x_odd(0, 2))

            def squares(l, n):
                for k in range(KC):
                    if k >= 2:
                        act.wait_ge(*sq_used(l, KC * n + k - 1))
                    act.activation(xsq[:, k % 2, :], xT[:, k, :], ACT.Square).then_inc(sq_ready.sem, 1)
                act.wait_ge(*var_ready(l, n + 1))
                act.activation(rsb[:, :], rsb[:, :], ACT.Sqrt).then_inc(std_ready.sem, 1)

            def modulate(l, n):
                for k in range(KC):
                    act.wait_ge(*tmp_ready(l, KC * n + k + 1))
                    if k >= 2:
                        act.wait_ge(*h_ready(l, KC * n + k - 1))
                        if n:
                            act.wait_ge(*hf_used(l, k - 1))
                    for s, (a, b) in enumerate(SEG):
                        ins = act.activation(hf[:, k % 2, a:b], tmp[:, k % 2, a:b], ACT.Identity,
                                             bias=ada[:, 24 * n + k, s:s + 1])
                    ins.then_inc(hf_ready.sem, 1)

            with act.Fori(0, LAYERS) as l:
                def high(v, j, dst=None, n=2048):
                    act.wait_ge(w_in[j].sem, l * (V_ALL // 2 * 16) + (v // 2 + 1) * 16)
                    act.copy(whi[j][:, 0:n] if dst is None else dst, wf[j][:, 0:n]).then_inc(w_hi.sem, 1)

                def high_at(i, v, j, step=2):
                    act.wait_ge(w_in[j].sem, l * (V_ALL // 2 * 16) + i * (8 * step) + (v // 2 + 1) * 16)
                    act.copy(whi[j][:, :], wf[j][:, :]).then_inc(w_hi.sem, 1)

                act.wait_ge(*params_in(l, 21 * 16))
                act.copy(wuhi[:, :], wuf[:, :]).then_inc(wu_hi.sem, 1)
                act.wait_ge(*lam_sum(l, 1))
                act.activation(lamt[:, 66:68], lamt[:, 64:66], ACT.Exp).then_inc(lam_exp.sem, 1)
                with act.Fori(0, ADA_UNITS // 2) as i:
                    for j in range(2):
                        act.wait_ge(*ada_used(l, i * 2 + (j - 1)))
                        high_at(i, j, j)
                act.wait_ge(*ada_ready(l, 1))
                for u in range(2):
                    high(V_IN + u, u)
                squares(l, 0)
                modulate(l, 0)
                act.wait_ge(*du_done(l, 2))
                high(V_IN + 2, 0)
                for c in range(2):
                    act.wait_ge(*du_done(l, 3 + c))
                    act.activation(zsg[:, c, :], pr(2 + c), ACT.Sigmoid).then_inc(sig_ready.sem, 1)
                high(V_IN + 3, 1)
                for u in range(2, IN_UNITS):
                    n = 256 if u < IN_UNITS - 1 else 160
                    for tile in range(TILES):
                        g = (u - 2) * TILES + tile
                        act.wait_ge(*proj_done(l, g + 1))
                        act.copy(proj[:, tile, 256 * (u - 2):256 * (u - 2) + n], bank(g % 8, n)
                                 ).then_inc(proj_ready.sem, 1)
                    if u + 2 < IN_UNITS:
                        high(V_IN + u + 2, u % 2, n=2048 if u + 2 < IN_UNITS - 1 else KC * 160)
                for c in range(2):
                    act.wait_ge(*zc_ready(l, c + 1))
                    act.activation(zsg[:, c, :], zc[:, c, :], ACT.Square).then_inc(zsq_ready.sem, 1)
                act.wait_ge(*zvar_ready(l, 1))
                act.activation(rsb[:, :], rsb[:, :], ACT.Sqrt).then_inc(zstd_ready.sem, 1)
                for c in range(2):
                    act.wait_ge(*zn_ready(l, c + 1))
                    act.activation(zs[:, c, :], zc[:, c, :], ACT.Silu, bias=pcol[:, PC_LB + c:PC_LB + c + 1],
                                   scale=pcol[:, PC_LG + c:PC_LG + c + 1]).then_inc(zs_ready.sem, 1)
                act.wait_ge(*cache_in(l, 9 * 16))
                act.wait_ge(*proj_ready(l, 40))
                for br, col in enumerate((C_AV, C_BV)):
                    act.copy(vhi[:, 1:5, 256 * br:256 * br + 256], proj[:, 1:5, col:col + 256])
                    act.copy(vhi[:, 5, 256 * br:256 * br + 256], proj[:, 0, col:col + 256])
                act.copy(vhi[:, 0, 0:512], cache[:, 512:1024]).then_inc(v_hi.sem, 1)
                act.wait_ge(*cv_var(l, 1))
                act.activation(cstat[:, 1, :], cstat[:, 0, :], ACT.Sqrt).then_inc(cv_std.sem, 1)
                SCALE = (32 ** -0.5, 64 ** -0.5, 64 ** -0.5)

                def cols(n):
                    kt = 0 if n == TILES else keytile(n)
                    return slice(kt * P, (kt + 1) * P)

                def turned(n, br, src, ready):
                    tk = slice(n * P, (n + 1) * P)
                    act.mul(qThi[:, 2 * br:2 * br + 2, tk], src[:, 0:256].rearrange("p (c n) -> p c n", c=2), SCALE[br])
                    act.copy(kThi[:, 2 * br:2 * br + 2, cols(n)], src[:, 256:512].rearrange("p (c n) -> p c n", c=2)
                             ).then_inc(ready.sem, 1)

                for n in range(TILES + 1):
                    own = n < TILES
                    if own:
                        for br in range(2):
                            act.wait_ge(*ab_t(l, 2 * n + br + 1))
                            turned(n, br, bank(4 + br + 2 * (n % 2)), ab_hi)
                    else:
                        act.wait_ge(*ab_t(l, 11))
                        act.copy(kThi[:, 0:4, cols(n)], bank(6).rearrange("p (c n) -> p c n", c=4)
                                 ).then_inc(ab_hi.sem, 1)
                    act.wait_ge(*cn_t(l, n + 1))
                    if n:
                        act.wait_ge(*up_done(l, n))
                    lo = 0 if own else 256
                    act.copy(cThi[:, lo:384], bank(0)[:, lo:384]).then_inc(cT_hi.sem, 1)
                    act.wait_ge(*up_done(l, n + 1))
                    if n:
                        act.wait_ge(*c_t(l, n))
                    kt = keytile(n) if own else 0
                    kv = bank(2, 384).rearrange("p (h n) -> p h n", h=4)
                    if own:
                        act.copy(qkc[:, 0:256], bank(1, 256))
                    krope = proj[:, n, C_CKR:C_CKR + 32] if own else cache[:, 1152:1184]
                    qk = qkc[:, 256:512].rearrange("p (h n) -> p h n", h=4)
                    act.copy(qk[:, :, 0:32], kv[:, :, 0:32])
                    act.copy(qk[:, :, 32:64], krope.rearrange("p (o n) -> p o n", o=1).to_broadcast([P, 4, 32]))
                    act.copy(vhi[:, kt, 512:768].rearrange("p (h n) -> p h n", h=4), kv[:, :, 32:96]
                             ).then_inc(qkc_raw.sem, 1)
                    act.wait_ge(*c_t(l, n + 1))
                    if own:
                        turned(n, 2, bank(3), c_hi)
                    else:
                        act.copy(kThi[:, 4:6, cols(n)], bank(3)[:, 256:512].rearrange("p (c n) -> p c n", c=2)
                                 ).then_inc(c_hi.sem, 1)
                for ti, tile in enumerate((1, 2, 3, 4, 0)):
                    nk = TOK if tile else P
                    for step in range(HDS + 2):
                        if step < HDS:
                            for m in ((2 * step, 2 * step + 1) if step < 4 else (step + 4,)):
                                old = (m - 4) % MAPS
                                oti = ti - (m < 4)
                                if oti >= 0:
                                    if old < 8:
                                        act.wait_ge(*mix_ready(l, oti * 4 + old // 2 + 1))
                                    else:
                                        act.wait_ge(*pt_done(l, oti * HDS + old - 4 + 1))
                                act.wait_ge(*mx_ready(l, ti * MAPS + m + 1))
                                act.activation(ex[:, m % 4, 0:nk], pr(m % 2)[:, 0:nk], ACT.Exp,
                                               bias=stat[:, 0, m:m + 1], accum_out=stat[:, 1, m:m + 1]
                                               ).then_inc(ex_ready.sem, 1)
                        if 1 <= step <= HDS:
                            hd = step - 1
                            act.wait_ge(*pt_done(l, ti * HDS + hd + 1))
                            if ti or hd >= 2:
                                act.wait_ge(*pv_done(l, ti * HDS + hd - 1))
                            act.copy(pthi[:, hd % 2, 0:nk], pr(2)[:, 0:nk]).then_inc(pt_hi.sem, 1)
                        if step >= 2:
                            hd = step - 2
                            m = 2 * hd if hd < 4 else hd + 4
                            act.wait_ge(*pv_done(l, ti * HDS + hd + 1))
                            act.wait_ge(*rec_ready(l, ti * HDS + hd + 1))
                            if ti and hd == 0:
                                act.wait_ge(*ot_done(l, ti))
                            act.mul(otok[:, hd * 64:(hd + 1) * 64], bank(6 + hd % 2, 64), stat[:, 2, m:m + 1]
                                    ).then_inc(o_ready.sem, 1)
                    act.wait_ge(*ovar_ready(l, ti + 1))
                    act.activation(ostat[:, 1, :], ostat[:, 0, :], ACT.Sqrt).then_inc(ostd_ready.sem, 1)
                    act.wait_ge(*ot_done(l, ti + 1))
                    if ti == 0:
                        act.wait_ge(*own_out(l, 6 * 16))
                    act.copy(oThi[:, :, tile * P:(tile + 1) * P], PS[:, 2, 0:768].rearrange("p (c n) -> p c n", c=6)
                             ).then_inc(ot_hi.sem, 1)
                for b in range(WO_UNITS):
                    high(V_WO + b, b % 2, dst=wohi[:, b, :, :].rearrange("p k n -> p (k n)"))
                for j in range(2):
                    high(V_GATE + j, j)
                with act.Fori(0, KC // 2) as d2:
                    for b in range(4):
                        for c in range(2):
                            act.wait_ge(*g_done(l, d2 * 8 + (2 * b + c + 1)))
                            act.wait_ge(*m_used(l, d2 * 8 + (2 * b + c - 1)))
                            act.activation(sg[:, c, :], pr(c), ACT.Sigmoid,
                                           bias=pcol[:, ds(d2 * 2 + (PC_BG + 8 * b + c), 1)]).then_inc(g_ready.sem, 1)
                        high_at(d2, V_GATE + 2 + b, b % 2, 4)
                    for c in range(2):
                        act.wait_ge(*m_ready(l, d2 * 2 + (c + 1)))
                        act.copy(mhi[:, ds(d2 * 2 + c, 1), :].rearrange("p o n -> p (o n)"), macc[:, c, :]
                                 ).then_inc(m_hi.sem, 1)
                with act.Fori(0, 2) as i:
                    for j in range(2):
                        act.wait_ge(*y_done(l, i * 4 + (2 * j + 2)))
                        high_at(i, V_OUT + 2 + j, j)
                act.wait_ge(*x1_ready(l, 8))
                squares(l, 1)
                modulate(l, 1)
                act.wait_ge(*rmax_ready(l, 1))
                act.activation(ex5[:, :, :], ex5[:, :, :], ACT.Exp).then_inc(rexp_ready.sem, 1)
                act.wait_ge(*dwt_done(l, 1))
                act.copy(dwT, pr(2)[0:16, :]).then_inc(dwT_ready.sem, 1)
                act.wait_ge(*dwT_ready(l, 1))
                act.dma_start(t["dw_rows"], dwT).then_inc(dw_out.sem, 16)
                with act.Fori(0, EXPERTS) as e:
                    for c in range(2):
                        act.wait_ge(*gu_done(l, e * 4 + (c + 1)))
                        act.wait_ge(*gu_mul(l, e * 2))
                        act.activation(sg[:, c, :], pr(c), ACT.Silu).then_inc(silu_ready.sem, 1)
                    high_at(e, V_M1 + 2, 0)
                    act.wait_ge(*gu_done(l, e * 4 + 4))
                    high_at(e, V_M1 + 3, 1)
                    for c in range(2):
                        act.wait_ge(*a_ready(l, e * 2 + (c + 1)))
                        act.copy(acthi[:, ds(e * 2 + c, 1), :].rearrange("p o n -> p (o n)"), mt[:, c, :]
                                 ).then_inc(a_hi.sem, 1)
                with act.Fori(0, 7) as d:
                    for j in range(2):
                        act.wait_ge(*(y2_done if j else half_used)(l, d + 1))
                        high_at(d, V_M2 + 2 + j, j)
            act.wait_ge(*x2_ready(LAYERS - 1, 8))
            squares(LAYERS, 0)
            for k in range(KC):
                act.wait_ge(*fin_t(0, k + 1))
                act.copy(ytok[:, :, k * P:(k + 1) * P], pr(k % 2).rearrange("p (t n) -> p t n", t=TILES)
                         ).then_inc(fin_out.sem, 1)

        @block.gpsimd
        def _(pool):
            with pool.Fori(0, LAYERS) as l:
                def low(count, j, dst=None, n=2048):
                    pool.wait_ge(w_hi.sem, count)
                    hi = whi[j][:, 0:n] if dst is None else dst[0]
                    lo = wlo[j][:, 0:n] if dst is None else dst[1]
                    pool.tensor_tensor(lo, wf[j][:, 0:n], hi, ALU.subtract).then_inc(w_lo.sem, 1)

                with pool.Fori(0, ADA_UNITS // 2) as i:
                    for j in range(2):
                        low(l * V_ALL + i * 2 + (j + 1), j, n=768)
                for u in range(IN_UNITS):
                    low(l * V_ALL + (V_IN + u + 1), u % 2, n=2048 if u < IN_UNITS - 1 else KC * 160)
                for b in range(WO_UNITS):
                    flat = [w[:, b, :, :].rearrange("p k n -> p (k n)") for w in (wohi, wolo)]
                    low(l * V_ALL + (V_WO + b + 1), b % 2, flat)
                with pool.Fori(0, (V_M1 + 2 - V_GATE) // 2) as i:
                    for j in range(2):
                        low(l * V_ALL + i * 2 + (V_GATE + j + 1), j)
                with pool.Fori(0, EXPERTS // 2) as e2:
                    for je in range(2):
                        low(l * V_ALL + e2 * 4 + (V_M1 + 2 * je + 3), 0)
                        low(l * V_ALL + e2 * 4 + (V_M1 + 2 * je + 4), 1)
                        pool.wait_ge(dw_in[je].sem, l * 128 + e2 * 16 + 16)
                        for c in range(2):
                            pool.wait_ge(*gu_mul(l, e2 * 4 + (2 * je + c + 1)))
                            pool.tensor_tensor(mt[:, c, :], mt[:, c, :], dwb[je], ALU.mult).then_inc(a_ready.sem, 1)
                with pool.Fori(0, 7) as d:
                    for j in range(2):
                        low(l * V_ALL + d * 2 + (V_M2 + 2 + j + 1), j)

        @block.vector
        def _(dve):
            dve.memset(ones[:, :], 1.0).then_inc(set_ready.sem, 1)
            dve.wait_ge(*consts_in(0, 7 * 16))
            dve.tensor_copy(band[:, :], bandf[:, :]).then_inc(set_ready.sem, 1)
            dve.nop().then_inc(ada_used.sem, 2)
            dve.nop().then_inc(g_ready.sem, 2)
            dve.nop().then_inc(m_used.sem, 2)
            dve.nop().then_inc(x1_ready.sem, 4)
            dve.nop().then_inc(x2_ready.sem, 2)
            dve.nop().then_inc(a_ready.sem, 4)
            for tile in (1, 3):
                dve.wait_ge(*xt_done(0, tile + 1))
                dve.tensor_copy(xT[:, :, tile * P:(tile + 1) * P], PS[:, tile, :].rearrange("p (k n) -> p k n", k=KC)
                                ).then_inc(x_odd.sem, 1)
            dve.wait_ge(*cond_f(0, 2))
            dve.tensor_tensor(sclo[:, :, :], scf[:, :, :], schi[:, :, :], ALU.subtract)
            dve.tensor_copy(gfin[:, :], PS[:, 1, 2 * KC:3 * KC]).then_inc(cond_ready.sem, 1)

            def root(l, n):
                dve.wait_ge(*sq_used(l, KC * (n + 1)))
                dve.tensor_scalar(rsb[:, :], pr(2), 1.0 / D, EPS, ALU.mult, ALU.add).then_inc(var_ready.sem, 1)
                dve.wait_ge(*std_ready(l, n + 1))
                dve.reciprocal(rsb[:, :], rsb[:, :])
                dve.drain()

            def norm(l, n):
                root(l, n)

                def scaled(k):
                    if k >= 2:
                        dve.wait_ge(*hf_ready(l, KC * n + k - 1))
                    for s, (a, b) in enumerate(SEG):
                        ins = dve.scalar_tensor_tensor(out=tmp[:, k % 2, a:b], in0=xT[:, k, a:b],
                                                       scalar=gs[:, n, k, s:s + 1], in1=rsb[:, a:b],
                                                       op0=ALU.mult, op1=ALU.mult)
                    ins.then_inc(tmp_ready.sem, 1)

                scaled(0)
                for k in range(KC):
                    if k + 1 < KC:
                        scaled(k + 1)
                    dve.wait_ge(*hf_ready(l, KC * n + k + 1))
                    dve.tensor_copy(hhi[:, k, :], hf[:, k % 2, :]).then_inc(hhi_ready.sem, 1)
                    dve.wait_ge(*hhi_ready(l, KC * n + k + 1))
                    dve.tensor_tensor(hlo[:, k, :], hf[:, k % 2, :], hhi[:, k, :], ALU.subtract
                                      ).then_inc(h_ready.sem, 1)

            def bc(ap, shape):
                return ap.to_broadcast(shape)

            with dve.Fori(0, LAYERS) as l:
                dve.wait_ge(*par_t(l, 1))
                dve.tensor_copy(pcol[:, :], bank(6)[:, 0:PC_N])
                dve.tensor_copy(cw[:, :, :], bank(6)[:, 104:168].rearrange("p (c n) -> p c n", c=2)[:, :, 0:CONV_K])
                dve.tensor_copy(rpf[:, :], bank(6)[0:31, 168:228]).then_inc(par_ready.sem, 1)
                dve.drain()
                dve.tensor_copy(rp[:, 0, :], rpf[:, :])
                dve.drain()
                dve.tensor_tensor(rpd[:, :], rpf[:, :], rp[:, 0, :], ALU.subtract)
                dve.drain()
                dve.tensor_copy(rp[:, 1, :], rpd[:, :])
                dve.drain()
                dve.tensor_tensor(rpf[:, :], rpd[:, :], rp[:, 1, :], ALU.subtract)
                dve.drain()
                dve.tensor_copy(rp[:, 2, :], rpf[:, :]).then_inc(rp_ready.sem, 1)
                dve.wait_ge(*params_in(l, 21 * 16))
                dve.tensor_tensor(lamt[:, 0:64].rearrange("p (a n) -> p a n", a=2), lamv[:, 0:4:2, :], lamv[:, 1:4:2, :],
                                  ALU.mult)
                dve.drain()
                dve.tensor_reduce(lamt[:, 64:66], lamt[:, 0:64].rearrange("p (a n) -> p a n", a=2), AX_X, ALU.add
                                  ).then_inc(lam_sum.sem, 1)
                dve.tensor_scalar(rowg[:, 0:64], rowg[:, 0:64], lamc[:, 1:2], None, ALU.mult)
                dve.wait_ge(*wu_hi(l, 1))
                dve.tensor_tensor(wulo[:, :], wuf[:, :], wuhi[:, :], ALU.subtract).then_inc(wu_ready.sem, 1)
                dve.wait_ge(*lam_exp(l, 1))
                dve.tensor_tensor(lamt[:, 68:69], lamt[:, 67:68], lamt[:, 66:67], ALU.subtract)
                dve.drain()
                dve.tensor_tensor(lamt[:, 69:70], lamt[:, 68:69], lamc[:, 0:1], ALU.subtract)
                nlam = lamt[:, 69:70]
                for g in range(8):
                    dve.wait_ge(*band_done(l, g + 1))
                    for half in range(2):
                        ps = slice(64 * half, 64 * half + 64)
                        src = bank(g % 4, 480)[ps, :].rearrange("p (k h r) -> p h r k", k=8, h=4)
                        m = maskb[ps, 8 * g:8 * g + 8].rearrange("p (a b k) -> p a b k", a=1, b=1)
                        ins = dve.tensor_tensor(bias[ps, :, :, 8 * g:8 * g + 8], src[:, :, 1 - half:15 - half, :],
                                                bc(m, [64, 4, 14, 8]), ALU.add)
                    ins.then_inc(bias_ready.sem, 1)
                with dve.Fori(0, ADA_UNITS // 2) as i:
                    for j in range(2):
                        dve.wait_ge(w_hi.sem, l * V_ALL + i * 2 + (j + 1))
                        dve.tensor_tensor(wlo[j][:, 768:2048], wf[j][:, 768:2048], whi[j][:, 768:2048], ALU.subtract
                                          ).then_inc(w_lo_dve.sem, 1)
                dve.wait_ge(*ada_used(l, ADA_UNITS))
                dve.tensor_tensor(ada[:, :, :], PS[:, 3, 512:608].rearrange("p (k s) -> p k s", s=2),
                                  bc(pcol[:, PC_ADA:PC_G1].rearrange("p (k o) -> p k o", o=1), [P, 48, 2]), ALU.add)
                dve.drain()
                for n, g in enumerate((PC_G1, PC_G2)):
                    ins = dve.scalar_tensor_tensor(out=gs[:, n, :, :], in0=ada[:, 24 * n + 8:24 * n + 16, :], scalar=1.0,
                                                   in1=bc(pcol[:, g:g + 8].rearrange("p (k o) -> p k o", o=1), [P, 8, 2]),
                                                   op0=ALU.add, op1=ALU.mult)
                ins.then_inc(ada_ready.sem, 1)
                dve.drain()
                norm(l, 0)
                dve.wait_ge(*sig_ready(l, 1))
                for a, b in ((0, PAD), (PAD + CTX, 2 * PAD + CTX), (2 * PAD + TOK, 3 * PAD + TOK)):
                    dve.memset(zpad[:, :, a:b], 0.0)
                for c in range(2):
                    dve.wait_ge(*sig_ready(l, c + 1))
                    for (a, b), z0 in zip(SEG, (PAD, 2 * PAD)):
                        ins = dve.tensor_tensor(zpad[:, c, z0 + a:z0 + b], pr(c)[:, a:b], zsg[:, c, a:b], ALU.mult)
                    ins.then_inc(z_ready.sem, 1)
                NZ = TOK + PAD
                for k in range(CONV_K):
                    dve.drain()
                    for c in range(2):
                        if k == 0:
                            dve.tensor_scalar(zacc[:, c, :], zpad[:, c, 0:NZ], cw[:, c, 0:1],
                                              pcol[:, PC_CB + c:PC_CB + c + 1], ALU.mult, ALU.add)
                        else:
                            ins = dve.scalar_tensor_tensor(out=zacc[:, c, :], in0=zpad[:, c, k:k + NZ],
                                                           scalar=cw[:, c, k:k + 1], in1=zacc[:, c, :],
                                                           op0=ALU.mult, op1=ALU.add)
                ins.then_inc(cv_ready.sem, 1)
                dve.wait_ge(*mu_done(l, 1))
                dve.tensor_scalar(rsb[:, :], pr(0), 1.0 / CONV_CH, None, ALU.mult)
                dve.drain()
                for c in range(2):
                    for (a, b), z0 in zip(SEG, (0, PAD)):
                        ins = dve.tensor_tensor(zc[:, c, a:b], zacc[:, c, z0 + a:z0 + b], rsb[:, a:b], ALU.subtract)
                    ins.then_inc(zc_ready.sem, 1)
                dve.drain()
                dve.wait_ge(*zv_done(l, 1))
                dve.tensor_scalar(rsb[:, :], pr(1), 1.0 / CONV_CH, EPS, ALU.mult, ALU.add).then_inc(zvar_ready.sem, 1)
                dve.wait_ge(*zstd_ready(l, 1))
                dve.reciprocal(rsb[:, :], rsb[:, :])
                dve.drain()
                for c in range(2):
                    dve.tensor_tensor(zc[:, c, :], zc[:, c, :], rsb[:, :], ALU.mult).then_inc(zn_ready.sem, 1)
                dve.drain()
                for c in range(2):
                    dve.wait_ge(*zs_ready(l, c + 1))
                    dve.tensor_copy(zhi[:, c, :], zs[:, c, :])
                dve.drain()
                ins = dve.tensor_tensor(zlo[:, :, :], zs[:, :, :], zhi[:, :, :], ALU.subtract).then_inc(z_split.sem, 1)
                dve.drain()
                dve.wait_ge(*proj_ready(l, 40))
                cq2 = csq[:, 0:1280].rearrange("p (t n) -> p t n", t=TILES)
                ck2 = csq[:, 1280:1920].rearrange("p (t n) -> p t n", t=TILES)
                dve.tensor_tensor(cq2, proj[:, :, C_CQ:C_CKV], proj[:, :, C_CQ:C_CKV], ALU.mult)
                dve.tensor_tensor(ck2, proj[:, :, C_CKV:C_CKR], proj[:, :, C_CKV:C_CKR], ALU.mult)
                dve.drain()
                dve.tensor_reduce(cstat[:, 2, 0:5], cq2, AX_X, ALU.add)
                dve.tensor_reduce(cstat[:, 2, 5:10], ck2, AX_X, ALU.add)
                dve.drain()
                dve.tensor_scalar(cstat[:, 0, 0:5], cstat[:, 2, 0:5], 1.0 / 256, EPS, ALU.mult, ALU.add)
                dve.tensor_scalar(cstat[:, 0, 5:10], cstat[:, 2, 5:10], 1.0 / 128, EPS, ALU.mult, ALU.add
                                  ).then_inc(cv_var.sem, 1)
                dve.wait_ge(*cv_std(l, 1))
                dve.reciprocal(cstat[:, 2, :], cstat[:, 1, :])
                dve.wait_ge(*v_hi(l, 1))
                for br, col in enumerate((C_AV, C_BV)):
                    w = slice(256 * br, 256 * br + 256)
                    dve.tensor_tensor(vlo[:, 1:5, w], proj[:, 1:5, col:col + 256], vhi[:, 1:5, w], ALU.subtract)
                    dve.tensor_tensor(vlo[:, 5, w], proj[:, 0, col:col + 256], vhi[:, 5, w], ALU.subtract)
                dve.tensor_tensor(vlo[:, 0, 0:512], cache[:, 512:1024], vhi[:, 0, 0:512], ALU.subtract
                                  ).then_inc(v_ready.sem, 1)
                SCALE = (32 ** -0.5, 64 ** -0.5, 64 ** -0.5)

                def rotate(src, out, tile, heads):
                    c = cosb[:, tile - 1:tile, :]
                    r1 = rope1[:, 0:heads * 32].rearrange("p (h n) -> p h n", n=32)
                    r2 = rope2[:, 0:heads * 32].rearrange("p (h n) -> p h n", n=32)
                    dve.tensor_tensor(r1, src, bc(c, [P, heads, 32]), ALU.mult)
                    for half in range(2):
                        for a in range(2):
                            o = 16 * a + 8 * half
                            i = 16 * a + 8 * (1 - half)
                            dve.tensor_tensor(r2[:, :, o:o + 8], src[:, :, i:i + 8],
                                              bc(sinb[:, tile - 1:tile, o:o + 8], [P, heads, 8]), ALU.mult)
                    dve.drain()
                    return dve.tensor_tensor(out, r1, r2, ALU.add)

                def cols(n):
                    kt = 0 if n == TILES else keytile(n)
                    return slice(kt * P, (kt + 1) * P)

                def turned(n, br, src, ready):
                    tk = slice(n * P, (n + 1) * P)
                    b2 = slice(2 * br, 2 * br + 2)
                    dve.scalar_tensor_tensor(out=qTlo[:, b2, tk], in0=src[:, 0:256].rearrange("p (c n) -> p c n", c=2),
                                             scalar=SCALE[br], in1=qThi[:, b2, tk], op0=ALU.mult, op1=ALU.subtract)
                    dve.tensor_tensor(kTlo[:, b2, cols(n)], src[:, 256:512].rearrange("p (c n) -> p c n", c=2),
                                      kThi[:, b2, cols(n)], ALU.subtract).then_inc(ready.sem, 1)

                for n in range(TILES + 1):
                    own = n < TILES
                    dve.drain()
                    if own and n:
                        dve.wait_ge(*ab_t(l, 2 * n - 1))
                        rotate(proj[:, n, 0:512].rearrange("p (h n) -> p h n", n=32),
                               roped.rearrange("p (h n) -> p h n", n=32), n, 16).then_inc(roped_ready.sem, 1)
                    elif not n:
                        dve.nop().then_inc(roped_ready.sem, 1)
                    if own:
                        if n:
                            dve.wait_ge(*cn_t(l, n))
                        for a, b, r, g in ((0, 256, n, 64), (256, 384, 5 + n, 320)):
                            ins = dve.scalar_tensor_tensor(out=cn[:, a:b], in0=proj[:, n, C_CQ + a:C_CQ + b],
                                                           scalar=cstat[:, 2, r:r + 1], in1=rowg[:, g:g + b - a],
                                                           op0=ALU.mult, op1=ALU.mult)
                        if n == 0:
                            dve.drain()
                            ins = dve.scalar_tensor_tensor(out=proj[:, 0, C_CKV:C_CKR], in0=proj[:, 0, C_CKV:C_CKR],
                                                           scalar=cstat[:, 2, 5:6], in1=rowg[:, 320:448],
                                                           op0=ALU.mult, op1=ALU.mult)
                        ins.then_inc(cn_ready.sem, 1)
                        for br in range(2):
                            dve.wait_ge(*ab_hi(l, 2 * n + br + 1))
                            turned(n, br, bank(4 + br + 2 * (n % 2)), ab_ready)
                    else:
                        dve.nop().then_inc(cn_ready.sem, 1)
                        dve.wait_ge(*ab_hi(l, 11))
                        dve.tensor_tensor(kTlo[:, 0:4, cols(n)], bank(6).rearrange("p (c n) -> p c n", c=4),
                                          kThi[:, 0:4, cols(n)], ALU.subtract).then_inc(ab_ready.sem, 1)
                    dve.wait_ge(*cT_hi(l, n + 1))
                    lo = 0 if own else 256
                    dve.tensor_tensor(cTlo[:, lo:384], bank(0)[:, lo:384], cThi[:, lo:384], ALU.subtract
                                      ).then_inc(cT_ready.sem, 1)
                    dve.wait_ge(*qkc_raw(l, n + 1))
                    kt = keytile(n) if own else 0
                    dve.tensor_tensor(vlo[:, kt, 512:768].rearrange("p (h n) -> p h n", h=4),
                                      bank(2, 384).rearrange("p (h n) -> p h n", h=4)[:, :, 32:96],
                                      vhi[:, kt, 512:768].rearrange("p (h n) -> p h n", h=4), ALU.subtract
                                      ).then_inc(up_free.sem, 1)
                    if own and n:
                        v = qkc.rearrange("p (h n) -> p h n", h=8)[:, :, 32:64]
                        dve.drain()
                        rotate(v, v, n, 8).then_inc(qkc_ready.sem, 1)
                    else:
                        dve.nop().then_inc(qkc_ready.sem, 1)
                    dve.wait_ge(*c_hi(l, n + 1))
                    if own:
                        turned(n, 2, bank(3), c_ready)
                    else:
                        dve.tensor_tensor(kTlo[:, 4:6, cols(n)], bank(3)[:, 256:512].rearrange("p (c n) -> p c n", c=2),
                                          kThi[:, 4:6, cols(n)], ALU.subtract).then_inc(c_ready.sem, 1)
                for ti, tile in enumerate((1, 2, 3, 4, 0)):
                    nk = TOK if tile else P
                    for step in range(HDS + 2):
                        if step < HDS:
                            for m in ((2 * step, 2 * step + 1) if step < 4 else (step + 4,)):
                                dve.wait_ge(*s_done(l, ti * MAPS + m + 1))
                                if 8 <= m < 12 and tile:
                                    s0 = 6 - 2 * (tile - 1)
                                    dve.tensor_tensor(pr(m % 2)[:, CTX:TOK], pr(m % 2)[:, CTX:TOK],
                                                      bias[:, m - 8, s0:s0 + 8, :].rearrange("p r c -> p (r c)"), ALU.add)
                                    dve.drain()
                                dve.tensor_reduce(stat[:, 0, m:m + 1], pr(m % 2)[:, 0:nk], AX_X, ALU.max, negate=True
                                                  ).then_inc(mx_ready.sem, 1)
                        if 1 <= step <= HDS:
                            hd = step - 1
                            dve.wait_ge(*pt_hi(l, ti * HDS + hd + 1))
                            dve.tensor_tensor(ptlo[:, hd % 2, 0:nk], pr(2)[:, 0:nk], pthi[:, hd % 2, 0:nk], ALU.subtract
                                              ).then_inc(pt_ready.sem, 1)
                        if step < HDS:
                            m = 2 * step if step < 4 else step + 4
                            nm = 2 if step < 4 else 1
                            dve.wait_ge(*ex_ready(l, ti * MAPS + m + nm))
                            dve.reciprocal(stat[:, 2, m:m + nm], stat[:, 1, m:m + nm]).then_inc(rec_ready.sem, 1)
                            if step < 4:
                                dve.drain()
                                dve.scalar_tensor_tensor(out=cfa[:, 0, step:step + 1], in0=stat[:, 1, m:m + 1],
                                                         scalar=nlam, in1=stat[:, 2, m + 1:m + 2],
                                                         op0=ALU.mult, op1=ALU.mult)
                                dve.drain()
                                if step >= 2:
                                    dve.wait_ge(*pt_done(l, ti * HDS + step - 1))
                                dve.scalar_tensor_tensor(out=wmix[:, step % 2, 0:nk], in0=ex[:, (m + 1) % 4, 0:nk],
                                                         scalar=cfa[:, 0, step:step + 1], in1=ex[:, m % 4, 0:nk],
                                                         op0=ALU.mult, op1=ALU.add).then_inc(mix_ready.sem, 1)
                    dve.wait_ge(*o_ready(l, (ti + 1) * HDS))
                    oa = otok[:, 0:256].rearrange("p (h n) -> p h n", h=4)
                    dve.tensor_tensor(osq, otok[:, 0:256], otok[:, 0:256], ALU.mult)
                    dve.drain()
                    dve.tensor_reduce(ostat[:, 2, :], osq.rearrange("p (h n) -> p h n", h=4), AX_X, ALU.add)
                    dve.drain()
                    dve.tensor_scalar(ostat[:, 0, :], ostat[:, 2, :], 1.0 / 64, EPS, ALU.mult, ALU.add
                                      ).then_inc(ovar_ready.sem, 1)
                    dve.wait_ge(*ostd_ready(l, ti + 1))
                    dve.reciprocal(ostat[:, 2, :], ostat[:, 1, :])
                    dve.drain()
                    dve.tensor_tensor(oa, oa, bc(ostat[:, 2, :].rearrange("p (h o) -> p h o", o=1), [P, 4, 64]), ALU.mult)
                    dve.drain()
                    dve.tensor_tensor(oa, oa, bc(rowg[:, 0:64].rearrange("p (o n) -> p o n", o=1), [P, 4, 64]), ALU.mult
                                      ).then_inc(on_ready.sem, 1)
                    dve.wait_ge(*ot_hi(l, ti + 1))
                    if ti == 0:
                        dve.wait_ge(*own_out(l, 6 * 16)) 
                    dve.tensor_tensor(oTlo[:, :, tile * P:(tile + 1) * P],
                                      PS[:, 2, 0:768].rearrange("p (c n) -> p c n", c=6),
                                      oThi[:, :, tile * P:(tile + 1) * P], ALU.subtract).then_inc(ot_ready.sem, 1)
                with dve.Fori(0, KC // 2) as d2:
                    for b in range(4):
                        for c in range(2):
                            dve.drain()
                            dve.wait_ge(*b_done(l, d2 * 8 + (2 * b + c + 1)))
                            dve.wait_ge(*g_ready(l, d2 * 8 + (2 * b + c + 1)))
                            dst = mt[:, c, :] if b else macc[:, c, :]
                            dve.tensor_tensor(dst, pr(2 + c), sg[:, c, :], ALU.mult).then_inc(m_used.sem, 1)
                            if b:
                                dve.drain()
                                ins = dve.tensor_tensor(macc[:, c, :], macc[:, c, :], mt[:, c, :], ALU.add)
                            if b == 3:
                                ins.then_inc(m_ready.sem, 1)
                    for c in range(2):
                        dve.wait_ge(*m_hi(l, d2 * 2 + (c + 1)))
                        dve.tensor_tensor(mlo[:, ds(d2 * 2 + c, 1), :].rearrange("p o n -> p (o n)"), macc[:, c, :],
                                          mhi[:, ds(d2 * 2 + c, 1), :].rearrange("p o n -> p (o n)"), ALU.subtract
                                          ).then_inc(m_split.sem, 1)

                def residual(k, pair, gate, ready):
                    for s, (a, b) in enumerate(SEG):
                        xk = xT[:, ds(k, 1), a:b].rearrange("p o n -> p (o n)")
                        ins = dve.scalar_tensor_tensor(out=xk, in0=pr(pair)[:, a:b],
                                                       scalar=ada[:, ds(k + gate, 1), s:s + 1].rearrange("p o n -> p (o n)"),
                                                       in1=xk, op0=ALU.mult, op1=ALU.add)
                    ins.then_inc(ready.sem, 1)

                with dve.Fori(0, 2) as i:
                    for c in range(4):
                        dve.wait_ge(*y_done(l, i * 4 + (c + 1)))
                        residual(i * 4 + c, c, 16, x1_ready)
                dve.wait_ge(*x1_ready(l, 8))
                norm(l, 1)
                dve.drain()
                dve.wait_ge(*hf_used(l, KC))
                dve.tensor_scalar(lgT, pr(3)[0:20, :], rbias[:, 0:1], None, ALU.add).then_inc(lg_ready.sem, 1)
                dve.wait_ge(*lgt_done(l, 1))
                dve.tensor_copy(route[:, :, :], bank(4, 100).rearrange("p (t n) -> p t n", t=TILES))
                dve.drain()

                def col(n, shape):
                    return bc(rcol[:, n, :].rearrange("p (t o) -> p t o", o=1), shape)

                T4 = [P, TILES, 4]

                def first_max(src, out, n):
                    dve.tensor_reduce(rcol[:, n, :], src, AX_X, ALU.max)
                    dve.drain()
                    dve.tensor_tensor(out, src, col(n, T4), ALU.is_equal)
                    dve.drain()
                    dve.tensor_tensor(out, out, bc(tie[:, :].rearrange("p (o n) -> p o n", o=1), T4), ALU.mult)
                    dve.drain()
                    dve.tensor_reduce(rcol[:, 7, :], out, AX_X, ALU.max)
                    dve.drain()
                    dve.tensor_tensor(out, out, col(7, T4), ALU.is_equal)
                    dve.drain()

                lg = route[:, :, 0:4]
                oh, oh1, oh2, sel, sel2 = (rw[:, :, 16 + 4 * q:20 + 4 * q] for q in range(5))
                first_max(lg, oh, 0)
                dve.tensor_tensor(ex5[:, :, 0:4], lg, col(0, T4), ALU.subtract)
                w16 = rw[:, :, 0:16].rearrange("p t (g e) -> p t g e", g=4)
                for g in range(4):
                    dve.tensor_tensor(rw[:, :, 4 * g:4 * g + 4], route[:, :, 4 + 4 * g:8 + 4 * g],
                                      bc(oh[:, :, g:g + 1], T4), ALU.mult)
                dve.drain()
                dve.tensor_reduce(sel, rw[:, :, 0:16].rearrange("p t (g e) -> p t e g", g=4), AX_X, ALU.add)
                dve.drain()
                first_max(sel, oh1, 1)
                dve.scalar_tensor_tensor(out=sel2, in0=oh1, scalar=NEG, in1=sel, op0=ALU.mult, op1=ALU.add)
                dve.drain()
                first_max(sel2, oh2, 2)
                dve.tensor_tensor(ex5[:, :, 4], rcol[:, 2, :], rcol[:, 1, :], ALU.subtract).then_inc(rmax_ready.sem, 1)
                dve.wait_ge(*rexp_ready(l, 1))
                dve.tensor_reduce(rcol[:, 3, :], ex5[:, :, 0:4], AX_X, ALU.add)
                dve.tensor_scalar(rcol[:, 4, :], ex5[:, :, 4], 1.0, None, ALU.add)
                dve.drain()
                dve.tensor_tensor(rcol[:, 5, :], rcol[:, 3, :], rcol[:, 4, :], ALU.mult)
                dve.drain()
                dve.reciprocal(rcol[:, 3, :], rcol[:, 5, :])
                dve.drain()
                dve.tensor_tensor(rcol[:, 4, :], rcol[:, 3, :], ex5[:, :, 4], ALU.mult)
                dve.drain()
                dve.tensor_tensor(oh1, oh1, col(3, T4), ALU.mult)
                dve.tensor_tensor(oh2, oh2, col(4, T4), ALU.mult)
                dve.drain()
                dve.tensor_tensor(sel, oh1, oh2, ALU.add)
                dve.drain()
                for g in range(4):
                    ins = dve.tensor_tensor(rw[:, :, 4 * g:4 * g + 4], sel, bc(oh[:, :, g:g + 1], T4), ALU.mult)
                ins.then_inc(dw_ready.sem, 1)
                with dve.Fori(0, EXPERTS) as e:
                    for c in range(2):
                        dve.drain()
                        dve.wait_ge(*gu_done(l, e * 4 + (c + 3)))
                        dve.wait_ge(*silu_ready(l, e * 2 + (c + 1)))
                        dve.tensor_tensor(mt[:, c, :], pr(2 + c), sg[:, c, :], ALU.mult).then_inc(gu_mul.sem, 1)
                    for c in range(2):
                        dve.wait_ge(*a_hi(l, e * 2 + (c + 1)))
                        dve.tensor_tensor(actlo[:, ds(e * 2 + c, 1), :].rearrange("p o n -> p (o n)"), mt[:, c, :],
                                          acthi[:, ds(e * 2 + c, 1), :].rearrange("p o n -> p (o n)"), ALU.subtract
                                          ).then_inc(a_split.sem, 1)
                with dve.Fori(0, KC // 2) as d2:
                    for jd in range(2):
                        dve.wait_ge(*y2_done(l, d2 * 2 + (jd + 1)))
                        residual(d2 * 2 + jd, jd, 40, x2_ready)
            root(LAYERS, 0)
            for k in range(KC):
                if k >= 2:
                    dve.wait_ge(*fin_t(0, k - 1))
                dve.scalar_tensor_tensor(out=tmp[:, k % 2, :], in0=xT[:, k, :], scalar=gfin[:, k:k + 1], in1=rsb[:, :],
                                         op0=ALU.mult, op1=ALU.mult).then_inc(fin_ready.sem, 1)


_INS = ['x_prompt', 'x_sample', 'cache_a_k', 'cache_a_v', 'cache_b_k', 'cache_b_v', 'cache_c_kv', 'cache_c_krope',
        'c', 'c_ctx', 'norm1_g', 'norm2_g', 'w_ada', 'b_ada', 'w_in', 'a_lambda', 'a_subln_g', 'a_wo', 'b_rpb', 'b_wo',
        'c_q_norm_g', 'c_kv_norm_g', 'c_wuq', 'c_wukv', 'c_wo', 'd_conv_w', 'd_conv_b', 'd_ln_g', 'd_ln_b', 'd_wo',
        'w_gate', 'b_gate', 'w_out', 'moe_w_group', 'moe_b_group', 'moe_w_expert', 'moe_b_expert', 'moe_w1', 'moe_w2',
        'final_norm_g']
_OUTS = [('y_prompt', (1, 128, 1024)), ('y_sample', (1, 512, 1024)), ('new_a_k', (1, 2, 128, 4, 64)),
         ('new_a_v', (1, 2, 128, 4, 64)), ('new_b_k', (1, 2, 128, 4, 64)), ('new_b_v', (1, 2, 128, 4, 64)),
         ('new_c_kv', (1, 2, 128, 128)), ('new_c_krope', (1, 2, 128, 32))]


def shape_constants():
    f = np.float32
    h = 8
    tok = np.arange(LAT)
    inv = (f(10000.0) ** (-np.arange(h, dtype=f) / f(h))).astype(f)
    ar = (tok // GRID_W).astype(f)[:, None] * inv[None, :]
    ac = (tok % GRID_W).astype(f)[:, None] * inv[None, :]
    ang = np.concatenate([ar, ar, ac, ac], axis=-1)
    sign = np.repeat(np.array([-1, 1, -1, 1], dtype=f), h)
    cos = np.cos(ang).astype(f).reshape(4, P, 32).transpose(1, 0, 2)
    sin = (np.sin(ang).astype(f) * sign).reshape(4, P, 32).transpose(1, 0, 2)
    q = np.arange(P) % GRID_W
    start = np.clip(q - 8, 0, GRID_W - 16)[:, None]
    k = np.arange(GRID_W)[None, :]
    mask = np.where((k >= start) & (k < start + 16), 0.0, NEG).astype(f)
    j, w = np.arange(31)[:, None], np.arange(207)[None, :]
    band = ((w + j == 94) | (w + j == 94 + 64)).astype(f)
    init = [0.8 - 0.6 * math.exp(-0.3 * layer) for layer in range(LAYERS)]
    return {
        'k_ident': np.eye(P, dtype=f), 'k_cos': np.ascontiguousarray(cos), 'k_sin': np.ascontiguousarray(sin),
        'k_mask': mask, 'k_band': band, 'k_tie': np.tile(np.array([4, 3, 2, 1], dtype=f), (P, 1)),
        'k_lam': np.array([[x, 1.0 - x] for x in init], dtype=f),
    }


def kernel(**inputs):
    import numpy as _np
    import concourse.bacc as _bacc
    from concourse.bass_utils import run_bass_kernel_spmd as _run

    nc = _bacc.Bacc("TRN2", target_bir_lowering=False, num_devices=1)
    arrays, aps = {}, {}
    given = {name: _np.ascontiguousarray(inputs[name]) for name in _INS}
    for name, a in {**given, **shape_constants()}.items():
        arrays[f"in_{name}"] = a
        aps[name] = nc.dram_tensor(f"in_{name}", a.shape, mybir.dt.from_np(a.dtype), kind="ExternalInput").ap()
    for name, shape in _OUTS:
        aps[name] = nc.dram_tensor(f"out_{name}", shape, F32, kind="ExternalOutput").ap()
    aps["dw_rows"] = nc.dram_tensor("dw_rows", [EXPERTS, TOK], F32, kind="Internal").ap()
    build(nc, aps)
    r = _run(nc, [arrays], core_ids=[0])
    return tuple(r.results[0][f"out_{name}"] for name, _ in _OUTS)
```

```python
import math
from contextlib import ExitStack

import concourse.bass as bass
import numpy as np
from concourse import mybir

F32 = mybir.dt.float32
F16 = mybir.dt.float16
BF16 = mybir.dt.bfloat16
I32 = mybir.dt.int32
ALU = mybir.AluOpType
ACT = mybir.ActivationFunctionType
AX_X = mybir.AxisListType.X
ds = bass.ds

P = 128
LAYERS = 2
D = 1024
KC = D // P
CTX, LAT = 128, 512
TOK = CTX + LAT
TILES = TOK // P
EPS = 1e-6
GRID_W = 64
CONV_K, CONV_CH = 31, 256
PAD = CONV_K // 2
IN_COLS = 2464
HEADS = 4
EXPERTS, F_EXP = 16, 256
N_GROUPS = 4
NEG = -1e30

C_AQ, C_AV, C_BQ, C_BV, C_CQ, C_CKV, C_CKR, C_DU = 0, 512, 768, 1280, 1536, 1792, 1920, 1952
TOKCOLS = C_DU

ADA_UNITS = 6 * D // 256
IN_UNITS = 10
WO_UNITS = 4
GATE_UNITS = 16
OUT_UNITS = 4
V_IN = ADA_UNITS
V_WO = V_IN + IN_UNITS
V_GATE = V_WO + WO_UNITS
V_OUT = V_GATE + GATE_UNITS
V_ALL = V_OUT + OUT_UNITS

CHUNKS = (2 * TOK + EXPERTS * (P - 1)) // P
PAIRS = (CHUNKS - 1) // 2
A_SCALE = 1.0 / 16

PC_ADA, PC_G1, PC_G2, PC_BG, PC_CB, PC_LG, PC_LB, PC_N = 0, 48, 56, 64, 96, 98, 100, 102

MAPS = 16
HDS = 12


class Signal:

    def __init__(self, sem, per_layer, before=0):
        self.sem, self.per_layer, self.before = sem, per_layer, before

    def __call__(self, layer, n):
        return self.sem, layer * self.per_layer + (self.before + n)


def build(nc, t):
    ctx = ExitStack()
    with ctx:
        def sb(name, shape, dt=F32):
            return ctx.enter_context(nc.sbuf_tensor(name, shape, dt))

        def sig(name, per_layer=0, before=0):
            return Signal(ctx.enter_context(nc.semaphore(name)), per_layer, before)

        xT = sb("xT", [P, KC, TOK])
        hpart = sb("hpart", [P, KC * TOK])
        hhi = hpart[:, 0:KC * TOK // 2].bitcast(F16).rearrange("p (k n) -> p k n", k=KC)
        hlo = hpart[:, KC * TOK // 2:KC * TOK].bitcast(F16).rearrange("p (k n) -> p k n", k=KC)
        wf = [sb(f"wf{j}", [P, 2048]) for j in range(2)]
        whi = [sb(f"whi{j}", [P, 2048], F16) for j in range(2)]
        wlo = [sb(f"wlo{j}", [P, 2048], F16) for j in range(2)]
        arena = sb("arena", [P, 23072])
        scratch = sb("scratch", [P, 4100])
        bias = sb("bias", [P, HEADS, 14, GRID_W])
        rsb = sb("rsb", [P, TOK])
        zhi = rsb[:, :].bitcast(F16).rearrange("p (c n) -> p c n", c=2)
        zlo = sb("zlo", [P, 2, TOK], F16)
        ident = sb("ident", [P, P])
        ones = sb("ones", [P, P])
        cosb = sb("cosb", [P, TILES - 1, 32])
        sinb = sb("sinb", [P, TILES - 1, 32])
        band = sb("band", [31, 207], BF16)
        prow = scratch[0:PC_N, 1152:1280]
        pcol = sb("pcol", [P, PC_N])
        cwrow = scratch[0:CONV_K, 896:1152]
        cw = sb("cw", [P, 2, CONV_K])
        rowg = sb("rowg", [P, 64 + 256 + 128])
        lamc = sb("lamc", [P, 2])
        lamt = sb("lamt", [P, 72])
        wr = sb("wr", [P, KC, 20])
        rbias = sb("rbias", [20, 1])
        gfin = sb("gfin", [P, KC])
        scf = sb("scf", [P, KC, 2])
        schi = sb("schi", [P, KC, 2], F16)
        sclo = sb("sclo", [P, KC, 2], F16)
        ada = sb("ada", [P, 6 * KC, 2])
        gs = sb("gs", [P, 2, KC, 2])
        stat = sb("stat", [P, 3, MAPS])
        cfa = sb("cfa", [P, 2, 4])
        cstat = sb("cstat", [P, 3, 10])
        ostat = sb("ostat", [P, 3, 4])
        wuf = scratch[:, 0:896]
        lamv = scratch[:, 1280:1408].rearrange("p (a n) -> p a n", a=4)
        rprow = scratch[0:60, 1408:1439]
        rpf = scratch[0:31, 1440:1500]
        rpd = scratch[0:31, 1500:1560]
        rp = scratch[0:31, 1560:1650].bitcast(BF16).rearrange("p (a n) -> p a n", a=3)
        maskb = scratch[:, 2040:2104]
        bandf = scratch[0:31, 1700:1907]
        crow = scratch[0:3 * KC, 1910:2038]
        wuhi = sb("wuhi", [P, 2 * 256 + 384], F16)
        wulo = sb("wulo", [P, 2 * 256 + 384], F16)
        PS = ctx.enter_context(nc.psum_tensor("PS", [P, 4, 1024], F32))

        proj = arena[:, 0:TILES * TOKCOLS].rearrange("p (t n) -> p t n", t=TILES)
        AR = TILES * TOKCOLS * 2
        ab = arena[:, :].bitcast(F16)
        kThi = ab[:, AR:AR + 4608].rearrange("p (c k) -> p c k", c=6)
        kTlo = ab[:, AR + 4608:AR + 9216].rearrange("p (c k) -> p c k", c=6)
        vhi = ab[:, AR + 9216:AR + 13824].rearrange("p (c k) -> p c k", c=6)
        vlo = ab[:, AR + 13824:AR + 18432].rearrange("p (c k) -> p c k", c=6)
        qThi = ab[:, AR + 18432:AR + 22272].rearrange("p (c k) -> p c k", c=6)
        qTlo = ab[:, AR + 22272:AR + 26112].rearrange("p (c k) -> p c k", c=6)
        oThi = ab[:, 0:3840].rearrange("p (c k) -> p c k", c=6)
        oTlo = ab[:, 3840:7680].rearrange("p (c k) -> p c k", c=6)
        pthi = ab[:, 7680:8960].rearrange("p (s k) -> p s k", s=2)
        ptlo = ab[:, 8960:10240].rearrange("p (s k) -> p s k", s=2)
        otok = arena[:, 5120:5888]
        wohi = ab[:, AR:AR + 8192].rearrange("p (b c n) -> p b c n", b=4, c=2)
        wolo = ab[:, AR + 8192:AR + 16384].rearrange("p (b c n) -> p b c n", b=4, c=2)
        mhi = ab[:, AR + 16384:AR + 21504].rearrange("p (c k) -> p c k", c=KC)
        mlo = ab[:, AR + 21504:AR + 26624].rearrange("p (c k) -> p c k", c=KC)
        mwf = [wf[0][:, :], wf[1][:, :]] + [arena[:, 2048 * n:2048 * (n + 1)] for n in range(4)]
        mpt = [arena[:, 8192 + 1024 * n:8192 + 1024 * (n + 1)].bitcast(F16) for n in range(8)]
        mwhi = [whi[0][:, :], whi[1][:, :]] + mpt[0:4]
        mwlo = [wlo[0][:, :], wlo[1][:, :]] + mpt[4:8]
        htok = arena[:, 16384:16384 + TILES * D].rearrange("p (t n) -> p t n", t=TILES)
        xg = [hpart[:, 1024 * j:1024 * (j + 1)] for j in range(2)]
        hsv = [hpart[:, 2048 + 512 * n:2048 + 512 * (n + 1)].bitcast(F16).rearrange("p (k n) -> p k n", k=KC)
               for n in range(4)]
        hshi, hslo = hsv[0:2], hsv[2:4]
        cga = htok
        cgb = hpart[:, :].rearrange("p (t n) -> p t n", t=TILES)
        xtok = arena[:, 0:TILES * D].rearrange("p (t n) -> p t n", t=TILES)
        ytok = arena[:, 0:TILES * D].rearrange("p (t n) -> p t n", t=TILES)

        xsq = scratch[:, 0:1280].rearrange("p (s n) -> p s n", s=2)
        tmp = scratch[:, 1280:2560].rearrange("p (s n) -> p s n", s=2)
        hf = scratch[:, 2560:3840].rearrange("p (s n) -> p s n", s=2)
        zpad = scratch[:, 0:1370].rearrange("p (c n) -> p c n", c=2)
        zacc = scratch[:, 1370:2680].rearrange("p (c n) -> p c n", c=2)
        zsg = scratch[:, 2680:3960].rearrange("p (c n) -> p c n", c=2)
        zc = scratch[:, 0:1280].rearrange("p (c n) -> p c n", c=2)
        zs = scratch[:, 1370:2650].rearrange("p (c n) -> p c n", c=2)
        csq = scratch[:, 0:1920]
        rope1 = scratch[:, 0:512]
        rope2 = scratch[:, 512:1024]
        roped = scratch[:, 1024:1536]
        qkc = scratch[:, 1536:2048]
        cn = scratch[:, 2048:2432]
        cThi = scratch[:, 2432:2624].bitcast(F16)
        cTlo = scratch[:, 2624:2816].bitcast(F16)
        cache = scratch[:, 2816:4000]
        ex = scratch[:, 0:2560].rearrange("p (s n) -> p s n", s=4)
        wmix = scratch[:, 2560:3840].rearrange("p (s n) -> p s n", s=2)
        osq = scratch[:, 3840:4096]
        sg = scratch[:, 0:1280].rearrange("p (s n) -> p s n", s=2)
        mt = scratch[:, 1280:2560].rearrange("p (s n) -> p s n", s=2)
        macc = scratch[:, 2560:3840].rearrange("p (s n) -> p s n", s=2)
        lgT = scratch[0:20, 3200:3840]
        ybuf = [scratch[:, 1024 * j:1024 * (j + 1)] for j in range(2)]
        msg = [scratch[:, 2048 + 256 * j:2304 + 256 * j] for j in range(2)]
        mact = [scratch[:, 2560 + 256 * j:2816 + 256 * j] for j in range(2)]
        atv = [scratch[:, 3072 + 128 * n:3200 + 128 * n].bitcast(F16).rearrange("p (c n) -> p c n", c=2)
               for n in range(4)]
        athi, atlo = atv[0:2], atv[2:4]
        rowhot = scratch[:, 0:1280].rearrange("p (n q) -> p n q", n=10)
        chhot = scratch[:, 1280:1540].rearrange("p (n c) -> p n c", n=10)
        tbl = scratch[:, 1540:1960]
        ohm = scratch[:, 1960:2120].rearrange("p (n e) -> p n e", n=10)
        cum = scratch[:, 2120:2200].rearrange("p (t e) -> p t e", t=TILES)
        acc = scratch[:, 2200:2296].rearrange("p (t e) -> p t e", t=TILES + 1)
        nch = scratch[:, 2296:2312]
        csum = [scratch[:, 2312 + 24 * n:2336 + 24 * n] for n in range(2)]
        first = scratch[:, 2360:2376]
        rsel = scratch[:, 2376:2446].rearrange("p (q n) -> p q n", q=7)
        cef = scratch[:, 2446:2472]
        wuf32 = wuhi[:, :].bitcast(F32)
        route = wuf32[:, 0:100].rearrange("p (t n) -> p t n", t=5)
        rw = wuf32[:, 100:300].rearrange("p (t n) -> p t n", t=5)
        rcol = wuf32[:, 300:340].rearrange("p (q t) -> p q t", t=5)
        ex5 = wuf32[:, 340:365].rearrange("p (t n) -> p t n", t=5)
        tie = sb("tie", [P, 4])
        small = wulo[:, :].bitcast(F32)
        rk = small[:, 0:266]
        iota, before = rk[:, 0:P], rk[:, P:2 * P]
        tokid, steps = rk[:, 2 * P:2 * P + 5], rk[:, 2 * P + 5:2 * P + 10]
        slotf = small[:, 266:276].bitcast(I32)
        idxf = small[:, 276:278].bitcast(I32)
        idxall = small[:, 278:278 + CHUNKS + 1]
        smalli = small[:, 278 + CHUNKS + 1:448].bitcast(I32)
        sloti, idxi = smalli[:, 0:10], smalli[:, 10:12]
        cexp = smalli[:, 12:12 + CHUNKS + 1]
        loopf = sb("loopf", [P, 3])
        loopi = sb("loopi", [P, 3], I32)
        zero1 = sb("zero1", [P, 1], I32)

        def pr(pair):
            return PS[:, pair, 384:1024]

        SEG = [(0, CTX), (CTX, TOK)]

        def bank(n, w=512):
            return PS[:, n // 2, 512 * (n % 2):512 * (n % 2) + w]

        consts_in = sig("consts_in")
        params_in = sig("params_in", 21 * 16)
        cache_in = sig("cache_in", 9 * 16)
        w_in = [sig(f"w_in{j}", V_ALL // 2 * 16) for j in range(2)]
        w_hi = sig("w_hi", V_ALL)
        w_lo = sig("w_lo", V_ALL, 1)
        w_lo_dve = sig("w_lo_dve", ADA_UNITS, 1)
        ada_used = sig("ada_used", ADA_UNITS, 2)
        set_ready = sig("set_ready")
        xt_done = sig("xt_done")
        x_even = sig("x_even")
        x_odd = sig("x_odd")
        cond_t = sig("cond_t")
        cond_f = sig("cond_f")
        cond_ready = sig("cond_ready")
        par_t = sig("par_t", 1)
        par_ready = sig("par_ready", 1)
        rp_ready = sig("rp_ready", 1)
        band_done = sig("band_done", 8)
        bias_ready = sig("bias_ready", 8)
        wu_hi = sig("wu_hi", 1)
        wu_ready = sig("wu_ready", 1)
        lam_sum = sig("lam_sum", 1)
        lam_exp = sig("lam_exp", 1)
        ada_ready = sig("ada_ready", 1)
        sq_ready = sig("sq_ready", 16)
        sq_used = sig("sq_used", 16)
        var_ready = sig("var_ready", 2)
        std_ready = sig("std_ready", 2)
        tmp_ready = sig("tmp_ready", 16)
        hf_ready = sig("hf_ready", 16)
        hhi_ready = sig("hhi_ready", 8)
        h_ready = sig("h_ready", 8)
        hf_used = sig("hf_used", 8)
        du_done = sig("du_done", 4)
        sig_ready = sig("sig_ready", 2)
        z_ready = sig("z_ready", 2)
        proj_done = sig("proj_done", 40)
        proj_ready = sig("proj_ready", 40)
        cv_ready = sig("cv_ready", 1)
        mu_done = sig("mu_done", 1)
        zc_ready = sig("zc_ready", 2)
        zsq_ready = sig("zsq_ready", 2)
        zv_done = sig("zv_done", 1)
        zvar_ready = sig("zvar_ready", 1)
        zstd_ready = sig("zstd_ready", 1)
        zn_ready = sig("zn_ready", 2)
        zs_ready = sig("zs_ready", 2)
        zhi_ready = sig("zhi_ready", 2)
        z_split = sig("z_split", 1)
        cs_ready = sig("cs_ready", 1)
        cv_var = sig("cv_var", 1)
        cv_std = sig("cv_std", 1)
        roped_ready = sig("roped_ready", 5)
        ab_t = sig("ab_t", 11)
        ab_hi = sig("ab_hi", 11)
        ab_ready = sig("ab_ready", 11)
        cn_ready = sig("cn_ready", 6)
        cn_t = sig("cn_t", 6)
        cT_hi = sig("cT_hi", 6)
        cT_ready = sig("cT_ready", 6)
        up_done = sig("up_done", 6)
        qkc_raw = sig("qkc_raw", 6)
        up_free = sig("up_free", 6)
        qkc_ready = sig("qkc_ready", 6)
        c_t = sig("c_t", 6)
        c_hi = sig("c_hi", 6)
        c_ready = sig("c_ready", 6)
        v_hi = sig("v_hi", 1)
        v_ready = sig("v_ready", 1)
        own_out = sig("own_out", 6 * 16)
        s_done = sig("s_done", TILES * MAPS)
        mx_ready = sig("mx_ready", TILES * MAPS)
        ex_ready = sig("ex_ready", TILES * MAPS)
        mix_ready = sig("mix_ready", TILES * 4)
        pt_done = sig("pt_done", TILES * HDS)
        pt_hi = sig("pt_hi", TILES * HDS)
        pt_ready = sig("pt_ready", TILES * HDS, 1)
        pv_done = sig("pv_done", TILES * HDS)
        rec_ready = sig("rec_ready", TILES * HDS)
        o_ready = sig("o_ready", TILES * HDS)
        ovar_ready = sig("ovar_ready", TILES)
        ostd_ready = sig("ostd_ready", TILES)
        on_ready = sig("on_ready", TILES)
        ot_done = sig("ot_done", TILES)
        ot_hi = sig("ot_hi", TILES)
        ot_ready = sig("ot_ready", TILES, 1)
        g_done = sig("g_done", 32)
        g_ready = sig("g_ready", 32, 2)
        b_done = sig("b_done", 32)
        m_used = sig("m_used", 32, 2)
        m_ready = sig("m_ready", 8)
        m_hi = sig("m_hi", 8)
        m_split = sig("m_split", 8)
        y_done = sig("y_done", 8)
        x1_ready = sig("x1_ready", 8, 4)
        lg_ready = sig("lg_ready", 1)
        lgt_done = sig("lgt_done", 1)
        rmax_ready = sig("rmax_ready", 1)
        rexp_ready = sig("rexp_ready", 1)
        htk_ready = sig("htk_ready", 8)
        rows_out = sig("rows_out", 16)
        route_in = sig("route_in", 16)
        hot_ready = sig("hot_ready", 1)
        cnt_done = sig("cnt_done", 1)
        place_ready = sig("place_ready", 1)
        list_done = sig("list_done", 1)
        route_ready = sig("route_ready", 1)
        filled = sig("filled", CHUNKS // TILES * 16)
        started = sig("started")
        idx_ready, ht_done, hs_hi, hs_ready = (sig(n) for n in ("idx_ready", "ht_done", "hs_hi", "hs_ready"))
        mgu_done, msilu_ready, mact_ready = (sig(n) for n in ("mgu_done", "msilu_ready", "mact_ready"))
        at_done, at_hi, at_ready = (sig(n) for n in ("at_done", "at_hi", "at_ready"))
        my_done, my_ready = sig("my_done"), sig("my_ready")
        mw_hi = sig("mw_hi")
        mw_lo = sig("mw_lo")
        mw_lo2 = sig("mw_lo2")
        m_in = [sig(f"m_in{n}") for n in range(6)]
        xg_in = [sig(f"xg_in{j}") for j in range(2)]
        y_out = [sig(f"y_out{j}") for j in range(2)]
        cg_in = [sig(f"cg_in{n}", 32) for n in range(TILES)]
        comb_ready = sig("comb_ready", TILES)
        yt_done = sig("yt_done", TILES)
        x2_ready = sig("x2_ready", TILES, 1)
        fin_ready = sig("fin_ready")
        fin_t = sig("fin_t")
        fin_out = sig("fin_out")
        fin_saved = sig("fin_saved")

        block = ctx.enter_context(nc.Block())

        def passes(pe, out, st_hi, st_lo, mv_hi, mv_lo, first, last):
            for n, (st, mv) in enumerate(((st_hi, mv_hi), (st_hi, mv_lo), (st_lo, mv_hi))):
                ins = pe.matmul(out, st, mv, start=first and n == 0, stop=last and n == 2)
            return ins

        def passes640(pe, pair, st_hi, st_lo, mv_hi, mv_lo, first, last):
            for n, (st, mv) in enumerate(((st_hi, mv_hi), (st_hi, mv_lo), (st_lo, mv_hi))):
                for a, b in SEG:
                    ins = pe.matmul(pr(pair)[:, a:b], st, mv[:, a:b], start=first and n == 0, stop=last and n == 2)
            return ins

        def loops(eng):
            b, m, before = (eng.value_load(loopi[0:1, n:n + 1], min_val=0, max_val=LAYERS * (PAIRS + 1) if n != 1 else PAIRS)
                            for n in range(3))
            return b, m, before, b + before + 1

        def keytile(tile):
            return tile if tile else 5

        @block.sync
        def _(sp):
            for dst, src in ((ident, t["k_ident"]),
                             (bandf, t["k_band"]), (crow[0:KC, :], t["c_ctx"].rearrange("(k p) -> k p", p=P)),
                             (crow[KC:2 * KC, :], t["c"].rearrange("b (k p) -> (b k) p", p=P)),
                             (crow[2 * KC:3 * KC, :], t["final_norm_g"].rearrange("(k p) -> k p", p=P)),
                             (xtok[:, 0, :], t["x_prompt"].rearrange("b s d -> (b s) d")),
                             (xtok[:, 1:TILES, :], t["x_sample"].rearrange("b (t p) d -> p (b t) d", p=P))):
                sp.dma_start(dst[:] if not isinstance(dst, bass.AP) else dst, src).then_inc(consts_in.sem, 16)
            with sp.Fori(0, LAYERS) as l:
                def free(v):
                    sp.wait_ge(*w_lo(l, v - 1))

                def wcols(w, off, n=256):
                    return w[ds(l, 1), :, off:off + n].rearrange("o (k p) n -> p (o k) n", p=P)

                sp.wait_ge(*x2_ready(l, 0))
                small = [
                    (prow[PC_ADA:PC_G1, :], t["b_ada"][ds(l, 1), :].rearrange("o (k p) -> (o k) p", p=P)),
                    (prow[PC_G1:PC_G2, :], t["norm1_g"][ds(l, 1), :].rearrange("o (k p) -> (o k) p", p=P)),
                    (prow[PC_G2:PC_BG, :], t["norm2_g"][ds(l, 1), :].rearrange("o (k p) -> (o k) p", p=P)),
                    (prow[PC_BG:PC_CB, :], t["b_gate"][ds(l, 1), :].rearrange("o (k p) -> (o k) p", p=P)),
                    (prow[PC_CB:PC_LG, :], t["d_conv_b"][ds(l, 1), :].rearrange("o (k p) -> (o k) p", p=P)),
                    (prow[PC_LG:PC_LB, :], t["d_ln_g"][ds(l, 1), :].rearrange("o (k p) -> (o k) p", p=P)),
                    (prow[PC_LB:PC_N, :], t["d_ln_b"][ds(l, 1), :].rearrange("o (k p) -> (o k) p", p=P)),
                    (cwrow[:, :], t["d_conv_w"][ds(l, 1)].rearrange("o k c -> (o k) c")),
                    (rprow[:, :], t["b_rpb"][ds(l, 1)].rearrange("o h r c -> (o h r) c")),
                    (rowg[:, 0:64], t["a_subln_g"][ds(l, 1), :].partition_broadcast(P)),
                    (rowg[:, 64:320], t["c_q_norm_g"][ds(l, 1), :].partition_broadcast(P)),
                    (rowg[:, 320:448], t["c_kv_norm_g"][ds(l, 1), :].partition_broadcast(P)),
                    (lamv[:, :, :], t["a_lambda"][ds(l, 1)].partition_broadcast(P)),
                    (lamc[:, :], t["k_lam"][ds(l, 1), :].partition_broadcast(P)),
                    (wuf[:, 0:512].rearrange("p (k n) -> p k n", k=2),
                     t["c_wuq"][ds(l, 1)].rearrange("o (k p) n -> p (o k) n", p=P)),
                    (wuf[:, 512:896], t["c_wukv"][ds(l, 1)].rearrange("o p n -> (o p) n")),
                    (rbias[0:4, :], t["moe_b_group"][ds(l, 1), :].rearrange("o n -> n o")),
                    (rbias[4:20, :], t["moe_b_expert"][ds(l, 1), :].rearrange("o n -> n o")),
                    (wr[:, :, 0:4], t["moe_w_group"][ds(l, 1)].rearrange("o (k p) n -> p (o k) n", p=P)),
                    (wr[:, :, 4:20], t["moe_w_expert"][ds(l, 1)].rearrange("o (k p) n -> p (o k) n", p=P)),
                ]
                small.append((maskb, t["k_mask"]))
                for dst, src in small:
                    sp.dma_start(dst, src).then_inc(params_in.sem, 16)
                with sp.Fori(0, ADA_UNITS // 2) as i:
                    for j in range(2):
                        sp.wait_ge(*w_lo(l, i * 2))
                        sp.wait_ge(*w_lo_dve(l, i * 2))
                        sp.dma_start(wf[j][:, :].rearrange("p (k n) -> p k n", k=KC),
                                     t["w_ada"][ds(l, 1), :, ds(i * 512 + j * 256, 256)]
                                     .rearrange("o (k p) n -> p (o k) n", p=P)).then_inc(w_in[j].sem, 16)
                for u in range(IN_UNITS):
                    off = C_DU + 256 * u if u < 2 else 256 * (u - 2)
                    n = 256 if u < IN_UNITS - 1 else 160
                    free(V_IN + u)
                    if u == 0:
                        sp.dma_start(tie[:, :], t["k_tie"]).then_inc(cache_in.sem, 16)
                        sp.wait_ge(*w_lo_dve(l, ADA_UNITS))
                        sp.dma_start(cosb[:, :, :], t["k_cos"]).then_inc(cache_in.sem, 16)
                    if u == 2:
                        sp.dma_start(sinb[:, :, :], t["k_sin"]).then_inc(cache_in.sem, 16)
                    sp.dma_start(wf[u % 2][:, 0:KC * n].rearrange("p (k n) -> p k n", k=KC),
                                 wcols(t["w_in"], off, n)).then_inc(w_in[u % 2].sem, 16)
                sp.wait_ge(*z_split(l, 1))
                for c, (name, w) in enumerate((("cache_a_k", 256), ("cache_b_k", 256), ("cache_a_v", 256),
                                               ("cache_b_v", 256), ("cache_c_kv", 128), ("cache_c_krope", 32))):
                    src = t[name][:, ds(l, 1)]
                    src = src.rearrange("b o s h d -> (b o s) (h d)" if c < 4 else "b o s d -> (b o s) d")
                    off = 256 * c if c < 4 else (1024 if c == 4 else 1152)
                    sp.dma_start(cache[:, off:off + w], src).then_inc(cache_in.sem, 16)
                sp.wait_ge(*cn_ready(l, 1))
                for name, a, n in (("new_a_k", 256, 256), ("new_a_v", C_AV, 256), ("new_b_k", 1024, 256),
                                   ("new_b_v", C_BV, 256), ("new_c_krope", C_CKR, 32)):
                    dst = t[name][:, ds(l, 1)]
                    dst = dst.rearrange("b o s h d -> (b o s) (h d)" if n == 256 else "b o s d -> (b o s) d")
                    sp.dma_start(dst, proj[:, 0, a:a + n]).then_inc(own_out.sem, 16)
                sp.dma_start(t["new_c_kv"][:, ds(l, 1)].rearrange("b o s d -> (b o s) d"), proj[:, 0, C_CKV:C_CKR]
                             ).then_inc(own_out.sem, 16)
                for n in range(CHUNKS // TILES):
                    sp.dma_start(t["y_rows"][TOK * n:TOK * (n + 1), :].rearrange("(t p) d -> p t d", p=P),
                                 xT[:, :, :].rearrange("p k n -> p (k n)").rearrange("p (t d) -> p t d", t=TILES)
                                 ).then_inc(filled.sem, 16)
                for b, name in enumerate(("a_wo", "b_wo", "c_wo", "d_wo")):
                    free(V_WO + b)
                    sp.dma_start(wf[b % 2][:, :].rearrange("p (k n) -> p k n", k=2),
                                 t[name][ds(l, 1)].rearrange("o (k p) n -> p (o k) n", p=P)
                                 ).then_inc(w_in[b % 2].sem, 16)
                sp.wait_ge(*up_done(l, 6))
                sp.dma_start(rk, t["k_route"]).then_inc(route_in.sem, 16)
                with sp.Fori(0, KC // 2) as d2:
                    for b in range(4):
                        sp.wait_ge(*w_lo(l, d2 * 4 + (V_GATE + b - 1)))
                        sp.dma_start(wf[b % 2][:, :].rearrange("p (k n) -> p k n", k=KC),
                                     t["w_gate"][ds(l, 1), :, ds(d2 * 256 + b * D, 256)]
                                     .rearrange("o (k p) n -> p (o k) n", p=P)).then_inc(w_in[b % 2].sem, 16)
                with sp.Fori(0, 2) as i:
                    for j in range(2):
                        sp.wait_ge(*w_lo(l, i * 2 + (V_OUT + j - 1)))
                        sp.dma_start(wf[j][:, :].rearrange("p (k n) -> p k n", k=KC),
                                     t["w_out"][ds(l, 1), :, ds(i * 512 + j * 256, 256)]
                                     .rearrange("o (k p) n -> p (o k) n", p=P)).then_inc(w_in[j].sem, 16)
                sp.wait_ge(*htk_ready(l, KC))
                sp.dma_start(t["h2_rows"].rearrange("(t p) d -> p t d", p=P), htok[:, :, :]).then_inc(rows_out.sem, 16)
                sp.wait_ge(started.sem, 1)
                sp.wait_ge(*route_ready(l, 1))
                b, m, ran, done = loops(sp)

                def load(c, ci, j):
                    e = sp.value_load(cexp[0:1, ds(c, 1)], min_val=0, max_val=EXPERTS - 1)
                    for q in range(3):
                        if q < 2:
                            src = t["moe_w1"][ds(l, 1), ds(e, 1), 512 * q:512 * (q + 1), :]
                            dst = mwf[3 * j + q].rearrange("p (k n) -> p k n", k=4)
                        else:
                            src = t["moe_w2"][ds(l, 1), ds(e, 1), :, :]
                            dst = mwf[3 * j + q].rearrange("p (k n) -> p k n", k=2)
                        sp.dma_start(dst, src.rearrange("o e (k p) n -> p (o e k) n", p=P)
                                     ).then_inc(m_in[3 * j + q].sem, 16)

                for j in range(2):
                    load(j, 0, j)
                with sp.Fori(0, m) as i:
                    for j in range(2):
                        sp.wait_ge(mw_lo2.sem, b * 2 + (i * 2 + (j + 1)))
                        sp.wait_ge(mw_lo.sem, b * 4 + (i * 4 + (2 * j + 2)))
                        load(i * 2 + (2 + j), 0, j)

            sp.wait_ge(*own_out(LAYERS - 1, 6 * 16))
            for n, (name, a, b) in enumerate((("y_prompt", 0, 1), ("y_sample", 1, TILES))):
                sp.wait_ge(*fin_out(0, KC))
                dst = t[name].rearrange("b (t p) d -> p (b t) d", p=P)
                sp.dma_start(dst, ytok[:, a:b, :]).then_inc(fin_saved.sem, 16)
            sp.wait_ge(*fin_saved(0, 32))

        @block.tensor
        def _(pe):
            pe.wait_ge(*consts_in(0, 7 * 16))
            for tile in range(TILES):
                if tile == 4:
                    pe.wait_ge(*x_even(0, 1))
                for k in range(KC):
                    ins = pe.transpose(PS[:, tile % 4, k * P:(k + 1) * P], xtok[:, tile, k * P:(k + 1) * P], ident[:, :])
                ins.then_inc(xt_done.sem, 1)
            pe.wait_ge(*x_odd(0, 1))
            pe.transpose(PS[:, 1, 0:3 * KC], crow[:, :], ident[0:3 * KC, 0:3 * KC]).then_inc(cond_t.sem, 1)
            pe.wait_ge(*set_ready(0, 2))
            pe.wait_ge(*cond_ready(0, 1))

            def sums(l, n):
                for k in range(KC):
                    pe.wait_ge(*sq_ready(l, KC * n + k + 1))
                    for a, b in SEG:
                        ins = pe.matmul(pr(2)[:, a:b], ones[:, :], xsq[:, k % 2, a:b], start=k == 0, stop=k == KC - 1)
                    ins.then_inc(sq_used.sem, 1)

            with pe.Fori(0, LAYERS) as l:
                pe.wait_ge(*x2_ready(l, 0))
                pe.wait_ge(*params_in(l, 21 * 16))
                pe.transpose(bank(6)[:, 0:PC_N], prow[:, :], ident[0:PC_N, 0:PC_N])
                for c in range(2):
                    pe.transpose(bank(6)[:, 104 + 32 * c:104 + 32 * c + CONV_K], cwrow[:, c * P:(c + 1) * P],
                                 ident[0:CONV_K, 0:CONV_K])
                pe.transpose(bank(6)[0:31, 168:228], rprow[:, :], ident[0:60, 0:60]).then_inc(par_t.sem, 1)
                pe.wait_ge(*rp_ready(l, 1))
                for g in range(8):
                    if g >= 4:
                        pe.wait_ge(*bias_ready(l, g - 3))
                    for kl in range(8):
                        kc = 8 * g + kl
                        for part in range(3):
                            ins = pe.matmul(bank(g % 4)[:, kl * 60:(kl + 1) * 60], band[:, 79 - kc:207 - kc],
                                            rp[:, part, :], start=part == 0, stop=part == 2)
                    ins.then_inc(band_done.sem, 1)
                with pe.Fori(0, ADA_UNITS // 2) as i:
                    for j in range(2):
                        pe.wait_ge(*w_lo(l, i * 2 + (j + 1)))
                        pe.wait_ge(*w_lo_dve(l, i * 2 + (j + 1)))
                        for c in range(2):
                            for k in range(KC):
                                w = slice(k * 256 + c * P, k * 256 + (c + 1) * P)
                                ins = passes(pe, PS[:, 3, ds(i * 8 + (512 + 4 * j + 2 * c), 2)], whi[j][:, w],
                                             wlo[j][:, w], schi[:, k, :], sclo[:, k, :], k == 0, k == KC - 1)
                        ins.then_inc(ada_used.sem, 1)
                sums(l, 0)
                for u in range(2):
                    pe.wait_ge(*w_lo(l, V_IN + u + 1))
                    for c in range(2):
                        for k in range(KC):
                            if u == 0 and c == 0:
                                pe.wait_ge(*h_ready(l, k + 1))
                            w = slice(k * 256 + c * P, k * 256 + (c + 1) * P)
                            ins = passes640(pe, 2 * u + c, whi[u][:, w], wlo[u][:, w], hhi[:, k, :], hlo[:, k, :],
                                            k == 0, k == KC - 1)
                        ins.then_inc(du_done.sem, 1)
                for u in range(2, IN_UNITS):
                    n = 256 if u < IN_UNITS - 1 else 160
                    pe.wait_ge(*w_lo(l, V_IN + u + 1))
                    for tile in range(TILES):
                        g = (u - 2) * TILES + tile
                        if g < 8:
                            pe.wait_ge(*z_ready(l, 2))
                        else:
                            pe.wait_ge(*proj_ready(l, g - 7))
                        for k in range(KC):
                            ins = passes(pe, bank(g % 8, n), hhi[:, k, tile * P:(tile + 1) * P],
                                         hlo[:, k, tile * P:(tile + 1) * P], whi[u % 2][:, k * n:(k + 1) * n],
                                         wlo[u % 2][:, k * n:(k + 1) * n], k == 0, k == KC - 1)
                        ins.then_inc(proj_done.sem, 1)
                pe.wait_ge(*proj_ready(l, 40))
                pe.wait_ge(*cv_ready(l, 1))
                for (a, b), z0 in zip(SEG, (0, CTX + PAD)):
                    for c in range(2):
                        ins = pe.matmul(pr(0)[:, a:b], ones[:, :], zacc[:, c, z0:z0 + b - a], start=c == 0, stop=c == 1)
                ins.then_inc(mu_done.sem, 1)
                for c in range(2):
                    pe.wait_ge(*zsq_ready(l, c + 1))
                    for a, b in SEG:
                        ins = pe.matmul(pr(1)[:, a:b], ones[:, :], zsg[:, c, a:b], start=c == 0, stop=c == 1)
                ins.then_inc(zv_done.sem, 1)
                pe.wait_ge(*wu_ready(l, 1))
                pe.wait_ge(*cache_in(l, 9 * 16))
                pe.wait_ge(*zvar_ready(l, 1))
                for n in range(TILES + 1):
                    own = n < TILES
                    src = cache[:, 0:512] if not own else (roped if n else proj[:, 0, 0:512])
                    if own and n:
                        pe.wait_ge(*roped_ready(l, n + 1))
                    if n >= 2:
                        pe.wait_ge(*ab_ready(l, 2 * n - 3))
                    for c in range(4):
                        ins = pe.transpose(bank(4 + 2 * (n % 2))[:, c * P:(c + 1) * P], src[:, c * P:(c + 1) * P], ident[:, :])
                    ins.then_inc(ab_t.sem, 1)
                    if own:
                        if n >= 2:
                            pe.wait_ge(*ab_ready(l, 2 * n - 2))
                        for c in range(4):
                            ins = pe.transpose(bank(5 + 2 * (n % 2))[:, c * P:(c + 1) * P],
                                               proj[:, n, C_BQ + c * P:C_BQ + (c + 1) * P], ident[:, :])
                        ins.then_inc(ab_t.sem, 1)
                    pe.wait_ge(*cn_ready(l, n + 1))
                    if n:
                        pe.wait_ge(*cT_ready(l, n))
                    for c in range(0 if own else 2, 3):
                        src = cn[:, c * P:(c + 1) * P] if own else cache[:, 1024:1152]
                        ins = pe.transpose(bank(0)[:, c * P:(c + 1) * P], src, ident[:, :])
                    ins.then_inc(cn_t.sem, 1)
                    pe.wait_ge(*cT_ready(l, n + 1))
                    if n:
                        pe.wait_ge(*up_free(l, n))
                    if own:
                        for c in range(2):
                            passes(pe, bank(1, 256), cThi[:, c * P:(c + 1) * P], cTlo[:, c * P:(c + 1) * P],
                                   wuhi[:, c * 256:(c + 1) * 256], wulo[:, c * 256:(c + 1) * 256], c == 0, c == 1)
                    passes(pe, bank(2, 384), cThi[:, 256:384], cTlo[:, 256:384], wuhi[:, 512:896], wulo[:, 512:896],
                           True, True).then_inc(up_done.sem, 1)
                    pe.wait_ge(*qkc_ready(l, n + 1))
                    if n:
                        pe.wait_ge(*c_ready(l, n))
                    for c in range(0 if own else 2, 4):
                        ins = pe.transpose(bank(3)[:, c * P:(c + 1) * P], qkc[:, c * P:(c + 1) * P], ident[:, :])
                    ins.then_inc(c_t.sem, 1)
                pe.wait_ge(*ab_ready(l, 11))
                pe.wait_ge(*c_ready(l, 6))
                pe.wait_ge(*v_ready(l, 1))

                def score(ti, tile, m):
                    if ti or m >= 2:
                        pe.wait_ge(*ex_ready(l, ti * MAPS + m - 1))
                    if m < 8:
                        lo, n, c = 32 * (m % 4), 32, m // 4
                    else:
                        lo, n, c = 64 * (m % 2), 64, (m - 8) // 2 + 2
                    q = (slice(lo, lo + n), c, slice(tile * P, (tile + 1) * P))
                    for a, b in SEG if tile else SEG[:1]:
                        k = (slice(lo, lo + n), c, slice(a, b) if tile else slice(TOK, TOK + P))
                        ins = passes(pe, pr(m % 2)[:, a:b], qThi[q], qTlo[q], kThi[k], kTlo[k], True, True)
                    ins.then_inc(s_done.sem, 1)

                def maps(hd):
                    return (2 * hd, 2 * hd + 1) if hd < 4 else (hd + 4,)

                def turn(ti, tile, hd):
                    if hd < 4:
                        pe.wait_ge(*mix_ready(l, ti * 4 + hd + 1))
                        src = wmix[:, hd % 2, :]
                    else:
                        pe.wait_ge(*ex_ready(l, ti * MAPS + hd + 5))
                        src = ex[:, hd % 4, :]
                    pe.wait_ge(*pt_ready(l, ti * HDS + hd))
                    if hd == 0:
                        pe.wait_ge(*ot_ready(l, ti))
                    for c in range(TILES if tile else 1):
                        ins = pe.transpose(pr(2)[:, c * P:(c + 1) * P], src[:, c * P:(c + 1) * P], ident[:, :])
                    ins.then_inc(pt_done.sem, 1)

                def values(ti, tile, hd):
                    pe.wait_ge(*pt_ready(l, ti * HDS + hd + 1))
                    if ti or hd >= 2:
                        pe.wait_ge(*o_ready(l, ti * HDS + hd - 1))
                    kts = range(TILES) if tile else (5,)
                    for c, kt in enumerate(kts):
                        ins = passes(pe, bank(6 + hd % 2, 64), pthi[:, hd % 2, c * P:(c + 1) * P],
                                     ptlo[:, hd % 2, c * P:(c + 1) * P], vhi[:, kt, hd * 64:(hd + 1) * 64],
                                     vlo[:, kt, hd * 64:(hd + 1) * 64], c == 0, c == len(kts) - 1)
                    ins.then_inc(pv_done.sem, 1)

                for ti, tile in enumerate((1, 2, 3, 4, 0)):
                    for step in range(HDS + 2):
                        if step < HDS:
                            for m in maps(step):
                                score(ti, tile, m)
                        if 1 <= step <= HDS:
                            turn(ti, tile, step - 1)
                        if step >= 2:
                            values(ti, tile, step - 2)
                    pe.wait_ge(*on_ready(l, ti + 1))
                    pe.wait_ge(*pt_ready(l, (ti + 1) * HDS))
                    for c in range(6):
                        ins = pe.transpose(PS[:, 2, c * P:(c + 1) * P], otok[:, c * P:(c + 1) * P], ident[:, :])
                    ins.then_inc(ot_done.sem, 1)
                with pe.Fori(0, KC // 2) as d2:
                    pe.wait_ge(*ot_ready(l, TILES))
                    pe.wait_ge(*z_split(l, 1))
                    for b in range(4):
                        pe.wait_ge(*w_lo(l, d2 * 4 + (V_GATE + b + 1)))
                        bhi = [oThi[:, 2 * b + k, :] if b < 3 else zhi[:, k, :] for k in range(2)]
                        blo = [oTlo[:, 2 * b + k, :] if b < 3 else zlo[:, k, :] for k in range(2)]
                        for c in range(2):
                            pe.wait_ge(*m_used(l, d2 * 8 + (2 * b + c - 1)))
                            for k in range(2):
                                w = ds(d2 * 256 + c * P, P)
                                ins = passes640(pe, 2 + c, wohi[:, b, k, w], wolo[:, b, k, w], bhi[k], blo[k],
                                                k == 0, k == 1)
                            ins.then_inc(b_done.sem, 1)
                            pe.wait_ge(*g_ready(l, d2 * 8 + (2 * b + c - 1)))
                            for k in range(KC):
                                w = slice(k * 256 + c * P, k * 256 + (c + 1) * P)
                                ins = passes640(pe, c, whi[b % 2][:, w], wlo[b % 2][:, w], hhi[:, k, :], hlo[:, k, :],
                                                k == 0, k == KC - 1)
                            ins.then_inc(g_done.sem, 1)
                with pe.Fori(0, 2) as i:
                    pe.wait_ge(*m_split(l, KC))
                    for j in range(2):
                        pe.wait_ge(*w_lo(l, i * 2 + (V_OUT + j + 1)))
                        for c in range(2):
                            pe.wait_ge(x1_ready.sem, l * 8 + i * 4 + (2 * j + c + 1))
                            for k in range(KC):
                                w = slice(k * 256 + c * P, k * 256 + (c + 1) * P)
                                ins = passes640(pe, 2 * j + c, whi[j][:, w], wlo[j][:, w], mhi[:, k, :], mlo[:, k, :],
                                                k == 0, k == KC - 1)
                            ins.then_inc(y_done.sem, 1)
                sums(l, 1)
                for k in range(KC):
                    pe.wait_ge(*hf_ready(l, KC + k + 1))
                    for a, b in SEG:
                        ins = pe.matmul(pr(3)[0:20, a:b], wr[:, k, :], hf[:, k % 2, a:b], start=k == 0, stop=k == KC - 1)
                    if k >= 2:
                        pe.wait_ge(*htk_ready(l, k - 1))
                    for tile in range(TILES):
                        ins = pe.transpose(pr(k % 2)[:, tile * P:(tile + 1) * P], hf[:, k % 2, tile * P:(tile + 1) * P],
                                           ident[:, :])
                    ins.then_inc(hf_used.sem, 1)
                pe.wait_ge(*lg_ready(l, 1))
                for tile in range(TILES):
                    ins = pe.matmul(bank(4)[:, tile * 20:(tile + 1) * 20], lgT[:, tile * P:(tile + 1) * P],
                                    ident[0:20, 0:20], start=True, stop=True)
                ins.then_inc(lgt_done.sem, 1)
                pe.wait_ge(*hot_ready(l, 1))
                pe.wait_ge(*route_in(l, 16))
                pe.matmul(bank(4)[:, 128:208], before, cum.rearrange("p t e -> p (t e)"), start=True, stop=True)
                pe.matmul(bank(4)[:, 256:336], ones[:, :], cum.rearrange("p t e -> p (t e)"), start=True, stop=True
                          ).then_inc(cnt_done.sem, 1)
                pe.wait_ge(*place_ready(l, 1))
                for n in range(10):
                    ins = pe.matmul(bank(5)[:, 0:CHUNKS + 1], rowhot[:, n, :], chhot[:, n, :], start=n == 0, stop=n == 9)
                ins.then_inc(list_done.sem, 1)
                pe.wait_ge(started.sem, 1)
                pe.wait_ge(*route_ready(l, 1))
                b, m, ran, done = loops(pe)

                def turn_rows(c, j, ci, first=False):
                    pe.wait_ge(xg_in[j].sem, b * 16 + (ci * 16 + 16))
                    if not first:
                        pe.wait_ge(hs_ready.sem, b * 2 + c)
                    for k in range(KC):
                        ins = pe.transpose(PS[:, 0, k * P:(k + 1) * P], xg[j][:, k * P:(k + 1) * P], ident[:, :])
                    ins.then_inc(ht_done.sem, 1)

                def gate_up(c, j, first=False):
                    pe.wait_ge(hs_ready.sem, b * 2 + (c + 1))
                    if not first:
                        pe.wait_ge(mact_ready.sem, done + (c - 1))
                    for k in range(KC):
                        if k % 4 == 0:
                            pe.wait_ge(mw_lo.sem, b * 4 + (c * 2 + (k // 4 + 1)))
                        w = slice((k % 4) * 512, (k % 4) * 512 + 512)
                        ins = passes(pe, bank(2 + j), hshi[j][:, k, :], hslo[j][:, k, :], mwhi[3 * j + k // 4][:, w],
                                     mwlo[3 * j + k // 4][:, w], k == 0, k == KC - 1)
                    ins.then_inc(mgu_done.sem, 1)

                def turn_act(c, j, first=False):
                    pe.wait_ge(mact_ready.sem, done + (c + 1))
                    if not first:
                        pe.wait_ge(at_ready.sem, done + (c - 1))
                    for k in range(2):
                        ins = pe.transpose(bank(4 + j)[:, k * P:(k + 1) * P], mact[j][:, k * P:(k + 1) * P], ident[:, :])
                    ins.then_inc(at_done.sem, 1)

                def down(c, j, first=False):
                    pe.wait_ge(at_ready.sem, done + (c + 1))
                    pe.wait_ge(mw_lo2.sem, b * 2 + (c + 1))
                    if not first:
                        pe.wait_ge(my_ready.sem, done + c)
                    for half in range(2):
                        for k in range(2):
                            w = slice(k * D + 512 * half, k * D + 512 * half + 512)
                            ins = passes(pe, bank(6 + half), athi[j][:, k, :], atlo[j][:, k, :], mwhi[3 * j + 2][:, w],
                                         mwlo[3 * j + 2][:, w], k == 0, k == 1)
                    ins.then_inc(my_done.sem, 1)

                turn_rows(0, 0, 0, True)
                gate_up(0, 0, True)
                turn_rows(1, 1, 0)
                turn_act(0, 0, True)
                with pe.Fori(0, m) as i:
                    for n in range(2):
                        c, j = i * 2 + (1 + n), 1 - n
                        gate_up(c, j)
                        turn_rows(i * 2 + (2 + n), n, i + 1)
                        down(i * 2 + n, n)
                        turn_act(c, j)
                down(m * 2, 0)
                for tile in range(TILES):
                    pe.wait_ge(*comb_ready(l, tile + 1))
                    if tile >= 2:
                        pe.wait_ge(*x2_ready(l, tile - 1))
                    for k in range(KC):
                        ins = pe.transpose(PS[:, tile % 2, k * P:(k + 1) * P], ybuf[tile % 2][:, k * P:(k + 1) * P],
                                           ident[:, :])
                    ins.then_inc(yt_done.sem, 1)
            pe.wait_ge(*x2_ready(LAYERS - 1, TILES))
            sums(LAYERS, 0)
            for k in range(KC):
                pe.wait_ge(*fin_ready(0, k + 1))
                if k >= 2:
                    pe.wait_ge(*fin_out(0, k - 1))
                for tile in range(TILES):
                    ins = pe.transpose(pr(k % 2)[:, tile * P:(tile + 1) * P], tmp[:, k % 2, tile * P:(tile + 1) * P],
                                       ident[:, :])
                ins.then_inc(fin_t.sem, 1)

        @block.scalar
        def _(act):
            for tile in (0, 2, 4):
                act.wait_ge(*xt_done(0, tile + 1))
                ins = act.copy(xT[:, :, tile * P:(tile + 1) * P], PS[:, tile % 4, :].rearrange("p (k n) -> p k n", k=KC))
                ins.then_inc(x_even.sem, 1)
            act.wait_ge(*cond_t(0, 1))
            act.activation(scf[:, :, :], PS[:, 1, 0:2 * KC].rearrange("p (s k) -> p k s", s=2), ACT.Silu
                           ).then_inc(cond_f.sem, 1)
            act.wait_ge(*cond_f(0, 1))
            act.copy(schi[:, :, :], scf[:, :, :]).then_inc(cond_f.sem, 1)
            act.wait_ge(*x_odd(0, 2))

            def squares(l, n):
                for k in range(KC):
                    if k >= 2:
                        act.wait_ge(*sq_used(l, KC * n + k - 1))
                    act.activation(xsq[:, k % 2, :], xT[:, k, :], ACT.Square).then_inc(sq_ready.sem, 1)
                act.wait_ge(*var_ready(l, n + 1))
                act.activation(rsb[:, :], rsb[:, :], ACT.Sqrt).then_inc(std_ready.sem, 1)

            def modulate(l, n):
                for k in range(KC):
                    act.wait_ge(*tmp_ready(l, KC * n + k + 1))
                    if k >= 2:
                        act.wait_ge(*(hf_used if n else h_ready)(l, k - 1))
                    for s, (a, b) in enumerate(SEG):
                        ins = act.activation(hf[:, k % 2, a:b], tmp[:, k % 2, a:b], ACT.Identity,
                                             bias=ada[:, 24 * n + k, s:s + 1])
                    ins.then_inc(hf_ready.sem, 1)

            with act.Fori(0, LAYERS) as l:
                def high(v, j, dst=None, n=2048):
                    act.wait_ge(w_in[j].sem, l * (V_ALL // 2 * 16) + (v // 2 + 1) * 16)
                    act.copy(whi[j][:, 0:n] if dst is None else dst, wf[j][:, 0:n]).then_inc(w_hi.sem, 1)

                def high_at(i, v, j, step=2):
                    act.wait_ge(w_in[j].sem, l * (V_ALL // 2 * 16) + i * (8 * step) + (v // 2 + 1) * 16)
                    act.copy(whi[j][:, :], wf[j][:, :]).then_inc(w_hi.sem, 1)

                act.wait_ge(*params_in(l, 21 * 16))
                act.copy(wuhi[:, :], wuf[:, :]).then_inc(wu_hi.sem, 1)
                act.wait_ge(*lam_sum(l, 1))
                act.activation(lamt[:, 66:68], lamt[:, 64:66], ACT.Exp).then_inc(lam_exp.sem, 1)
                with act.Fori(0, ADA_UNITS // 2) as i:
                    for j in range(2):
                        act.wait_ge(*ada_used(l, i * 2 + (j - 1)))
                        high_at(i, j, j)
                act.wait_ge(*ada_ready(l, 1))
                for u in range(2):
                    high(V_IN + u, u)
                squares(l, 0)
                modulate(l, 0)
                act.wait_ge(*du_done(l, 2))
                high(V_IN + 2, 0)
                for c in range(2):
                    act.wait_ge(*du_done(l, 3 + c))
                    act.activation(zsg[:, c, :], pr(2 + c), ACT.Sigmoid).then_inc(sig_ready.sem, 1)
                high(V_IN + 3, 1)
                for u in range(2, IN_UNITS):
                    n = 256 if u < IN_UNITS - 1 else 160
                    for tile in range(TILES):
                        g = (u - 2) * TILES + tile
                        act.wait_ge(*proj_done(l, g + 1))
                        act.copy(proj[:, tile, 256 * (u - 2):256 * (u - 2) + n], bank(g % 8, n)
                                 ).then_inc(proj_ready.sem, 1)
                    if u + 2 < IN_UNITS:
                        high(V_IN + u + 2, u % 2, n=2048 if u + 2 < IN_UNITS - 1 else KC * 160)
                for c in range(2):
                    act.wait_ge(*zc_ready(l, c + 1))
                    act.activation(zsg[:, c, :], zc[:, c, :], ACT.Square).then_inc(zsq_ready.sem, 1)
                act.wait_ge(*zvar_ready(l, 1))
                act.activation(rsb[:, :], rsb[:, :], ACT.Sqrt).then_inc(zstd_ready.sem, 1)
                for c in range(2):
                    act.wait_ge(*zn_ready(l, c + 1))
                    act.activation(zs[:, c, :], zc[:, c, :], ACT.Silu, bias=pcol[:, PC_LB + c:PC_LB + c + 1],
                                   scale=pcol[:, PC_LG + c:PC_LG + c + 1]).then_inc(zs_ready.sem, 1)
                act.wait_ge(*cache_in(l, 9 * 16))
                act.wait_ge(*proj_ready(l, 40))
                for br, col in enumerate((C_AV, C_BV)):
                    act.copy(vhi[:, 1:5, 256 * br:256 * br + 256], proj[:, 1:5, col:col + 256])
                    act.copy(vhi[:, 5, 256 * br:256 * br + 256], proj[:, 0, col:col + 256])
                act.copy(vhi[:, 0, 0:512], cache[:, 512:1024]).then_inc(v_hi.sem, 1)
                act.wait_ge(*cv_var(l, 1))
                act.activation(cstat[:, 1, :], cstat[:, 0, :], ACT.Sqrt).then_inc(cv_std.sem, 1)
                SCALE = (32 ** -0.5, 64 ** -0.5, 64 ** -0.5)

                def cols(n):
                    kt = 0 if n == TILES else keytile(n)
                    return slice(kt * P, (kt + 1) * P)

                def turned(n, br, src, ready):
                    tk = slice(n * P, (n + 1) * P)
                    act.mul(qThi[:, 2 * br:2 * br + 2, tk], src[:, 0:256].rearrange("p (c n) -> p c n", c=2), SCALE[br])
                    act.copy(kThi[:, 2 * br:2 * br + 2, cols(n)], src[:, 256:512].rearrange("p (c n) -> p c n", c=2)
                             ).then_inc(ready.sem, 1)

                for n in range(TILES + 1):
                    own = n < TILES
                    if own:
                        for br in range(2):
                            act.wait_ge(*ab_t(l, 2 * n + br + 1))
                            turned(n, br, bank(4 + br + 2 * (n % 2)), ab_hi)
                    else:
                        act.wait_ge(*ab_t(l, 11))
                        act.copy(kThi[:, 0:4, cols(n)], bank(6).rearrange("p (c n) -> p c n", c=4)
                                 ).then_inc(ab_hi.sem, 1)
                    act.wait_ge(*cn_t(l, n + 1))
                    if n:
                        act.wait_ge(*up_done(l, n))
                    lo = 0 if own else 256
                    act.copy(cThi[:, lo:384], bank(0)[:, lo:384]).then_inc(cT_hi.sem, 1)
                    act.wait_ge(*up_done(l, n + 1))
                    if n:
                        act.wait_ge(*c_t(l, n))
                    kt = keytile(n) if own else 0
                    kv = bank(2, 384).rearrange("p (h n) -> p h n", h=4)
                    if own:
                        act.copy(qkc[:, 0:256], bank(1, 256))
                    krope = proj[:, n, C_CKR:C_CKR + 32] if own else cache[:, 1152:1184]
                    qk = qkc[:, 256:512].rearrange("p (h n) -> p h n", h=4)
                    act.copy(qk[:, :, 0:32], kv[:, :, 0:32])
                    act.copy(qk[:, :, 32:64], krope.rearrange("p (o n) -> p o n", o=1).to_broadcast([P, 4, 32]))
                    act.copy(vhi[:, kt, 512:768].rearrange("p (h n) -> p h n", h=4), kv[:, :, 32:96]
                             ).then_inc(qkc_raw.sem, 1)
                    act.wait_ge(*c_t(l, n + 1))
                    if own:
                        turned(n, 2, bank(3), c_hi)
                    else:
                        act.copy(kThi[:, 4:6, cols(n)], bank(3)[:, 256:512].rearrange("p (c n) -> p c n", c=2)
                                 ).then_inc(c_hi.sem, 1)
                for ti, tile in enumerate((1, 2, 3, 4, 0)):
                    nk = TOK if tile else P
                    for step in range(HDS + 2):
                        if step < HDS:
                            for m in ((2 * step, 2 * step + 1) if step < 4 else (step + 4,)):
                                old = (m - 4) % MAPS
                                oti = ti - (m < 4)
                                if oti >= 0:
                                    if old < 8:
                                        act.wait_ge(*mix_ready(l, oti * 4 + old // 2 + 1))
                                    else:
                                        act.wait_ge(*pt_done(l, oti * HDS + old - 4 + 1))
                                act.wait_ge(*mx_ready(l, ti * MAPS + m + 1))
                                act.activation(ex[:, m % 4, 0:nk], pr(m % 2)[:, 0:nk], ACT.Exp,
                                               bias=stat[:, 0, m:m + 1], accum_out=stat[:, 1, m:m + 1]
                                               ).then_inc(ex_ready.sem, 1)
                        if 1 <= step <= HDS:
                            hd = step - 1
                            act.wait_ge(*pt_done(l, ti * HDS + hd + 1))
                            if ti or hd >= 2:
                                act.wait_ge(*pv_done(l, ti * HDS + hd - 1))
                            act.copy(pthi[:, hd % 2, 0:nk], pr(2)[:, 0:nk]).then_inc(pt_hi.sem, 1)
                        if step >= 2:
                            hd = step - 2
                            m = 2 * hd if hd < 4 else hd + 4
                            act.wait_ge(*pv_done(l, ti * HDS + hd + 1))
                            act.wait_ge(*rec_ready(l, ti * HDS + hd + 1))
                            if ti and hd == 0:
                                act.wait_ge(*ot_done(l, ti))
                            act.mul(otok[:, hd * 64:(hd + 1) * 64], bank(6 + hd % 2, 64), stat[:, 2, m:m + 1]
                                    ).then_inc(o_ready.sem, 1)
                    act.wait_ge(*ovar_ready(l, ti + 1))
                    act.activation(ostat[:, 1, :], ostat[:, 0, :], ACT.Sqrt).then_inc(ostd_ready.sem, 1)
                    act.wait_ge(*ot_done(l, ti + 1))
                    if ti == 0:
                        act.wait_ge(*own_out(l, 6 * 16))
                    act.copy(oThi[:, :, tile * P:(tile + 1) * P], PS[:, 2, 0:768].rearrange("p (c n) -> p c n", c=6)
                             ).then_inc(ot_hi.sem, 1)
                for b in range(WO_UNITS):
                    high(V_WO + b, b % 2, dst=wohi[:, b, :, :].rearrange("p k n -> p (k n)"))
                for j in range(2):
                    high(V_GATE + j, j)
                with act.Fori(0, KC // 2) as d2:
                    for b in range(4):
                        for c in range(2):
                            act.wait_ge(*g_done(l, d2 * 8 + (2 * b + c + 1)))
                            act.wait_ge(*m_used(l, d2 * 8 + (2 * b + c - 1)))
                            act.activation(sg[:, c, :], pr(c), ACT.Sigmoid,
                                           bias=pcol[:, ds(d2 * 2 + (PC_BG + 8 * b + c), 1)]).then_inc(g_ready.sem, 1)
                        high_at(d2, V_GATE + 2 + b, b % 2, 4)
                    for c in range(2):
                        act.wait_ge(*m_ready(l, d2 * 2 + (c + 1)))
                        act.copy(mhi[:, ds(d2 * 2 + c, 1), :].rearrange("p o n -> p (o n)"), macc[:, c, :]
                                 ).then_inc(m_hi.sem, 1)
                for j in range(2):
                    act.wait_ge(*y_done(l, 2 * j + 2))
                    high(V_OUT + 2 + j, j)
                act.wait_ge(*x1_ready(l, 8))
                squares(l, 1)
                modulate(l, 1)
                act.wait_ge(*rmax_ready(l, 1))
                act.activation(ex5[:, :, :], ex5[:, :, :], ACT.Exp).then_inc(rexp_ready.sem, 1)
                act.wait_ge(started.sem, 1)
                act.wait_ge(*route_ready(l, 1))
                b, m, ran, done = loops(act)

                def part_high(c, j, ci, q, first=False):
                    act.wait_ge(m_in[3 * j + q].sem, b * 16 + (ci * 16 + 16))
                    if not first:
                        act.wait_ge((my_done if q == 2 else mgu_done).sem, done + (c - 1))
                    act.copy(mwhi[3 * j + q], mwf[3 * j + q]).then_inc(mw_hi.sem, 1)

                def rows_high(c, j, first=False):
                    act.wait_ge(ht_done.sem, b * 2 + (c + 1))
                    if not first:
                        act.wait_ge(mgu_done.sem, done + (c - 1))
                    act.copy(hshi[j], PS[:, 0, :].rearrange("p (k n) -> p k n", k=KC)).then_inc(hs_hi.sem, 1)

                def silu(c, j, first=False):
                    act.wait_ge(mgu_done.sem, done + (c + 1))
                    if not first:
                        act.wait_ge(mact_ready.sem, done + (c - 1))
                    act.activation(msg[j], bank(2 + j, 256), ACT.Silu).then_inc(msilu_ready.sem, 1)

                def act_high(c, j, first=False):
                    act.wait_ge(at_done.sem, done + (c + 1))
                    if not first:
                        act.wait_ge(my_done.sem, done + (c - 1))
                    act.mul(athi[j], bank(4 + j, 256).rearrange("p (c n) -> p c n", c=2), A_SCALE
                            ).then_inc(at_hi.sem, 1)

                def rows_back(c, j, par, row):
                    act.wait_ge(my_done.sem, done + (c + 1))
                    if par is not None:
                        act.wait_ge(y_out[j].sem, par)
                    act.copy(ybuf[j], PS[:, 3, :]).then_inc(my_ready.sem, 1)
                    act.wait_ge(my_ready.sem, done + (c + 1))
                    act.dma_start(t["y_rows"][ds(row, P), :], ybuf[j]).then_inc(y_out[j].sem, 16)

                act.wait_ge(*filled(l, CHUNKS // TILES * 16))
                for q in range(3):
                    part_high(0, 0, 0, q, True)
                rows_high(0, 0, True)
                for q in range(2):
                    part_high(1, 1, 0, q, True)
                silu(0, 0, True)
                rows_high(1, 1, True)
                part_high(1, 1, 0, 2, True)
                act_high(0, 0, True)
                with act.Fori(0, m) as i:
                    for n in range(2):
                        c, j = i * 2 + (1 + n), 1 - n
                        for q in range(2):
                            part_high(i * 2 + (2 + n), n, i + 1, q)
                        silu(c, j)
                        rows_high(i * 2 + (2 + n), n)
                        rows_back(i * 2 + n, n, (ran if n else b) * 16 + (i * 16 + 16), i * (2 * P) + n * P)
                        part_high(i * 2 + (2 + n), n, i + 1, 2)
                        act_high(c, j)
                rows_back(m * 2, 0, b * 16 + (m * 16 + 16), m * (2 * P))
            act.wait_ge(*x2_ready(LAYERS - 1, TILES))
            squares(LAYERS, 0)
            for k in range(KC):
                act.wait_ge(*fin_t(0, k + 1))
                act.copy(ytok[:, :, k * P:(k + 1) * P], pr(k % 2).rearrange("p (t n) -> p t n", t=TILES)
                         ).then_inc(fin_out.sem, 1)

        @block.gpsimd
        def _(pool):
            with pool.Fori(0, LAYERS) as l:
                def low(count, j, dst=None, n=2048):
                    pool.wait_ge(w_hi.sem, count)
                    hi = whi[j][:, 0:n] if dst is None else dst[0]
                    lo = wlo[j][:, 0:n] if dst is None else dst[1]
                    pool.tensor_tensor(lo, wf[j][:, 0:n], hi, ALU.subtract).then_inc(w_lo.sem, 1)

                with pool.Fori(0, ADA_UNITS // 2) as i:
                    for j in range(2):
                        low(l * V_ALL + i * 2 + (j + 1), j, n=768)
                for u in range(IN_UNITS):
                    low(l * V_ALL + (V_IN + u + 1), u % 2, n=2048 if u < IN_UNITS - 1 else KC * 160)
                for b in range(WO_UNITS):
                    flat = [w[:, b, :, :].rearrange("p k n -> p (k n)") for w in (wohi, wolo)]
                    low(l * V_ALL + (V_WO + b + 1), b % 2, flat)
                with pool.Fori(0, (V_ALL - V_GATE) // 2) as i:
                    for j in range(2):
                        low(l * V_ALL + i * 2 + (V_GATE + j + 1), j)
                pool.wait_ge(*route_ready(l, 1))
                pool.tensor_tensor(zero1[:, :], zero1[:, :], zero1[:, :], ALU.add)
                pool.drain()
                b, m, ran, done = loops(pool)

                def gather(c, j):
                    pool.wait_ge(idx_ready.sem, b * 2 + (c + 1))
                    pool.tensor_tensor(idxi[:, j:j + 1], idxf[:, j:j + 1], zero1[:, :], ALU.add)
                    pool.drain()
                    pool.indirect_dma_start(out=xg[j], out_offset=None, in_=t["h2_rows"],
                                            in_offset=bass.IndirectOffsetOnAxis(ap=idxi[:, j:j + 1], axis=0)
                                            ).then_inc(xg_in[j].sem, 16)

                def part_low(c, j):
                    pool.wait_ge(mw_hi.sem, b * 6 + (c * 3 + 3))
                    pool.tensor_tensor(mwlo[3 * j + 2], mwf[3 * j + 2], mwhi[3 * j + 2], ALU.subtract
                                       ).then_inc(mw_lo2.sem, 1)

                pool.wait_ge(*rows_out(l, 16))
                for c in range(2):
                    gather(c, c)
                    part_low(c, c)
                with pool.Fori(0, m) as i:
                    for n in range(2):
                        gather(i * 2 + (2 + n), n)
                        part_low(i * 2 + (2 + n), n)
                pool.wait_ge(hs_ready.sem, b * 2 + m * 2 + 2)
                pool.wait_ge(y_out[0].sem, b * 16 + (m * 16 + 32))
                pool.wait_ge(y_out[1].sem, ran * 16 + (m * 16 + 16))
                pool.tensor_tensor(sloti[:, :], slotf[:, :], zero1[:, :].to_broadcast([P, 10]), ALU.add)
                pool.drain()
                for tile in range(TILES):
                    for ch, dst in enumerate((cga, cgb)):
                        n = ch * TILES + tile
                        pool.indirect_dma_start(out=dst[:, tile, :], out_offset=None, in_=t["y_rows"],
                                                in_offset=bass.IndirectOffsetOnAxis(ap=sloti[:, n:n + 1], axis=0)
                                                ).then_inc(cg_in[tile].sem, 16)

        @block.vector
        def _(dve):
            dve.memset(ones[:, :], 1.0).then_inc(set_ready.sem, 1)
            dve.wait_ge(*consts_in(0, 7 * 16))
            dve.tensor_copy(band[:, :], bandf[:, :]).then_inc(set_ready.sem, 1)
            for s in (w_lo, w_lo_dve, pt_ready, ot_ready, mgu_done, msilu_ready, mact_ready, at_done, at_hi, at_ready,
                      my_done, my_ready):
                dve.nop().then_inc(s.sem, 1)
            for s in y_out:
                dve.nop().then_inc(s.sem, 16)
            dve.nop().then_inc(ada_used.sem, 2)
            dve.nop().then_inc(g_ready.sem, 2)
            dve.nop().then_inc(m_used.sem, 2)
            dve.nop().then_inc(x1_ready.sem, 4)
            dve.nop().then_inc(x2_ready.sem, 1)
            dve.nop().then_inc(started.sem, 1)
            dve.memset(zero1[:, :], 0).then_inc(set_ready.sem, 1)
            dve.memset(loopf[:, 0:1], 0.0)
            dve.memset(loopf[:, 1:2], -1.0)
            dve.memset(loopf[:, 2:3], 1.0)
            for tile in (1, 3):
                dve.wait_ge(*xt_done(0, tile + 1))
                dve.tensor_copy(xT[:, :, tile * P:(tile + 1) * P], PS[:, tile, :].rearrange("p (k n) -> p k n", k=KC)
                                ).then_inc(x_odd.sem, 1)
            dve.wait_ge(*cond_f(0, 2))
            dve.tensor_tensor(sclo[:, :, :], scf[:, :, :], schi[:, :, :], ALU.subtract)
            dve.tensor_copy(gfin[:, :], PS[:, 1, 2 * KC:3 * KC]).then_inc(cond_ready.sem, 1)

            def root(l, n):
                dve.wait_ge(*sq_used(l, KC * (n + 1)))
                dve.tensor_scalar(rsb[:, :], pr(2), 1.0 / D, EPS, ALU.mult, ALU.add).then_inc(var_ready.sem, 1)
                dve.wait_ge(*std_ready(l, n + 1))
                dve.reciprocal(rsb[:, :], rsb[:, :])
                dve.drain()

            def norm(l, n):
                root(l, n)

                def scaled(k):
                    if k >= 2:
                        dve.wait_ge(*hf_ready(l, KC * n + k - 1))
                    for s, (a, b) in enumerate(SEG):
                        ins = dve.scalar_tensor_tensor(out=tmp[:, k % 2, a:b], in0=xT[:, k, a:b],
                                                       scalar=gs[:, n, k, s:s + 1], in1=rsb[:, a:b],
                                                       op0=ALU.mult, op1=ALU.mult)
                    ins.then_inc(tmp_ready.sem, 1)

                scaled(0)
                for k in range(KC):
                    if k + 1 < KC:
                        scaled(k + 1)
                    if n:
                        dve.wait_ge(*hf_used(l, k + 1))
                        dve.tensor_copy(htok[:, :, k * P:(k + 1) * P], pr(k % 2).rearrange("p (t n) -> p t n", t=TILES)
                                        ).then_inc(htk_ready.sem, 1)
                        continue
                    dve.wait_ge(*hf_ready(l, KC * n + k + 1))
                    dve.tensor_copy(hhi[:, k, :], hf[:, k % 2, :]).then_inc(hhi_ready.sem, 1)
                    dve.wait_ge(*hhi_ready(l, k + 1))
                    dve.tensor_tensor(hlo[:, k, :], hf[:, k % 2, :], hhi[:, k, :], ALU.subtract
                                      ).then_inc(h_ready.sem, 1)

            def bc(ap, shape):
                return ap.to_broadcast(shape)

            with dve.Fori(0, LAYERS) as l:
                dve.wait_ge(*par_t(l, 1))
                dve.tensor_copy(pcol[:, :], bank(6)[:, 0:PC_N])
                dve.tensor_copy(cw[:, :, :], bank(6)[:, 104:168].rearrange("p (c n) -> p c n", c=2)[:, :, 0:CONV_K])
                dve.tensor_copy(rpf[:, :], bank(6)[0:31, 168:228]).then_inc(par_ready.sem, 1)
                dve.drain()
                dve.tensor_copy(rp[:, 0, :], rpf[:, :])
                dve.drain()
                dve.tensor_tensor(rpd[:, :], rpf[:, :], rp[:, 0, :], ALU.subtract)
                dve.drain()
                dve.tensor_copy(rp[:, 1, :], rpd[:, :])
                dve.drain()
                dve.tensor_tensor(rpf[:, :], rpd[:, :], rp[:, 1, :], ALU.subtract)
                dve.drain()
                dve.tensor_copy(rp[:, 2, :], rpf[:, :]).then_inc(rp_ready.sem, 1)
                dve.wait_ge(*params_in(l, 21 * 16))
                dve.tensor_tensor(lamt[:, 0:64].rearrange("p (a n) -> p a n", a=2), lamv[:, 0:4:2, :], lamv[:, 1:4:2, :],
                                  ALU.mult)
                dve.drain()
                dve.tensor_reduce(lamt[:, 64:66], lamt[:, 0:64].rearrange("p (a n) -> p a n", a=2), AX_X, ALU.add
                                  ).then_inc(lam_sum.sem, 1)
                dve.tensor_scalar(rowg[:, 0:64], rowg[:, 0:64], lamc[:, 1:2], None, ALU.mult)
                dve.wait_ge(*wu_hi(l, 1))
                dve.tensor_tensor(wulo[:, :], wuf[:, :], wuhi[:, :], ALU.subtract).then_inc(wu_ready.sem, 1)
                dve.wait_ge(*lam_exp(l, 1))
                dve.tensor_tensor(lamt[:, 68:69], lamt[:, 67:68], lamt[:, 66:67], ALU.subtract)
                dve.drain()
                dve.tensor_tensor(lamt[:, 69:70], lamt[:, 68:69], lamc[:, 0:1], ALU.subtract)
                nlam = lamt[:, 69:70]
                for g in range(8):
                    dve.wait_ge(*band_done(l, g + 1))
                    for half in range(2):
                        ps = slice(64 * half, 64 * half + 64)
                        src = bank(g % 4, 480)[ps, :].rearrange("p (k h r) -> p h r k", k=8, h=4)
                        m = maskb[ps, 8 * g:8 * g + 8].rearrange("p (a b k) -> p a b k", a=1, b=1)
                        ins = dve.tensor_tensor(bias[ps, :, :, 8 * g:8 * g + 8], src[:, :, 1 - half:15 - half, :],
                                                bc(m, [64, 4, 14, 8]), ALU.add)
                    ins.then_inc(bias_ready.sem, 1)
                with dve.Fori(0, ADA_UNITS // 2) as i:
                    for j in range(2):
                        dve.wait_ge(w_hi.sem, l * V_ALL + i * 2 + (j + 1))
                        dve.tensor_tensor(wlo[j][:, 768:2048], wf[j][:, 768:2048], whi[j][:, 768:2048], ALU.subtract
                                          ).then_inc(w_lo_dve.sem, 1)
                dve.wait_ge(*ada_used(l, ADA_UNITS))
                dve.tensor_tensor(ada[:, :, :], PS[:, 3, 512:608].rearrange("p (k s) -> p k s", s=2),
                                  bc(pcol[:, PC_ADA:PC_G1].rearrange("p (k o) -> p k o", o=1), [P, 48, 2]), ALU.add)
                dve.drain()
                for n, g in enumerate((PC_G1, PC_G2)):
                    ins = dve.scalar_tensor_tensor(out=gs[:, n, :, :], in0=ada[:, 24 * n + 8:24 * n + 16, :], scalar=1.0,
                                                   in1=bc(pcol[:, g:g + 8].rearrange("p (k o) -> p k o", o=1), [P, 8, 2]),
                                                   op0=ALU.add, op1=ALU.mult)
                ins.then_inc(ada_ready.sem, 1)
                dve.drain()
                norm(l, 0)
                dve.wait_ge(*sig_ready(l, 1))
                for a, b in ((0, PAD), (PAD + CTX, 2 * PAD + CTX), (2 * PAD + TOK, 3 * PAD + TOK)):
                    dve.memset(zpad[:, :, a:b], 0.0)
                for c in range(2):
                    dve.wait_ge(*sig_ready(l, c + 1))
                    for (a, b), z0 in zip(SEG, (PAD, 2 * PAD)):
                        ins = dve.tensor_tensor(zpad[:, c, z0 + a:z0 + b], pr(c)[:, a:b], zsg[:, c, a:b], ALU.mult)
                    ins.then_inc(z_ready.sem, 1)
                NZ = TOK + PAD
                for k in range(CONV_K):
                    dve.drain()
                    for c in range(2):
                        if k == 0:
                            dve.tensor_scalar(zacc[:, c, :], zpad[:, c, 0:NZ], cw[:, c, 0:1],
                                              pcol[:, PC_CB + c:PC_CB + c + 1], ALU.mult, ALU.add)
                        else:
                            ins = dve.scalar_tensor_tensor(out=zacc[:, c, :], in0=zpad[:, c, k:k + NZ],
                                                           scalar=cw[:, c, k:k + 1], in1=zacc[:, c, :],
                                                           op0=ALU.mult, op1=ALU.add)
                ins.then_inc(cv_ready.sem, 1)
                dve.wait_ge(*mu_done(l, 1))
                dve.tensor_scalar(rsb[:, :], pr(0), 1.0 / CONV_CH, None, ALU.mult)
                dve.drain()
                for c in range(2):
                    for (a, b), z0 in zip(SEG, (0, PAD)):
                        ins = dve.tensor_tensor(zc[:, c, a:b], zacc[:, c, z0 + a:z0 + b], rsb[:, a:b], ALU.subtract)
                    ins.then_inc(zc_ready.sem, 1)
                dve.drain()
                dve.wait_ge(*zv_done(l, 1))
                dve.tensor_scalar(rsb[:, :], pr(1), 1.0 / CONV_CH, EPS, ALU.mult, ALU.add).then_inc(zvar_ready.sem, 1)
                dve.wait_ge(*zstd_ready(l, 1))
                dve.reciprocal(rsb[:, :], rsb[:, :])
                dve.drain()
                for c in range(2):
                    dve.tensor_tensor(zc[:, c, :], zc[:, c, :], rsb[:, :], ALU.mult).then_inc(zn_ready.sem, 1)
                dve.drain()
                for c in range(2):
                    dve.wait_ge(*zs_ready(l, c + 1))
                    dve.tensor_copy(zhi[:, c, :], zs[:, c, :])
                dve.drain()
                ins = dve.tensor_tensor(zlo[:, :, :], zs[:, :, :], zhi[:, :, :], ALU.subtract).then_inc(z_split.sem, 1)
                dve.drain()
                dve.wait_ge(*proj_ready(l, 40))
                cq2 = csq[:, 0:1280].rearrange("p (t n) -> p t n", t=TILES)
                ck2 = csq[:, 1280:1920].rearrange("p (t n) -> p t n", t=TILES)
                dve.tensor_tensor(cq2, proj[:, :, C_CQ:C_CKV], proj[:, :, C_CQ:C_CKV], ALU.mult)
                dve.tensor_tensor(ck2, proj[:, :, C_CKV:C_CKR], proj[:, :, C_CKV:C_CKR], ALU.mult)
                dve.drain()
                dve.tensor_reduce(cstat[:, 2, 0:5], cq2, AX_X, ALU.add)
                dve.tensor_reduce(cstat[:, 2, 5:10], ck2, AX_X, ALU.add)
                dve.drain()
                dve.tensor_scalar(cstat[:, 0, 0:5], cstat[:, 2, 0:5], 1.0 / 256, EPS, ALU.mult, ALU.add)
                dve.tensor_scalar(cstat[:, 0, 5:10], cstat[:, 2, 5:10], 1.0 / 128, EPS, ALU.mult, ALU.add
                                  ).then_inc(cv_var.sem, 1)
                dve.wait_ge(*cv_std(l, 1))
                dve.reciprocal(cstat[:, 2, :], cstat[:, 1, :])
                dve.wait_ge(*v_hi(l, 1))
                for br, col in enumerate((C_AV, C_BV)):
                    w = slice(256 * br, 256 * br + 256)
                    dve.tensor_tensor(vlo[:, 1:5, w], proj[:, 1:5, col:col + 256], vhi[:, 1:5, w], ALU.subtract)
                    dve.tensor_tensor(vlo[:, 5, w], proj[:, 0, col:col + 256], vhi[:, 5, w], ALU.subtract)
                dve.tensor_tensor(vlo[:, 0, 0:512], cache[:, 512:1024], vhi[:, 0, 0:512], ALU.subtract
                                  ).then_inc(v_ready.sem, 1)
                SCALE = (32 ** -0.5, 64 ** -0.5, 64 ** -0.5)

                def rotate(src, out, tile, heads):
                    c = cosb[:, tile - 1:tile, :]
                    r1 = rope1[:, 0:heads * 32].rearrange("p (h n) -> p h n", n=32)
                    r2 = rope2[:, 0:heads * 32].rearrange("p (h n) -> p h n", n=32)
                    dve.tensor_tensor(r1, src, bc(c, [P, heads, 32]), ALU.mult)
                    for half in range(2):
                        for a in range(2):
                            o = 16 * a + 8 * half
                            i = 16 * a + 8 * (1 - half)
                            dve.tensor_tensor(r2[:, :, o:o + 8], src[:, :, i:i + 8],
                                              bc(sinb[:, tile - 1:tile, o:o + 8], [P, heads, 8]), ALU.mult)
                    dve.drain()
                    return dve.tensor_tensor(out, r1, r2, ALU.add)

                def cols(n):
                    kt = 0 if n == TILES else keytile(n)
                    return slice(kt * P, (kt + 1) * P)

                def turned(n, br, src, ready):
                    tk = slice(n * P, (n + 1) * P)
                    b2 = slice(2 * br, 2 * br + 2)
                    dve.scalar_tensor_tensor(out=qTlo[:, b2, tk], in0=src[:, 0:256].rearrange("p (c n) -> p c n", c=2),
                                             scalar=SCALE[br], in1=qThi[:, b2, tk], op0=ALU.mult, op1=ALU.subtract)
                    dve.tensor_tensor(kTlo[:, b2, cols(n)], src[:, 256:512].rearrange("p (c n) -> p c n", c=2),
                                      kThi[:, b2, cols(n)], ALU.subtract).then_inc(ready.sem, 1)

                for n in range(TILES + 1):
                    own = n < TILES
                    dve.drain()
                    if own and n:
                        dve.wait_ge(*ab_t(l, 2 * n - 1))
                        rotate(proj[:, n, 0:512].rearrange("p (h n) -> p h n", n=32),
                               roped.rearrange("p (h n) -> p h n", n=32), n, 16).then_inc(roped_ready.sem, 1)
                    elif not n:
                        dve.nop().then_inc(roped_ready.sem, 1)
                    if own:
                        if n:
                            dve.wait_ge(*cn_t(l, n))
                        for a, b, r, g in ((0, 256, n, 64), (256, 384, 5 + n, 320)):
                            ins = dve.scalar_tensor_tensor(out=cn[:, a:b], in0=proj[:, n, C_CQ + a:C_CQ + b],
                                                           scalar=cstat[:, 2, r:r + 1], in1=rowg[:, g:g + b - a],
                                                           op0=ALU.mult, op1=ALU.mult)
                        if n == 0:
                            dve.drain()
                            ins = dve.scalar_tensor_tensor(out=proj[:, 0, C_CKV:C_CKR], in0=proj[:, 0, C_CKV:C_CKR],
                                                           scalar=cstat[:, 2, 5:6], in1=rowg[:, 320:448],
                                                           op0=ALU.mult, op1=ALU.mult)
                        ins.then_inc(cn_ready.sem, 1)
                        for br in range(2):
                            dve.wait_ge(*ab_hi(l, 2 * n + br + 1))
                            turned(n, br, bank(4 + br + 2 * (n % 2)), ab_ready)
                    else:
                        dve.nop().then_inc(cn_ready.sem, 1)
                        dve.wait_ge(*ab_hi(l, 11))
                        dve.tensor_tensor(kTlo[:, 0:4, cols(n)], bank(6).rearrange("p (c n) -> p c n", c=4),
                                          kThi[:, 0:4, cols(n)], ALU.subtract).then_inc(ab_ready.sem, 1)
                    dve.wait_ge(*cT_hi(l, n + 1))
                    lo = 0 if own else 256
                    dve.tensor_tensor(cTlo[:, lo:384], bank(0)[:, lo:384], cThi[:, lo:384], ALU.subtract
                                      ).then_inc(cT_ready.sem, 1)
                    dve.wait_ge(*qkc_raw(l, n + 1))
                    kt = keytile(n) if own else 0
                    dve.tensor_tensor(vlo[:, kt, 512:768].rearrange("p (h n) -> p h n", h=4),
                                      bank(2, 384).rearrange("p (h n) -> p h n", h=4)[:, :, 32:96],
                                      vhi[:, kt, 512:768].rearrange("p (h n) -> p h n", h=4), ALU.subtract
                                      ).then_inc(up_free.sem, 1)
                    if own and n:
                        v = qkc.rearrange("p (h n) -> p h n", h=8)[:, :, 32:64]
                        dve.drain()
                        rotate(v, v, n, 8).then_inc(qkc_ready.sem, 1)
                    else:
                        dve.nop().then_inc(qkc_ready.sem, 1)
                    dve.wait_ge(*c_hi(l, n + 1))
                    if own:
                        turned(n, 2, bank(3), c_ready)
                    else:
                        dve.tensor_tensor(kTlo[:, 4:6, cols(n)], bank(3)[:, 256:512].rearrange("p (c n) -> p c n", c=2),
                                          kThi[:, 4:6, cols(n)], ALU.subtract).then_inc(c_ready.sem, 1)
                for ti, tile in enumerate((1, 2, 3, 4, 0)):
                    nk = TOK if tile else P
                    for step in range(HDS + 2):
                        if step < HDS:
                            for m in ((2 * step, 2 * step + 1) if step < 4 else (step + 4,)):
                                dve.wait_ge(*s_done(l, ti * MAPS + m + 1))
                                if 8 <= m < 12 and tile:
                                    s0 = 6 - 2 * (tile - 1)
                                    dve.tensor_tensor(pr(m % 2)[:, CTX:TOK], pr(m % 2)[:, CTX:TOK],
                                                      bias[:, m - 8, s0:s0 + 8, :].rearrange("p r c -> p (r c)"), ALU.add)
                                    dve.drain()
                                dve.tensor_reduce(stat[:, 0, m:m + 1], pr(m % 2)[:, 0:nk], AX_X, ALU.max, negate=True
                                                  ).then_inc(mx_ready.sem, 1)
                        if 1 <= step <= HDS:
                            hd = step - 1
                            dve.wait_ge(*pt_hi(l, ti * HDS + hd + 1))
                            dve.tensor_tensor(ptlo[:, hd % 2, 0:nk], pr(2)[:, 0:nk], pthi[:, hd % 2, 0:nk], ALU.subtract
                                              ).then_inc(pt_ready.sem, 1)
                        if step < HDS:
                            m = 2 * step if step < 4 else step + 4
                            nm = 2 if step < 4 else 1
                            dve.wait_ge(*ex_ready(l, ti * MAPS + m + nm))
                            dve.reciprocal(stat[:, 2, m:m + nm], stat[:, 1, m:m + nm]).then_inc(rec_ready.sem, 1)
                            if step < 4:
                                dve.drain()
                                dve.scalar_tensor_tensor(out=cfa[:, 0, step:step + 1], in0=stat[:, 1, m:m + 1],
                                                         scalar=nlam, in1=stat[:, 2, m + 1:m + 2],
                                                         op0=ALU.mult, op1=ALU.mult)
                                dve.drain()
                                if step >= 2:
                                    dve.wait_ge(*pt_done(l, ti * HDS + step - 1))
                                dve.scalar_tensor_tensor(out=wmix[:, step % 2, 0:nk], in0=ex[:, (m + 1) % 4, 0:nk],
                                                         scalar=cfa[:, 0, step:step + 1], in1=ex[:, m % 4, 0:nk],
                                                         op0=ALU.mult, op1=ALU.add).then_inc(mix_ready.sem, 1)
                    dve.wait_ge(*o_ready(l, (ti + 1) * HDS))
                    oa = otok[:, 0:256].rearrange("p (h n) -> p h n", h=4)
                    dve.tensor_tensor(osq, otok[:, 0:256], otok[:, 0:256], ALU.mult)
                    dve.drain()
                    dve.tensor_reduce(ostat[:, 2, :], osq.rearrange("p (h n) -> p h n", h=4), AX_X, ALU.add)
                    dve.drain()
                    dve.tensor_scalar(ostat[:, 0, :], ostat[:, 2, :], 1.0 / 64, EPS, ALU.mult, ALU.add
                                      ).then_inc(ovar_ready.sem, 1)
                    dve.wait_ge(*ostd_ready(l, ti + 1))
                    dve.reciprocal(ostat[:, 2, :], ostat[:, 1, :])
                    dve.drain()
                    dve.tensor_tensor(oa, oa, bc(ostat[:, 2, :].rearrange("p (h o) -> p h o", o=1), [P, 4, 64]), ALU.mult)
                    dve.drain()
                    dve.tensor_tensor(oa, oa, bc(rowg[:, 0:64].rearrange("p (o n) -> p o n", o=1), [P, 4, 64]), ALU.mult
                                      ).then_inc(on_ready.sem, 1)
                    dve.wait_ge(*ot_hi(l, ti + 1))
                    if ti == 0:
                        dve.wait_ge(*own_out(l, 6 * 16)) 
                    dve.tensor_tensor(oTlo[:, :, tile * P:(tile + 1) * P],
                                      PS[:, 2, 0:768].rearrange("p (c n) -> p c n", c=6),
                                      oThi[:, :, tile * P:(tile + 1) * P], ALU.subtract).then_inc(ot_ready.sem, 1)
                with dve.Fori(0, KC // 2) as d2:
                    for b in range(4):
                        for c in range(2):
                            dve.drain()
                            dve.wait_ge(*b_done(l, d2 * 8 + (2 * b + c + 1)))
                            dve.wait_ge(*g_ready(l, d2 * 8 + (2 * b + c + 1)))
                            dst = mt[:, c, :] if b else macc[:, c, :]
                            dve.tensor_tensor(dst, pr(2 + c), sg[:, c, :], ALU.mult).then_inc(m_used.sem, 1)
                            if b:
                                dve.drain()
                                ins = dve.tensor_tensor(macc[:, c, :], macc[:, c, :], mt[:, c, :], ALU.add)
                            if b == 3:
                                ins.then_inc(m_ready.sem, 1)
                    for c in range(2):
                        dve.wait_ge(*m_hi(l, d2 * 2 + (c + 1)))
                        dve.tensor_tensor(mlo[:, ds(d2 * 2 + c, 1), :].rearrange("p o n -> p (o n)"), macc[:, c, :],
                                          mhi[:, ds(d2 * 2 + c, 1), :].rearrange("p o n -> p (o n)"), ALU.subtract
                                          ).then_inc(m_split.sem, 1)

                def residual(k, pair, gate, ready):
                    for s, (a, b) in enumerate(SEG):
                        xk = xT[:, ds(k, 1), a:b].rearrange("p o n -> p (o n)")
                        ins = dve.scalar_tensor_tensor(out=xk, in0=pr(pair)[:, a:b],
                                                       scalar=ada[:, ds(k + gate, 1), s:s + 1].rearrange("p o n -> p (o n)"),
                                                       in1=xk, op0=ALU.mult, op1=ALU.add)
                    ins.then_inc(ready.sem, 1)

                with dve.Fori(0, 2) as i:
                    for c in range(4):
                        dve.wait_ge(*y_done(l, i * 4 + (c + 1)))
                        residual(i * 4 + c, c, 16, x1_ready)
                dve.wait_ge(*x1_ready(l, 8))
                norm(l, 1)
                dve.drain()
                dve.wait_ge(*hf_used(l, KC))
                dve.tensor_scalar(lgT, pr(3)[0:20, :], rbias[:, 0:1], None, ALU.add).then_inc(lg_ready.sem, 1)
                dve.wait_ge(*lgt_done(l, 1))
                dve.tensor_copy(route[:, :, :], bank(4, 100).rearrange("p (t n) -> p t n", t=TILES))
                dve.drain()

                def col(n, shape):
                    return bc(rcol[:, n, :].rearrange("p (t o) -> p t o", o=1), shape)

                T4 = [P, TILES, 4]

                def first_max(src, out, n):
                    dve.tensor_reduce(rcol[:, n, :], src, AX_X, ALU.max)
                    dve.drain()
                    dve.tensor_tensor(out, src, col(n, T4), ALU.is_equal)
                    dve.drain()
                    dve.tensor_tensor(out, out, bc(tie[:, :].rearrange("p (o n) -> p o n", o=1), T4), ALU.mult)
                    dve.drain()
                    dve.tensor_reduce(rcol[:, 7, :], out, AX_X, ALU.max)
                    dve.drain()
                    dve.tensor_tensor(out, out, col(7, T4), ALU.is_equal)
                    dve.drain()

                lg = route[:, :, 0:4]
                oh, oh1, oh2, sel, sel2 = (rw[:, :, 16 + 4 * q:20 + 4 * q] for q in range(5))
                first_max(lg, oh, 0)
                dve.tensor_tensor(ex5[:, :, 0:4], lg, col(0, T4), ALU.subtract)
                w16 = rw[:, :, 0:16].rearrange("p t (g e) -> p t g e", g=4)
                for g in range(4):
                    dve.tensor_tensor(rw[:, :, 4 * g:4 * g + 4], route[:, :, 4 + 4 * g:8 + 4 * g],
                                      bc(oh[:, :, g:g + 1], T4), ALU.mult)
                dve.drain()
                dve.tensor_reduce(sel, rw[:, :, 0:16].rearrange("p t (g e) -> p t e g", g=4), AX_X, ALU.add)
                dve.drain()
                first_max(sel, oh1, 1)
                dve.scalar_tensor_tensor(out=sel2, in0=oh1, scalar=NEG, in1=sel, op0=ALU.mult, op1=ALU.add)
                dve.drain()
                first_max(sel2, oh2, 2)
                dve.tensor_tensor(ex5[:, :, 4], rcol[:, 2, :], rcol[:, 1, :], ALU.subtract).then_inc(rmax_ready.sem, 1)
                dve.wait_ge(*rexp_ready(l, 1))
                dve.tensor_reduce(rcol[:, 3, :], ex5[:, :, 0:4], AX_X, ALU.add)
                dve.tensor_scalar(rcol[:, 4, :], ex5[:, :, 4], 1.0, None, ALU.add)
                dve.drain()
                dve.tensor_tensor(rcol[:, 5, :], rcol[:, 3, :], rcol[:, 4, :], ALU.mult)
                dve.drain()
                dve.reciprocal(rcol[:, 3, :], rcol[:, 5, :])
                dve.drain()
                dve.tensor_tensor(rcol[:, 4, :], rcol[:, 3, :], ex5[:, :, 4], ALU.mult)
                dve.drain()
                for n in (3, 4):
                    dve.tensor_scalar(rcol[:, n + 2, :], rcol[:, n, :], 1.0 / A_SCALE, None, ALU.mult)
                for ch, o in enumerate((oh1, oh2)):
                    for g in range(4):
                        dve.tensor_tensor(ohm[:, 5 * ch:5 * ch + 5, 4 * g:4 * g + 4], o, bc(oh[:, :, g:g + 1], T4), ALU.mult)
                dve.drain()
                dve.tensor_tensor(cum, ohm[:, 0:5, :], ohm[:, 5:10, :], ALU.add).then_inc(hot_ready.sem, 1)
                dve.wait_ge(*cnt_done(l, 1))
                dve.wait_ge(*route_in(l, 16))
                dve.memset(acc[:, 0, :], 0.0)
                for cs in csum:
                    dve.memset(cs[:, 0:8], 0.0)
                dve.drain()
                for tile in range(TILES):
                    dve.tensor_tensor(acc[:, tile + 1, :], acc[:, tile, :], bank(4)[:, 256 + 16 * tile:272 + 16 * tile],
                                      ALU.add)
                    dve.drain()
                dve.tensor_tensor(cum, bank(4)[:, 128:208].rearrange("p (t e) -> p t e", t=TILES), acc[:, 0:5, :], ALU.add)

                def flat(ap):
                    return ap.rearrange("p a b -> p (a b)")

                def count(out, left, right, op, a, b):
                    tb = tbl[:, 0:a * b].rearrange("p (a b) -> p a b", a=a)
                    dve.tensor_tensor(tb, bc(left.rearrange("p (a o) -> p a o", o=1), [P, a, b]),
                                      bc(right.rearrange("p (o b) -> p o b", o=1), [P, a, b]), op)
                    dve.drain()
                    dve.tensor_reduce(out, tb, AX_X, ALU.add)
                    dve.drain()

                count(nch, acc[:, 5, :], steps, ALU.is_gt, EXPERTS, 5)
                dve.tensor_copy(csum[0][:, 8:24], nch)
                dve.drain()
                for n, sh in enumerate((1, 2, 4, 8)):
                    a, o = csum[n % 2], csum[1 - n % 2]
                    dve.tensor_tensor(o[:, 8:24], a[:, 8:24], a[:, 8 - sh:24 - sh], ALU.add)
                    dve.drain()
                incl = csum[0][:, 8:24]
                dve.tensor_tensor(first, incl, nch, ALU.subtract)
                dve.drain()
                for ch in range(2):
                    tb = tbl[:, 160 * ch:160 * ch + 80].rearrange("p (t e) -> p t e", t=TILES)
                    dve.tensor_tensor(tb, ohm[:, 5 * ch:5 * ch + 5, :], cum, ALU.mult)
                    tb = tbl[:, 160 * ch + 80:160 * ch + 160].rearrange("p (t e) -> p t e", t=TILES)
                    dve.tensor_tensor(tb, ohm[:, 5 * ch:5 * ch + 5, :], bc(first.rearrange("p (o e) -> p o e", o=1), [P, 5, 16]),
                                      ALU.mult)
                dve.drain()
                r20 = scratch[:, 2376:2396]
                dve.tensor_reduce(r20, tbl[:, 0:320].rearrange("p (n e) -> p n e", n=20), AX_X, ALU.add)
                dve.drain()
                rank = rsel[:, 2, :]
                for ch in range(2):
                    dve.tensor_copy(rank[:, 5 * ch:5 * ch + 5], r20[:, 10 * ch:10 * ch + 5])
                    dve.tensor_copy(rsel[:, 3, 5 * ch:5 * ch + 5], r20[:, 10 * ch + 5:10 * ch + 10])
                dve.drain()
                whole, row, chunk = rsel[:, 4, :], rsel[:, 5, :], rsel[:, 6, :]
                count(whole, rank, steps[:, 1:5], ALU.is_ge, 10, 4)
                dve.scalar_tensor_tensor(out=row, in0=whole, scalar=-float(P), in1=rank, op0=ALU.mult, op1=ALU.add)
                dve.tensor_tensor(chunk, whole, rsel[:, 3, :], ALU.add)
                dve.drain()
                dve.scalar_tensor_tensor(out=slotf[:, :], in0=chunk, scalar=float(P), in1=row, op0=ALU.mult, op1=ALU.add)
                for n in range(10):
                    dve.tensor_scalar(rowhot[:, n, :], iota, row[:, n:n + 1], None, ALU.is_equal)
                    ins = dve.tensor_scalar(chhot[:, n, :], iota[:, 0:CHUNKS + 1], chunk[:, n:n + 1],
                                            tokid[:, n % 5:n % 5 + 1], ALU.is_equal, ALU.mult)
                ins.then_inc(place_ready.sem, 1)
                count(cef, iota[:, 0:CHUNKS + 1], incl, ALU.is_ge, CHUNKS + 1, EXPERTS)
                dve.tensor_scalar(cexp[:, :], cef, float(EXPERTS - 1), None, ALU.min)
                dve.scalar_tensor_tensor(out=rsel[:, 0, 0:1], in0=loopf[:, 0:1], scalar=1.0, in1=loopf[:, 1:2],
                                         op0=ALU.add, op1=ALU.add)
                dve.tensor_tensor(rsel[:, 0, 1:2], loopf[:, 2:3], loopf[:, 1:2], ALU.add)
                dve.drain()
                dve.tensor_copy(loopf[:, 0:1], rsel[:, 0, 0:1])
                dve.tensor_copy(loopf[:, 2:3], rsel[:, 0, 1:2])
                count(loopf[:, 1:2], incl[:, 15:16], iota[:, 1:CHUNKS + 1:2], ALU.is_gt, 1, PAIRS + 1)
                dve.tensor_copy(loopi[:, :], loopf[:, :])
                dve.wait_ge(*list_done(l, 1))
                dve.tensor_copy(idxall[:, :], bank(5, CHUNKS + 1)).then_inc(route_ready.sem, 1)
                dve.wait_ge(started.sem, 1)
                dve.wait_ge(*route_ready(l, 1))
                b, m, ran, done = loops(dve)

                def index(c, j):
                    dve.tensor_scalar(idxf[:, j:j + 1], idxall[:, ds(c, 1)], 0.0, None, ALU.add).then_inc(idx_ready.sem, 1)

                def part_low(c, j, q):
                    dve.wait_ge(mw_hi.sem, b * 6 + (c * 3 + (q + 1)))
                    dve.tensor_tensor(mwlo[3 * j + q], mwf[3 * j + q], mwhi[3 * j + q], ALU.subtract).then_inc(mw_lo.sem, 1)

                def rows_low(c, j):
                    dve.wait_ge(hs_hi.sem, b * 2 + (c + 1))
                    dve.tensor_tensor(hslo[j], PS[:, 0, :].rearrange("p (k n) -> p k n", k=KC), hshi[j], ALU.subtract
                                      ).then_inc(hs_ready.sem, 1)

                def multiply(c, j, first=False):
                    dve.wait_ge(msilu_ready.sem, done + (c + 1))
                    if not first:
                        dve.wait_ge(at_done.sem, done + (c - 1))
                    dve.tensor_tensor(mact[j], msg[j], bank(2 + j)[:, 256:512], ALU.mult).then_inc(mact_ready.sem, 1)

                def act_low(c, j):
                    dve.wait_ge(at_hi.sem, done + (c + 1))
                    dve.scalar_tensor_tensor(out=atlo[j], in0=bank(4 + j, 256).rearrange("p (c n) -> p c n", c=2),
                                             scalar=A_SCALE, in1=athi[j], op0=ALU.mult, op1=ALU.subtract
                                             ).then_inc(at_ready.sem, 1)

                for c in range(2):
                    index(c, c)
                for q in range(2):
                    part_low(0, 0, q)
                rows_low(0, 0)
                for q in range(2):
                    part_low(1, 1, q)
                multiply(0, 0, True)
                rows_low(1, 1)
                act_low(0, 0)
                with dve.Fori(0, m) as i:
                    for n in range(2):
                        c, j = i * 2 + (1 + n), 1 - n
                        dve.wait_ge(ht_done.sem, b * 2 + (i * 2 + (n + 1)))
                        index(i * 2 + (2 + n), n)
                        for q in range(2):
                            part_low(i * 2 + (2 + n), n, q)
                        multiply(c, j)
                        rows_low(i * 2 + (2 + n), n)
                        act_low(c, j)
                for tile in range(TILES):
                    dve.drain()
                    dve.wait_ge(*cg_in[tile](l, 32))
                    if tile >= 2:
                        dve.wait_ge(*yt_done(l, tile - 1))
                    dve.tensor_scalar(cga[:, tile, :], cga[:, tile, :], rcol[:, 5, tile:tile + 1], None, ALU.mult)
                    dve.drain()
                    dve.scalar_tensor_tensor(out=ybuf[tile % 2], in0=cgb[:, tile, :], scalar=rcol[:, 6, tile:tile + 1],
                                             in1=cga[:, tile, :], op0=ALU.mult, op1=ALU.add).then_inc(comb_ready.sem, 1)
                    dve.wait_ge(*yt_done(l, tile + 1))
                    s = 0 if tile == 0 else 1
                    xk = xT[:, :, tile * P:(tile + 1) * P]
                    yk = PS[:, tile % 2, :].rearrange("p (k n) -> p k n", k=KC)
                    dve.tensor_tensor(cga[:, tile, :].rearrange("p (k n) -> p k n", k=KC), yk,
                                      bc(ada[:, 40:48, s:s + 1], [P, KC, P]), ALU.mult)
                    dve.drain()
                    dve.tensor_tensor(xk, xk, cga[:, tile, :].rearrange("p (k n) -> p k n", k=KC), ALU.add
                                      ).then_inc(x2_ready.sem, 1)
            root(LAYERS, 0)
            for k in range(KC):
                if k >= 2:
                    dve.wait_ge(*fin_t(0, k - 1))
                dve.scalar_tensor_tensor(out=tmp[:, k % 2, :], in0=xT[:, k, :], scalar=gfin[:, k:k + 1], in1=rsb[:, :],
                                         op0=ALU.mult, op1=ALU.mult).then_inc(fin_ready.sem, 1)


_INS = ['x_prompt', 'x_sample', 'cache_a_k', 'cache_a_v', 'cache_b_k', 'cache_b_v', 'cache_c_kv', 'cache_c_krope',
        'c', 'c_ctx', 'norm1_g', 'norm2_g', 'w_ada', 'b_ada', 'w_in', 'a_lambda', 'a_subln_g', 'a_wo', 'b_rpb', 'b_wo',
        'c_q_norm_g', 'c_kv_norm_g', 'c_wuq', 'c_wukv', 'c_wo', 'd_conv_w', 'd_conv_b', 'd_ln_g', 'd_ln_b', 'd_wo',
        'w_gate', 'b_gate', 'w_out', 'moe_w_group', 'moe_b_group', 'moe_w_expert', 'moe_b_expert', 'moe_w1', 'moe_w2',
        'final_norm_g']
_OUTS = [('y_prompt', (1, 128, 1024)), ('y_sample', (1, 512, 1024)), ('new_a_k', (1, 2, 128, 4, 64)),
         ('new_a_v', (1, 2, 128, 4, 64)), ('new_b_k', (1, 2, 128, 4, 64)), ('new_b_v', (1, 2, 128, 4, 64)),
         ('new_c_kv', (1, 2, 128, 128)), ('new_c_krope', (1, 2, 128, 32))]


def shape_constants():
    f = np.float32
    h = 8
    tok = np.arange(LAT)
    inv = (f(10000.0) ** (-np.arange(h, dtype=f) / f(h))).astype(f)
    ar = (tok // GRID_W).astype(f)[:, None] * inv[None, :]
    ac = (tok % GRID_W).astype(f)[:, None] * inv[None, :]
    ang = np.concatenate([ar, ar, ac, ac], axis=-1)
    sign = np.repeat(np.array([-1, 1, -1, 1], dtype=f), h)
    cos = np.cos(ang).astype(f).reshape(4, P, 32).transpose(1, 0, 2)
    sin = (np.sin(ang).astype(f) * sign).reshape(4, P, 32).transpose(1, 0, 2)
    q = np.arange(P) % GRID_W
    start = np.clip(q - 8, 0, GRID_W - 16)[:, None]
    k = np.arange(GRID_W)[None, :]
    mask = np.where((k >= start) & (k < start + 16), 0.0, NEG).astype(f)
    j, w = np.arange(31)[:, None], np.arange(207)[None, :]
    band = ((w + j == 94) | (w + j == 94 + 64)).astype(f)
    init = [0.8 - 0.6 * math.exp(-0.3 * layer) for layer in range(LAYERS)]
    return {
        'k_ident': np.eye(P, dtype=f), 'k_cos': np.ascontiguousarray(cos), 'k_sin': np.ascontiguousarray(sin),
        'k_mask': mask, 'k_band': band, 'k_tie': np.tile(np.array([4, 3, 2, 1], dtype=f), (P, 1)),
        'k_route': np.concatenate([np.tile(np.arange(P), (P, 1)), np.triu(np.ones((P, P)), 1),
                                   np.arange(P)[:, None] + P * np.arange(TILES)[None, :],
                                   np.tile(P * np.arange(5), (P, 1))], axis=1).astype(f),
        'k_lam': np.array([[x, 1.0 - x] for x in init], dtype=f),
    }


def kernel(**inputs):
    import numpy as _np
    import concourse.bacc as _bacc
    from concourse.bass_utils import run_bass_kernel_spmd as _run

    nc = _bacc.Bacc("TRN2", target_bir_lowering=False, num_devices=1)
    arrays, aps = {}, {}
    given = {name: _np.ascontiguousarray(inputs[name]) for name in _INS}
    for name, a in {**given, **shape_constants()}.items():
        arrays[f"in_{name}"] = a
        aps[name] = nc.dram_tensor(f"in_{name}", a.shape, mybir.dt.from_np(a.dtype), kind="ExternalInput").ap()
    for name, shape in _OUTS:
        aps[name] = nc.dram_tensor(f"out_{name}", shape, F32, kind="ExternalOutput").ap()
    aps["h2_rows"] = nc.dram_tensor("h2_rows", [TOK, D], F32, kind="Internal").ap()
    aps["y_rows"] = nc.dram_tensor("y_rows", [CHUNKS * P, D], F32, kind="Internal").ap()
    build(nc, aps)
    r = _run(nc, [arrays], core_ids=[0])
    return tuple(r.results[0][f"out_{name}"] for name, _ in _OUTS)
```

```python
import math
from contextlib import ExitStack

import concourse.bass as bass
import numpy as np
from concourse import mybir

F32 = mybir.dt.float32
F16 = mybir.dt.float16
BF16 = mybir.dt.bfloat16
I32 = mybir.dt.int32
ALU = mybir.AluOpType
ACT = mybir.ActivationFunctionType
AX_X = mybir.AxisListType.X
ds = bass.ds

P = 128
LAYERS = 2
D = 1024
KC = D // P
CTX, LAT = 128, 512
TOK = CTX + LAT
TILES = TOK // P
EPS = 1e-6
GRID_W = 64
CONV_K, CONV_CH = 31, 256
PAD = CONV_K // 2
IN_COLS = 2464
HEADS = 4
EXPERTS, F_EXP = 16, 256
N_GROUPS = 4
NEG = -1e30

C_AQ, C_AV, C_BQ, C_BV, C_CQ, C_CKV, C_CKR, C_DU = 0, 512, 768, 1280, 1536, 1792, 1920, 1952
TOKCOLS = C_DU

ADA_UNITS = 6 * D // 256
ADA_SLOTS = 6
ADA_POOL = 768
IN_UNITS = 10
WO_UNITS = 4
GATE_UNITS = 16
OUT_UNITS = 4
V_IN = 0
V_WO = V_IN + IN_UNITS
V_GATE = V_WO + 2
V_OUT = V_GATE + GATE_UNITS
V_ALL = V_OUT + OUT_UNITS

CHUNKS = (2 * TOK + EXPERTS * (P - 1) + EXPERTS - 2) // P
PAIRS = (CHUNKS - 1) // 2
FILLS = 1 + -(-(CHUNKS - 1) // TILES)
A_SCALE = 1.0 / 16

PC_ADA, PC_G1, PC_G2, PC_BG, PC_CB, PC_LG, PC_LB, PC_N = 0, 48, 56, 64, 96, 98, 100, 102

LN_MEAN, LN_VAR = 28, 32

MAPS = 16
HDS = 12


class Signal:

    def __init__(self, sem, per_layer, before=0):
        self.sem, self.per_layer, self.before = sem, per_layer, before

    def __call__(self, layer, n):
        return self.sem, layer * self.per_layer + (self.before + n)


def build(nc, t):
    ctx = ExitStack()
    with ctx:
        def sb(name, shape, dt=F32):
            return ctx.enter_context(nc.sbuf_tensor(name, shape, dt))

        def sig(name, per_layer=0, before=0):
            return Signal(ctx.enter_context(nc.semaphore(name)), per_layer, before)

        xT = sb("xT", [P, KC, TOK])
        hpart = sb("hpart", [P, KC * TOK])
        hhi = hpart[:, 0:KC * TOK // 2].bitcast(F16).rearrange("p (k n) -> p k n", k=KC)
        hlo = hpart[:, KC * TOK // 2:KC * TOK].bitcast(F16).rearrange("p (k n) -> p k n", k=KC)
        wf = [sb(f"wf{j}", [P, 2048]) for j in range(2)]
        whi = [sb(f"whi{j}", [P, 2048], F16) for j in range(2)]
        wlo = [sb(f"wlo{j}", [P, 2048], F16) for j in range(2)]
        arena = sb("arena", [P, 23072])
        scratch = sb("scratch", [P, 4100])
        bias = sb("bias", [P, HEADS, 14, GRID_W])
        rsb = sb("rsb", [P, TOK])
        zhi = rsb[:, :].bitcast(F16).rearrange("p (c n) -> p c n", c=2)
        zlo = sb("zlo", [P, 2, TOK], F16)
        ident = sb("ident", [P, P])
        ones = sb("ones", [P, P])
        cosb = sb("cosb", [P, TILES - 1, 32])
        sinb = sb("sinb", [P, TILES - 1, 32])
        band = sb("band", [31, 207], BF16)
        prow = scratch[0:PC_N, 1152:1280]
        pcol = sb("pcol", [P, PC_N])
        cwrow = scratch[0:CONV_K, 896:1152]
        cw = sb("cw", [P, 2, CONV_K])
        rowg = sb("rowg", [P, 64 + 256 + 128])
        lamc = sb("lamc", [P, 2])
        lamt = sb("lamt", [P, 72])
        wr = sb("wr", [P, KC, 20])
        rbias = sb("rbias", [20, 1])
        gfin = sb("gfin", [P, KC])
        scf = sb("scf", [P, KC, 2])
        schi = sb("schi", [P, KC, 2], F16)
        sclo = sb("sclo", [P, KC, 2], F16)
        ada = sb("ada", [P, 6 * KC, 2])
        gs = sb("gs", [P, 2, KC, 2])
        stat = sb("stat", [P, 3, MAPS])
        cfa = sb("cfa", [P, 2, 4])
        cstat = sb("cstat", [P, 3, 10])
        ostat = sb("ostat", [P, 3, 4])
        wuf = scratch[:, 0:896]
        lamv = scratch[:, 1280:1408].rearrange("p (a n) -> p a n", a=4)
        rprow = scratch[0:60, 1408:1439]
        rpf = scratch[0:31, 1440:1500]
        rpd = scratch[0:31, 1500:1560]
        rp = scratch[0:31, 1560:1650].bitcast(BF16).rearrange("p (a n) -> p a n", a=3)
        maskb = scratch[:, 2040:2104]
        bandf = scratch[0:31, 1700:1907]
        crow = scratch[0:3 * KC, 1910:2038]
        wuhi = sb("wuhi", [P, 2 * 256 + 384], F16)
        wulo = sb("wulo", [P, 2 * 256 + 384], F16)
        PS = ctx.enter_context(nc.psum_tensor("PS", [P, 4, 1024], F32))

        proj = arena[:, 0:TILES * TOKCOLS].rearrange("p (t n) -> p t n", t=TILES)
        AR = TILES * TOKCOLS * 2
        ab = arena[:, :].bitcast(F16)
        kThi = ab[:, AR:AR + 4608].rearrange("p (c k) -> p c k", c=6)
        kTlo = ab[:, AR + 4608:AR + 9216].rearrange("p (c k) -> p c k", c=6)
        vhi = ab[:, AR + 9216:AR + 13824].rearrange("p (c k) -> p c k", c=6)
        vlo = ab[:, AR + 13824:AR + 18432].rearrange("p (c k) -> p c k", c=6)
        qThi = ab[:, AR + 18432:AR + 22272].rearrange("p (c k) -> p c k", c=6)
        qTlo = ab[:, AR + 22272:AR + 26112].rearrange("p (c k) -> p c k", c=6)
        oThi = ab[:, 0:3840].rearrange("p (c k) -> p c k", c=6)
        oTlo = ab[:, 3840:7680].rearrange("p (c k) -> p c k", c=6)
        pthi = ab[:, 7680:8960].rearrange("p (s k) -> p s k", s=2)
        ptlo = ab[:, 8960:10240].rearrange("p (s k) -> p s k", s=2)
        otok = arena[:, 5120:6656].rearrange("p (s n) -> p s n", s=2)
        wohi = ab[:, AR:AR + 8192].rearrange("p (b c n) -> p b c n", b=4, c=2)
        wolo = ab[:, AR + 8192:AR + 16384].rearrange("p (b c n) -> p b c n", b=4, c=2)
        wox = [arena[:, 6656:8704], bias[:, :, :, :].rearrange("p h r c -> p (h r c)")[:, 0:2048]]
        mhi = ab[:, AR + 16384:AR + 21504].rearrange("p (c k) -> p c k", c=KC)
        mlo = ab[:, AR + 21504:AR + 26624].rearrange("p (c k) -> p c k", c=KC)
        mwf = [wf[0][:, :], wf[1][:, :]] + [arena[:, 2048 * n:2048 * (n + 1)] for n in range(4)]
        mpt = [arena[:, 8192 + 1024 * n:8192 + 1024 * (n + 1)].bitcast(F16) for n in range(8)]
        mwhi = [whi[0][:, :], whi[1][:, :]] + mpt[0:4]
        mwlo = [wlo[0][:, :], wlo[1][:, :]] + mpt[4:8]
        htok = arena[:, 16384:16384 + TILES * D].rearrange("p (t n) -> p t n", t=TILES)
        xg = [hpart[:, 1024 * j:1024 * (j + 1)] for j in range(2)]
        hsv = [hpart[:, 2048 + 512 * n:2048 + 512 * (n + 1)].bitcast(F16).rearrange("p (k n) -> p k n", k=KC)
               for n in range(4)]
        hshi, hslo = hsv[0:2], hsv[2:4]
        cga = htok
        cgb = hpart[:, :].rearrange("p (t n) -> p t n", t=TILES)
        awf = [arena[:, 2048 * n:2048 * (n + 1)] for n in range(ADA_SLOTS)]
        apt = [arena[:, 12288 + 1024 * n:12288 + 1024 * (n + 1)].bitcast(F16) for n in range(4)]
        awhi, awlo = apt[0:2], apt[2:4]
        xtok = arena[:, 16384:16384 + TILES * D].rearrange("p (t n) -> p t n", t=TILES)
        ytok = arena[:, 0:TILES * D].rearrange("p (t n) -> p t n", t=TILES)

        xsq = scratch[:, 0:1280].rearrange("p (s n) -> p s n", s=2)
        xsq1 = arena[:, 21792:23072].rearrange("p (s n) -> p s n", s=2)
        tmp = scratch[:, 1280:2560].rearrange("p (s n) -> p s n", s=2)
        hf = scratch[:, 2560:3840].rearrange("p (s n) -> p s n", s=2)
        zpad = scratch[:, 0:1370].rearrange("p (c n) -> p c n", c=2)
        zacc = scratch[:, 1370:2680].rearrange("p (c n) -> p c n", c=2)
        zsg = scratch[:, 2680:3960].rearrange("p (c n) -> p c n", c=2)
        zc = scratch[:, 0:1280].rearrange("p (c n) -> p c n", c=2)
        zs = scratch[:, 1370:2650].rearrange("p (c n) -> p c n", c=2)
        csq = scratch[:, 0:1920]
        rope1 = scratch[:, 0:512]
        rope2 = scratch[:, 512:1024]
        roped = scratch[:, 1024:1536]
        qkc = scratch[:, 1536:2048]
        cn = scratch[:, 2048:2432]
        cThi = scratch[:, 2432:2624].bitcast(F16)
        cTlo = scratch[:, 2624:2816].bitcast(F16)
        cache = scratch[:, 2816:4000]
        ex = scratch[:, 0:2560].rearrange("p (s n) -> p s n", s=4)
        wmix = scratch[:, 2560:3840].rearrange("p (s n) -> p s n", s=2)
        osq = scratch[:, 3840:4096]
        sg = scratch[:, 0:1280].rearrange("p (s n) -> p s n", s=2)
        mt = scratch[:, 1280:2560].rearrange("p (s n) -> p s n", s=2)
        macc = scratch[:, 2560:3840].rearrange("p (s n) -> p s n", s=2)
        lgT = scratch[0:20, 3200:3840]
        ybuf = [scratch[:, 1024 * j:1024 * (j + 1)] for j in range(2)]
        msg = [scratch[:, 2048 + 256 * j:2304 + 256 * j] for j in range(2)]
        mact = [scratch[:, 2560 + 256 * j:2816 + 256 * j] for j in range(2)]
        atv = [scratch[:, 3072 + 128 * n:3200 + 128 * n].bitcast(F16).rearrange("p (c n) -> p c n", c=2)
               for n in range(4)]
        athi, atlo = atv[0:2], atv[2:4]
        rowhot = scratch[:, 0:1280].rearrange("p (n q) -> p n q", n=10)
        chhot = scratch[:, 1280:1280 + 10 * (CHUNKS + 2)].rearrange("p (n c) -> p n c", n=10)
        tbl = scratch[:, 2560:3040]
        ohm = scratch[:, 1960:2120].rearrange("p (n e) -> p n e", n=10)
        cum = scratch[:, 2120:2200].rearrange("p (t e) -> p t e", t=TILES)
        acc = scratch[:, 2200:2296].rearrange("p (t e) -> p t e", t=TILES + 1)
        nch = scratch[:, 2296:2312]
        csum = [scratch[:, 2312 + 24 * n:2336 + 24 * n] for n in range(2)]
        first = scratch[:, 2360:2376]
        rsel = scratch[:, 2376:2446].rearrange("p (q n) -> p q n", q=7)
        cef = scratch[:, 2446:2472]
        wuf32 = wuhi[:, :].bitcast(F32)
        route = wuf32[:, 0:100].rearrange("p (t n) -> p t n", t=5)
        rw = wuf32[:, 100:300].rearrange("p (t n) -> p t n", t=5)
        rcol = wuf32[:, 300:340].rearrange("p (q t) -> p q t", t=5)
        ex5 = wuf32[:, 340:365].rearrange("p (t n) -> p t n", t=5)
        tie = sb("tie", [P, 4])
        small = wulo[:, :].bitcast(F32)
        rk = small[:, 0:266]
        iota, before = rk[:, 0:P], rk[:, P:2 * P]
        tokid, steps = rk[:, 2 * P:2 * P + 5], rk[:, 2 * P + 5:2 * P + 10]
        slotf = small[:, 266:276].bitcast(I32)
        idxall = small[:, 276:276 + CHUNKS + 2].bitcast(I32)
        smalli = small[:, 276 + CHUNKS + 2:448].bitcast(I32)
        sloti, idxi = smalli[:, 0:10], smalli[:, 10:12]
        cexp = smalli[:, 12:12 + CHUNKS + 1]
        loopf = sb("loopf", [P, 3])
        loopi = sb("loopi", [P, 3], I32)
        zero1 = sb("zero1", [P, 1], I32)

        def pr(pair):
            return PS[:, pair, 384:1024]

        SEG = [(0, CTX), (CTX, TOK)]

        def bank(n, w=512):
            return PS[:, n // 2, 512 * (n % 2):512 * (n % 2) + w]

        consts_in = sig("consts_in")
        params_in = sig("params_in", 21 * 16)
        cache_in = sig("cache_in", 9 * 16)
        w_in = [sig(f"w_in{j}", V_ALL // 2 * 16) for j in range(2)]
        w_hi = sig("w_hi", V_ALL)
        w_lo = sig("w_lo", V_ALL, 1)
        x_in = [sig(f"x_in{n}", 16) for n in range(2)]
        x_hi, x_lo = sig("x_hi", 2), sig("x_lo", 2)
        wo_lo = sig("wo_lo", WO_UNITS, 1)
        a_in = [sig(f"a_in{n}", ADA_UNITS // ADA_SLOTS * 16) for n in range(ADA_SLOTS)]
        a_hi = sig("a_hi", ADA_UNITS)
        a_lo = sig("a_lo", ADA_UNITS, 1)
        a_lo_dve = sig("a_lo_dve", ADA_UNITS, 1)
        ada_used = sig("ada_used", ADA_UNITS, 2)
        set_ready = sig("set_ready")
        xt_done = sig("xt_done")
        x_even = sig("x_even")
        x_odd = sig("x_odd")
        cond_t = sig("cond_t")
        cond_f = sig("cond_f")
        cond_ready = sig("cond_ready")
        par_t = sig("par_t", 1)
        rp_ready = sig("rp_ready", 1)
        band_done = sig("band_done", 8)
        bias_ready = sig("bias_ready", 8)
        wu_hi = sig("wu_hi", 1)
        wu_ready = sig("wu_ready", 1)
        lam_sum = sig("lam_sum", 1)
        lam_exp = sig("lam_exp", 1)
        ada_ready = sig("ada_ready", 1)
        sq_ready = sig("sq_ready", 16)
        sq_used = sig("sq_used", 16)
        var_ready = sig("var_ready", 2)
        std_ready = sig("std_ready", 2)
        tmp_ready = sig("tmp_ready", 16)
        hf_ready = sig("hf_ready", 16)
        h_ready = sig("h_ready", 8)
        hf_used = sig("hf_used", 8)
        du_done = sig("du_done", 4)
        sig_ready = sig("sig_ready", 2)
        z_ready = sig("z_ready", 2)
        proj_done = sig("proj_done", 40)
        proj_ready = sig("proj_ready", 40)
        cv_ready = sig("cv_ready", 1)
        mu_done = sig("mu_done", 1)
        zc_ready = sig("zc_ready", 2)
        zsq_ready = sig("zsq_ready", 2)
        zv_done = sig("zv_done", 1)
        zvar_ready = sig("zvar_ready", 1)
        zstd_ready = sig("zstd_ready", 1)
        zn_ready = sig("zn_ready", 2)
        zs_ready = sig("zs_ready", 2)
        z_split = sig("z_split", 1)
        cv_var = sig("cv_var", 1)
        cv_std = sig("cv_std", 1)
        roped_ready = sig("roped_ready", 4)
        ab_t = sig("ab_t", 11)
        ab_hi = sig("ab_hi", 11)
        ab_ready = sig("ab_ready", 11)
        cn_ready = sig("cn_ready", 6)
        cn_t = sig("cn_t", 6)
        cT_hi = sig("cT_hi", 6)
        cT_ready = sig("cT_ready", 6)
        up_done = sig("up_done", 6)
        qkc_raw = sig("qkc_raw", 6)
        up_free = sig("up_free", 6)
        qkc_ready = sig("qkc_ready", 6)
        c_t = sig("c_t", 6)
        c_hi = sig("c_hi", 6)
        c_ready = sig("c_ready", 6)
        v_hi = sig("v_hi", 1)
        v_ready = sig("v_ready", 1)
        own_out = sig("own_out", 6 * 16)
        s_done = sig("s_done", TILES * MAPS)
        mx_ready = sig("mx_ready", TILES * MAPS)
        ex_ready = sig("ex_ready", TILES * MAPS)
        mix_ready = sig("mix_ready", TILES * 4)
        pt_done = sig("pt_done", TILES * HDS)
        pt_hi = sig("pt_hi", TILES * HDS)
        pt_ready = sig("pt_ready", TILES * HDS, 1)
        pv_done = sig("pv_done", TILES * HDS)
        rec_ready = sig("rec_ready", TILES * HDS)
        o_ready = sig("o_ready", TILES * HDS)
        ovar_ready = sig("ovar_ready", TILES)
        ostd_ready = sig("ostd_ready", TILES)
        on_ready = sig("on_ready", TILES)
        ot_done = sig("ot_done", TILES)
        ot_hi = sig("ot_hi", TILES)
        ot_ready = sig("ot_ready", TILES, 1)
        g_done = sig("g_done", 32)
        g_ready = sig("g_ready", 32, 2)
        b_done = sig("b_done", 32)
        m_used = sig("m_used", 32, 2)
        m_ready = sig("m_ready", 8)
        m_hi = sig("m_hi", 8)
        m_split = sig("m_split", 8)
        y_done = sig("y_done", 8)
        x1_ready = sig("x1_ready", 8, 2)
        lg_ready = sig("lg_ready", 1)
        lgt_done = sig("lgt_done", 1)
        rmax_ready = sig("rmax_ready", 1)
        rexp_ready = sig("rexp_ready", 1)
        htk_ready = sig("htk_ready", 8)
        rows_out = sig("rows_out", 16)
        route_in = sig("route_in", 16)
        hot_ready = sig("hot_ready", 1)
        cnt_done = sig("cnt_done", 1)
        place_ready = sig("place_ready", 1)
        list_done = sig("list_done", 1)
        route_ready = sig("route_ready", 1)
        filled = sig("filled", FILLS * 16)
        base_ready = sig("base_ready", 1)
        started = sig("started")
        ht_done, hs_hi, hs_ready = (sig(n) for n in ("ht_done", "hs_hi", "hs_ready"))
        mgu_done, msilu_ready, mact_ready = (sig(n) for n in ("mgu_done", "msilu_ready", "mact_ready"))
        at_done, at_hi, at_ready = (sig(n) for n in ("at_done", "at_hi", "at_ready"))
        my_done, my_ready = sig("my_done"), sig("my_ready")
        mw_hi = sig("mw_hi")
        mw_lo = sig("mw_lo")
        mw_lo2 = sig("mw_lo2")
        m_in = [sig(f"m_in{n}") for n in range(6)]
        xg_in = [sig(f"xg_in{j}") for j in range(2)]
        y_out = [sig(f"y_out{j}") for j in range(2)]
        cg_in = [sig(f"cg_in{n}", 32) for n in range(TILES)]
        comb_ready = sig("comb_ready", TILES, TILES)
        yt_done = sig("yt_done", TILES)
        x2_ready = sig("x2_ready", TILES, 1)
        fin_ready = sig("fin_ready")
        fin_t = sig("fin_t")
        fin_out = sig("fin_out")
        fin_saved = sig("fin_saved")

        block = ctx.enter_context(nc.Block())

        def passes(pe, out, st_hi, st_lo, mv_hi, mv_lo, first, last):
            for n, (st, mv) in enumerate(((st_hi, mv_hi), (st_hi, mv_lo), (st_lo, mv_hi))):
                ins = pe.matmul(out, st, mv, start=first and n == 0, stop=last and n == 2)
            return ins

        def passes640(pe, pair, st_hi, st_lo, mv_hi, mv_lo, first, last):
            for n, (st, mv) in enumerate(((st_hi, mv_hi), (st_hi, mv_lo), (st_lo, mv_hi))):
                for a, b in SEG:
                    ins = pe.matmul(pr(pair)[:, a:b], st, mv[:, a:b], start=first and n == 0, stop=last and n == 2)
            return ins

        def ran_before(eng):
            b, ran = (eng.value_load(loopi[0:1, n:n + 1], min_val=0, max_val=LAYERS * (PAIRS + 1)) for n in (0, 2))
            return b, ran, b + ran + 1

        def pairs_now(eng):
            return eng.value_load(loopi[0:1, 1:2], min_val=0, max_val=PAIRS)

        ORDER = (1, 2, 3, 4, 0)
        HEADS_ALL = TILES * HDS

        def head(g):
            if not 0 <= g < HEADS_ALL:
                return None
            ti, hd = divmod(g, HDS)
            return ti, ORDER[ti], hd, ((2 * hd, 2 * hd + 1) if hd < 4 else (hd + 4,))

        def keytile(tile):
            return tile if tile else 5

        @block.sync
        def _(sp):
            for dst, src in ((ident, t["k_ident"]),
                             (bandf, t["k_band"]), (crow[0:KC, :], t["c_ctx"].rearrange("(k p) -> k p", p=P)),
                             (crow[KC:2 * KC, :], t["c"].rearrange("b (k p) -> (b k) p", p=P)),
                             (crow[2 * KC:3 * KC, :], t["final_norm_g"].rearrange("(k p) -> k p", p=P)),
                             (xtok[:, 0, :], t["x_prompt"].rearrange("b s d -> (b s) d")),
                             (xtok[:, 1:TILES, :], t["x_sample"].rearrange("b (t p) d -> p (b t) d", p=P))):
                sp.dma_start(dst[:] if not isinstance(dst, bass.AP) else dst, src).then_inc(consts_in.sem, 16)
            with sp.Fori(0, LAYERS) as l:
                def free(v):
                    sp.wait_ge(*w_lo(l, v - 1))

                def wcols(w, off, n=256):
                    return w[ds(l, 1), :, off:off + n].rearrange("o (k p) n -> p (o k) n", p=P)

                def ada_load(u, j):
                    sp.dma_start(awf[j].rearrange("p (k n) -> p k n", k=KC),
                                 t["w_ada"][ds(l, 1), :, ds(u * 256, 256)]
                                 .rearrange("o (k p) n -> p (o k) n", p=P)).then_inc(a_in[j].sem, 16)

                sp.wait_ge(*comb_ready(l, 1 - TILES))
                for j in range(ADA_SLOTS):
                    ada_load(j, j)
                sp.wait_ge(*x2_ready(l, 0))
                small = [
                    (prow[PC_ADA:PC_G1, :], t["b_ada"][ds(l, 1), :].rearrange("o (k p) -> (o k) p", p=P)),
                    (prow[PC_G1:PC_G2, :], t["norm1_g"][ds(l, 1), :].rearrange("o (k p) -> (o k) p", p=P)),
                    (prow[PC_G2:PC_BG, :], t["norm2_g"][ds(l, 1), :].rearrange("o (k p) -> (o k) p", p=P)),
                    (prow[PC_BG:PC_CB, :], t["b_gate"][ds(l, 1), :].rearrange("o (k p) -> (o k) p", p=P)),
                    (prow[PC_CB:PC_LG, :], t["d_conv_b"][ds(l, 1), :].rearrange("o (k p) -> (o k) p", p=P)),
                    (prow[PC_LG:PC_LB, :], t["d_ln_g"][ds(l, 1), :].rearrange("o (k p) -> (o k) p", p=P)),
                    (prow[PC_LB:PC_N, :], t["d_ln_b"][ds(l, 1), :].rearrange("o (k p) -> (o k) p", p=P)),
                    (cwrow[:, :], t["d_conv_w"][ds(l, 1)].rearrange("o k c -> (o k) c")),
                    (rprow[:, :], t["b_rpb"][ds(l, 1)].rearrange("o h r c -> (o h r) c")),
                    (rowg[:, 0:64], t["a_subln_g"][ds(l, 1), :].partition_broadcast(P)),
                    (rowg[:, 64:320], t["c_q_norm_g"][ds(l, 1), :].partition_broadcast(P)),
                    (rowg[:, 320:448], t["c_kv_norm_g"][ds(l, 1), :].partition_broadcast(P)),
                    (lamv[:, :, :], t["a_lambda"][ds(l, 1)].partition_broadcast(P)),
                    (lamc[:, :], t["k_lam"][ds(l, 1), :].partition_broadcast(P)),
                    (wuf[:, 0:512].rearrange("p (k n) -> p k n", k=2),
                     t["c_wuq"][ds(l, 1)].rearrange("o (k p) n -> p (o k) n", p=P)),
                    (wuf[:, 512:896], t["c_wukv"][ds(l, 1)].rearrange("o p n -> (o p) n")),
                    (rbias[0:4, :], t["moe_b_group"][ds(l, 1), :].rearrange("o n -> n o")),
                    (rbias[4:20, :], t["moe_b_expert"][ds(l, 1), :].rearrange("o n -> n o")),
                    (wr[:, :, 0:4], t["moe_w_group"][ds(l, 1)].rearrange("o (k p) n -> p (o k) n", p=P)),
                    (wr[:, :, 4:20], t["moe_w_expert"][ds(l, 1)].rearrange("o (k p) n -> p (o k) n", p=P)),
                ]
                small.append((maskb, t["k_mask"]))
                for dst, src in small:
                    sp.dma_start(dst, src).then_inc(params_in.sem, 16)
                with sp.Fori(0, ADA_UNITS // ADA_SLOTS - 1) as i:
                    for j in range(ADA_SLOTS):
                        sp.wait_ge(started.sem, 1)
                        sp.wait_ge(*a_lo(l, i * ADA_SLOTS + (j + 1)))
                        sp.wait_ge(*a_lo_dve(l, i * ADA_SLOTS + (j + 1)))
                        ada_load(i * ADA_SLOTS + (ADA_SLOTS + j), j)
                for u in range(IN_UNITS):
                    off = C_DU + 256 * u if u < 2 else 256 * (u - 2)
                    n = 256 if u < IN_UNITS - 1 else 160
                    free(V_IN + u)
                    if u == 0:
                        sp.dma_start(tie[:, :], t["k_tie"]).then_inc(cache_in.sem, 16)
                        sp.wait_ge(*ada_used(l, ADA_UNITS - 1))
                        sp.dma_start(cosb[:, :, :], t["k_cos"]).then_inc(cache_in.sem, 16)
                    if u == 2:
                        sp.dma_start(sinb[:, :, :], t["k_sin"]).then_inc(cache_in.sem, 16)
                    sp.dma_start(wf[u % 2][:, 0:KC * n].rearrange("p (k n) -> p k n", k=KC),
                                 wcols(t["w_in"], off, n)).then_inc(w_in[u % 2].sem, 16)
                sp.wait_ge(*z_split(l, 1))
                for c, (name, w) in enumerate((("cache_a_k", 256), ("cache_b_k", 256), ("cache_a_v", 256),
                                               ("cache_b_v", 256), ("cache_c_kv", 128), ("cache_c_krope", 32))):
                    src = t[name][:, ds(l, 1)]
                    src = src.rearrange("b o s h d -> (b o s) (h d)" if c < 4 else "b o s d -> (b o s) d")
                    off = 256 * c if c < 4 else (1024 if c == 4 else 1152)
                    sp.dma_start(cache[:, off:off + w], src).then_inc(cache_in.sem, 16)
                sp.wait_ge(*cn_ready(l, 1))
                for name, a, n in (("new_a_k", 256, 256), ("new_a_v", C_AV, 256), ("new_b_k", 1024, 256),
                                   ("new_b_v", C_BV, 256), ("new_c_krope", C_CKR, 32)):
                    dst = t[name][:, ds(l, 1)]
                    dst = dst.rearrange("b o s h d -> (b o s) (h d)" if n == 256 else "b o s d -> (b o s) d")
                    sp.dma_start(dst, proj[:, 0, a:a + n]).then_inc(own_out.sem, 16)
                sp.dma_start(t["new_c_kv"][:, ds(l, 1)].rearrange("b o s d -> (b o s) d"), proj[:, 0, C_CKV:C_CKR]
                             ).then_inc(own_out.sem, 16)
                def fill(c, n):
                    sp.dma_start(t["y_rows"][P * c:P * (c + n), :].rearrange("(t p) d -> p t d", p=P),
                                 xT[:, :, :].rearrange("p k n -> p (k n)")[:, 0:n * D].rearrange("p (t d) -> p t d", t=n)
                                 ).then_inc(filled.sem, 16)

                for c in range(0, CHUNKS - 1, TILES):
                    fill(c, min(TILES, CHUNKS - 1 - c))
                def wo_load(name, dst, done):
                    sp.dma_start(dst.rearrange("p (k n) -> p k n", k=2),
                                 t[name][ds(l, 1)].rearrange("o (k p) n -> p (o k) n", p=P)).then_inc(done.sem, 16)

                for b, name in enumerate(("a_wo", "b_wo")):
                    free(V_WO + b)
                    wo_load(name, wf[b][:, :], w_in[b])
                sp.wait_ge(*c_ready(l, 6))
                wo_load("c_wo", wox[0], x_in[0])
                sp.wait_ge(*up_done(l, 6))
                sp.dma_start(rk, t["k_route"]).then_inc(route_in.sem, 16)
                sp.wait_ge(*mx_ready(l, (TILES - 1) * MAPS))
                wo_load("d_wo", wox[1], x_in[1])
                sp.wait_ge(*wo_lo(l, 2))
                fill(CHUNKS - 1, 1)
                with sp.Fori(0, KC // 2) as d2:
                    for b in range(4):
                        sp.wait_ge(*w_lo(l, d2 * 4 + (V_GATE + b - 1)))
                        sp.dma_start(wf[b % 2][:, :].rearrange("p (k n) -> p k n", k=KC),
                                     t["w_gate"][ds(l, 1), :, ds(d2 * 256 + b * D, 256)]
                                     .rearrange("o (k p) n -> p (o k) n", p=P)).then_inc(w_in[b % 2].sem, 16)
                with sp.Fori(0, 2) as i:
                    for j in range(2):
                        sp.wait_ge(*w_lo(l, i * 2 + (V_OUT + j - 1)))
                        sp.dma_start(wf[j][:, :].rearrange("p (k n) -> p k n", k=KC),
                                     t["w_out"][ds(l, 1), :, ds(i * 512 + j * 256, 256)]
                                     .rearrange("o (k p) n -> p (o k) n", p=P)).then_inc(w_in[j].sem, 16)
                sp.wait_ge(started.sem, 1)
                sp.wait_ge(*base_ready(l, 1))
                b, ran, done = ran_before(sp)

                def load(e, j, q):
                    if q < 2:
                        src = t["moe_w1"][ds(l, 1), e, 512 * q:512 * (q + 1), :]
                        dst = mwf[3 * j + q].rearrange("p (k n) -> p k n", k=4)
                    else:
                        src = t["moe_w2"][ds(l, 1), e, :, :]
                        dst = mwf[3 * j + q].rearrange("p (k n) -> p k n", k=2)
                    sp.dma_start(dst, src.rearrange("o e (k p) n -> p (o e k) n", p=P)).then_inc(m_in[3 * j + q].sem, 16)

                sp.wait_ge(*w_lo(l, V_ALL))
                sp.wait_ge(*y_done(l, 8))
                for j in range(2):
                    for q in range(3):
                        load(slice(j, j + 1), j, q)
                sp.wait_ge(*htk_ready(l, KC))
                sp.dma_start(t["h2_rows"].rearrange("(t p) d -> p t d", p=P), htok[:, :, :]).then_inc(rows_out.sem, 16)
                sp.wait_ge(started.sem, 1)
                sp.wait_ge(*route_ready(l, 1))
                m = pairs_now(sp)
                with sp.Fori(0, m) as i:
                    for j in range(2):
                        e = sp.value_load(cexp[0:1, ds(i * 2 + (2 + j), 1)], min_val=0, max_val=EXPERTS - 1)
                        for q in range(3):
                            if q < 2:
                                sp.wait_ge(mw_lo.sem, b * 4 + (i * 4 + (2 * j + q + 1)))
                            else:
                                sp.wait_ge(mw_lo2.sem, b * 2 + (i * 2 + (j + 1)))
                            load(ds(e, 1), j, q)

            sp.wait_ge(*own_out(LAYERS - 1, 6 * 16))
            for n, (name, a, b) in enumerate((("y_prompt", 0, 1), ("y_sample", 1, TILES))):
                sp.wait_ge(*fin_out(0, KC))
                dst = t[name].rearrange("b (t p) d -> p (b t) d", p=P)
                sp.dma_start(dst, ytok[:, a:b, :]).then_inc(fin_saved.sem, 16)
            sp.wait_ge(*fin_saved(0, 32))

        @block.tensor
        def _(pe):
            pe.wait_ge(*consts_in(0, 7 * 16))
            for tile in range(TILES):
                if tile == 4:
                    pe.wait_ge(*x_even(0, 1))
                for k in range(KC):
                    ins = pe.transpose(PS[:, tile % 4, k * P:(k + 1) * P], xtok[:, tile, k * P:(k + 1) * P], ident[:, :])
                ins.then_inc(xt_done.sem, 1)
            pe.wait_ge(*x_odd(0, 1))
            pe.transpose(PS[:, 1, 0:3 * KC], crow[:, :], ident[0:3 * KC, 0:3 * KC]).then_inc(cond_t.sem, 1)
            pe.wait_ge(*set_ready(0, 2))
            pe.wait_ge(*cond_ready(0, 1))

            def sum_up(l, n, k):
                pe.wait_ge(*sq_ready(l, KC * n + k + 1))
                for a, b in SEG:
                    ins = pe.matmul(pr(2)[:, a:b], ones[:, :], (xsq if n else xsq1)[:, k % 2, a:b], start=k == 0,
                                    stop=k == KC - 1)
                ins.then_inc(sq_used.sem, 1)

            with pe.Fori(0, LAYERS) as l:
                pe.wait_ge(*x2_ready(l, 0))

                def adaln(u, j):
                    pe.wait_ge(*a_lo(l, u + 1))
                    pe.wait_ge(*a_lo_dve(l, u + 1))
                    for c in range(2):
                        for k in range(KC):
                            w = slice(k * 256 + c * P, k * 256 + (c + 1) * P)
                            o = 512 + 4 * u + 2 * c
                            out = PS[:, 3, o:o + 2] if isinstance(u, int) else PS[:, 3, ds(u * 4 + (512 + 2 * c), 2)]
                            ins = passes(pe, out, awhi[j % 2][:, w], awlo[j % 2][:, w], schi[:, k, :], sclo[:, k, :],
                                         k == 0, k == KC - 1)
                    ins.then_inc(ada_used.sem, 1)

                for j in range(ADA_SLOTS):
                    adaln(j, j)
                for k in range(KC):
                    sum_up(l, 0, k)
                pe.wait_ge(*params_in(l, 21 * 16))
                pe.transpose(bank(6)[:, 0:PC_N], prow[:, :], ident[0:PC_N, 0:PC_N])
                for c in range(2):
                    pe.transpose(bank(6)[:, 104 + 32 * c:104 + 32 * c + CONV_K], cwrow[:, c * P:(c + 1) * P],
                                 ident[0:CONV_K, 0:CONV_K])
                pe.transpose(bank(6)[0:31, 168:228], rprow[:, :], ident[0:60, 0:60]).then_inc(par_t.sem, 1)
                pe.wait_ge(*rp_ready(l, 1))
                for g in range(8):
                    if g >= 4:
                        pe.wait_ge(*bias_ready(l, g - 3))
                    for kl in range(8):
                        kc = 8 * g + kl
                        for part in range(3):
                            ins = pe.matmul(bank(g % 4)[:, kl * 60:(kl + 1) * 60], band[:, 79 - kc:207 - kc],
                                            rp[:, part, :], start=part == 0, stop=part == 2)
                    ins.then_inc(band_done.sem, 1)
                with pe.Fori(0, ADA_UNITS // ADA_SLOTS - 1) as i:
                    for j in range(ADA_SLOTS):
                        adaln(i * ADA_SLOTS + (ADA_SLOTS + j), j)
                for u in range(2):
                    pe.wait_ge(*w_lo(l, V_IN + u + 1))
                    for c in range(2):
                        for k in range(KC):
                            if u == 0 and c == 0:
                                pe.wait_ge(*h_ready(l, k + 1))
                            w = slice(k * 256 + c * P, k * 256 + (c + 1) * P)
                            ins = passes640(pe, 2 * u + c, whi[u][:, w], wlo[u][:, w], hhi[:, k, :], hlo[:, k, :],
                                            k == 0, k == KC - 1)
                        ins.then_inc(du_done.sem, 1)
                for u in range(2, IN_UNITS):
                    n = 256 if u < IN_UNITS - 1 else 160
                    pe.wait_ge(*w_lo(l, V_IN + u + 1))
                    for tile in range(TILES):
                        g = (u - 2) * TILES + tile
                        if g == LN_MEAN:
                            pe.wait_ge(*proj_ready(l, g - 2))
                            pe.wait_ge(*cv_ready(l, 1))
                            for (a, b), z0 in zip(SEG, (0, CTX + PAD)):
                                for c in range(2):
                                    ins = pe.matmul(pr(0)[:, a:b], ones[:, :], zacc[:, c, z0:z0 + b - a],
                                                    start=c == 0, stop=c == 1)
                            ins.then_inc(mu_done.sem, 1)
                        if g == LN_VAR:
                            for c in range(2):
                                pe.wait_ge(*zsq_ready(l, c + 1))
                                for a, b in SEG:
                                    ins = pe.matmul(pr(1)[:, a:b], ones[:, :], zsg[:, c, a:b], start=c == 0, stop=c == 1)
                            ins.then_inc(zv_done.sem, 1)
                        if g < 8:
                            pe.wait_ge(*z_ready(l, 2))
                        elif g == LN_VAR:
                            pe.wait_ge(*zc_ready(l, 1))
                        elif g == LN_VAR + 2:
                            pe.wait_ge(*zvar_ready(l, 1))
                        else:
                            pe.wait_ge(*proj_ready(l, g - 7))
                        for k in range(KC):
                            ins = passes(pe, bank(g % 8, n), hhi[:, k, tile * P:(tile + 1) * P],
                                         hlo[:, k, tile * P:(tile + 1) * P], whi[u % 2][:, k * n:(k + 1) * n],
                                         wlo[u % 2][:, k * n:(k + 1) * n], k == 0, k == KC - 1)
                        ins.then_inc(proj_done.sem, 1)
                pe.wait_ge(*wu_ready(l, 1))
                pe.wait_ge(*cache_in(l, 9 * 16))
                pe.wait_ge(*proj_ready(l, 40))
                for n in range(TILES + 2):
                    own = n < TILES
                    if n <= TILES:
                        pe.wait_ge(*cn_ready(l, n + 1))
                        if n:
                            pe.wait_ge(*cT_ready(l, n))
                        for c in range(0 if own else 2, 3):
                            src = cn[:, c * P:(c + 1) * P] if own else cache[:, 1024:1152]
                            ins = pe.transpose(bank(0)[:, c * P:(c + 1) * P], src, ident[:, :])
                        ins.then_inc(cn_t.sem, 1)
                        src = cache[:, 0:512] if not own else (roped if n else proj[:, 0, 0:512])
                        if own and n:
                            pe.wait_ge(*roped_ready(l, n))
                        if n >= 2:
                            pe.wait_ge(*ab_ready(l, 2 * n - 3))
                        for c in range(4):
                            ins = pe.transpose(bank(4 + 2 * (n % 2))[:, c * P:(c + 1) * P], src[:, c * P:(c + 1) * P],
                                               ident[:, :])
                        ins.then_inc(ab_t.sem, 1)
                    if own:
                        if n >= 2:
                            pe.wait_ge(*ab_ready(l, 2 * n - 2))
                        for c in range(4):
                            ins = pe.transpose(bank(5 + 2 * (n % 2))[:, c * P:(c + 1) * P],
                                               proj[:, n, C_BQ + c * P:C_BQ + (c + 1) * P], ident[:, :])
                        ins.then_inc(ab_t.sem, 1)
                    if n:
                        pe.wait_ge(*qkc_ready(l, n))
                        if n >= 2:
                            pe.wait_ge(*c_ready(l, n - 1))
                        for c in range(0 if n <= TILES else 2, 4):
                            ins = pe.transpose(bank(3)[:, c * P:(c + 1) * P], qkc[:, c * P:(c + 1) * P], ident[:, :])
                        ins.then_inc(c_t.sem, 1)
                    if n <= TILES:
                        pe.wait_ge(*cT_ready(l, n + 1))
                        if n:
                            pe.wait_ge(*up_free(l, n))
                        if own:
                            for c in range(2):
                                passes(pe, bank(1, 256), cThi[:, c * P:(c + 1) * P], cTlo[:, c * P:(c + 1) * P],
                                       wuhi[:, c * 256:(c + 1) * 256], wulo[:, c * 256:(c + 1) * 256], c == 0, c == 1)
                        passes(pe, bank(2, 384), cThi[:, 256:384], cTlo[:, 256:384], wuhi[:, 512:896], wulo[:, 512:896],
                               True, True).then_inc(up_done.sem, 1)
                pe.wait_ge(*ab_ready(l, 11))
                pe.wait_ge(*c_ready(l, 6))
                pe.wait_ge(*v_ready(l, 1))

                def score(ti, tile, m):
                    if ti or m >= 2:
                        pe.wait_ge(*ex_ready(l, ti * MAPS + m - 1))
                    if m < 8:
                        lo, n, c = 32 * (m % 4), 32, m // 4
                    else:
                        lo, n, c = 64 * (m % 2), 64, (m - 8) // 2 + 2
                    q = (slice(lo, lo + n), c, slice(tile * P, (tile + 1) * P))
                    for a, b in SEG if tile else SEG[:1]:
                        k = (slice(lo, lo + n), c, slice(a, b) if tile else slice(TOK, TOK + P))
                        ins = passes(pe, pr(m % 2)[:, a:b], qThi[q], qTlo[q], kThi[k], kTlo[k], True, True)
                    ins.then_inc(s_done.sem, 1)

                def turn(ti, tile, hd):
                    if hd < 4:
                        pe.wait_ge(*mix_ready(l, ti * 4 + hd + 1))
                        src = wmix[:, hd % 2, :]
                    else:
                        pe.wait_ge(*ex_ready(l, ti * MAPS + hd + 5))
                        src = ex[:, hd % 4, :]
                    pe.wait_ge(*pt_ready(l, ti * HDS + hd))
                    if ti and hd == 2:
                        pe.wait_ge(*ot_ready(l, ti))
                    for c in range(TILES if tile else 1):
                        ins = pe.transpose(pr(2)[:, c * P:(c + 1) * P], src[:, c * P:(c + 1) * P], ident[:, :])
                    ins.then_inc(pt_done.sem, 1)

                def values(ti, tile, hd):
                    pe.wait_ge(*pt_ready(l, ti * HDS + hd + 1))
                    if ti or hd >= 2:
                        pe.wait_ge(*o_ready(l, ti * HDS + hd - 1))
                    kts = range(TILES) if tile else (5,)
                    for c, kt in enumerate(kts):
                        ins = passes(pe, bank(6 + hd % 2, 64), pthi[:, hd % 2, c * P:(c + 1) * P],
                                     ptlo[:, hd % 2, c * P:(c + 1) * P], vhi[:, kt, hd * 64:(hd + 1) * 64],
                                     vlo[:, kt, hd * 64:(hd + 1) * 64], c == 0, c == len(kts) - 1)
                    ins.then_inc(pv_done.sem, 1)

                for g in range(-1, HEADS_ALL + 4):
                    if head(g + 1):
                        for m in head(g + 1)[3]:
                            score(*head(g + 1)[:2], m)
                    if head(g - 4) and head(g - 4)[2] == HDS - 1:
                        ti = head(g - 4)[0]
                        pe.wait_ge(*o_ready(l, (ti + 1) * HDS))
                        pe.wait_ge(*on_ready(l, ti + 1))
                        pe.wait_ge(*pt_ready(l, min(g - 1, HEADS_ALL)))
                        for c in range(6):
                            ins = pe.transpose(PS[:, 2, c * P:(c + 1) * P], otok[:, ti % 2, c * P:(c + 1) * P], ident[:, :])
                        ins.then_inc(ot_done.sem, 1)
                    if head(g - 1):
                        turn(*head(g - 1)[:3])
                    if head(g - 2):
                        values(*head(g - 2)[:3])
                with pe.Fori(0, KC // 2) as d2:
                    pe.wait_ge(*ot_ready(l, TILES))
                    pe.wait_ge(*z_split(l, 1))
                    pe.wait_ge(*wo_lo(l, WO_UNITS))
                    pe.wait_ge(*x_lo(l, 2))
                    for b in range(4):
                        pe.wait_ge(*w_lo(l, d2 * 4 + (V_GATE + b + 1)))
                        bhi = [oThi[:, 2 * b + k, :] if b < 3 else zhi[:, k, :] for k in range(2)]
                        blo = [oTlo[:, 2 * b + k, :] if b < 3 else zlo[:, k, :] for k in range(2)]
                        for c in range(2):
                            pe.wait_ge(*m_used(l, d2 * 8 + (2 * b + c - 1)))
                            for k in range(2):
                                w = ds(d2 * 256 + c * P, P)
                                ins = passes640(pe, 2 + c, wohi[:, b, k, w], wolo[:, b, k, w], bhi[k], blo[k],
                                                k == 0, k == 1)
                            ins.then_inc(b_done.sem, 1)
                            pe.wait_ge(*g_ready(l, d2 * 8 + (2 * b + c - 1)))
                            for k in range(KC):
                                w = slice(k * 256 + c * P, k * 256 + (c + 1) * P)
                                ins = passes640(pe, c, whi[b % 2][:, w], wlo[b % 2][:, w], hhi[:, k, :], hlo[:, k, :],
                                                k == 0, k == KC - 1)
                            ins.then_inc(g_done.sem, 1)
                pe.wait_ge(*m_split(l, KC))
                for u in range(OUT_UNITS):
                    pe.wait_ge(*w_lo(l, V_OUT + u + 1))
                    for c in range(2):
                        d = 2 * u + c
                        pe.wait_ge(*x1_ready(l, d - 1))
                        for k in range(KC):
                            w = slice(k * 256 + c * P, k * 256 + (c + 1) * P)
                            ins = passes640(pe, c, whi[u % 2][:, w], wlo[u % 2][:, w], mhi[:, k, :], mlo[:, k, :],
                                            k == 0, k == KC - 1)
                        ins.then_inc(y_done.sem, 1)
                        if d:
                            sum_up(l, 1, d - 1)
                sum_up(l, 1, KC - 1)
                for k in range(KC):
                    pe.wait_ge(*hf_ready(l, KC + k + 1))
                    for a, b in SEG:
                        ins = pe.matmul(pr(3)[0:20, a:b], wr[:, k, :], hf[:, k % 2, a:b], start=k == 0, stop=k == KC - 1)
                    if k >= 2:
                        pe.wait_ge(*htk_ready(l, k - 1))
                    for tile in range(TILES):
                        ins = pe.transpose(pr(k % 2)[:, tile * P:(tile + 1) * P], hf[:, k % 2, tile * P:(tile + 1) * P],
                                           ident[:, :])
                    ins.then_inc(hf_used.sem, 1)
                pe.wait_ge(*lg_ready(l, 1))
                for tile in range(TILES):
                    ins = pe.matmul(bank(4)[:, tile * 20:(tile + 1) * 20], lgT[:, tile * P:(tile + 1) * P],
                                    ident[0:20, 0:20], start=True, stop=True)
                ins.then_inc(lgt_done.sem, 1)
                pe.wait_ge(*hot_ready(l, 1))
                pe.wait_ge(*route_in(l, 16))
                pe.matmul(bank(4)[:, 128:208], before, cum.rearrange("p t e -> p (t e)"), start=True, stop=True)
                pe.matmul(bank(4)[:, 256:336], ones[:, :], cum.rearrange("p t e -> p (t e)"), start=True, stop=True
                          ).then_inc(cnt_done.sem, 1)
                pe.wait_ge(*place_ready(l, 1))
                for n in range(10):
                    ins = pe.matmul(bank(5)[:, 0:CHUNKS + 2], rowhot[:, n, :], chhot[:, n, :], start=n == 0, stop=n == 9)
                ins.then_inc(list_done.sem, 1)
                pe.wait_ge(started.sem, 1)
                pe.wait_ge(*base_ready(l, 1))
                b, ran, done = ran_before(pe)
                pe.wait_ge(started.sem, 1)
                pe.wait_ge(*route_ready(l, 1))
                m = pairs_now(pe)

                def turn_rows(c, j, ci, first=False):
                    pe.wait_ge(xg_in[j].sem, (b if j else b + l) * 16 + (ci * 16 + 16))
                    if not first:
                        pe.wait_ge(hs_ready.sem, b * 2 + c)
                    for k in range(KC):
                        ins = pe.transpose(PS[:, 0, k * P:(k + 1) * P], xg[j][:, k * P:(k + 1) * P], ident[:, :])
                    ins.then_inc(ht_done.sem, 1)

                def gate_up(c, j, first=False):
                    pe.wait_ge(hs_ready.sem, b * 2 + (c + 1))
                    if not first:
                        pe.wait_ge(mact_ready.sem, done + (c - 1))
                    for k in range(KC):
                        if k % 4 == 0:
                            pe.wait_ge(mw_lo.sem, b * 4 + (c * 2 + (k // 4 + 1)))
                        w = slice((k % 4) * 512, (k % 4) * 512 + 512)
                        ins = passes(pe, bank(2 + j), hshi[j][:, k, :], hslo[j][:, k, :], mwhi[3 * j + k // 4][:, w],
                                     mwlo[3 * j + k // 4][:, w], k == 0, k == KC - 1)
                    ins.then_inc(mgu_done.sem, 1)

                def turn_act(c, j, first=False):
                    pe.wait_ge(mact_ready.sem, done + (c + 1))
                    if not first:
                        pe.wait_ge(at_ready.sem, done + (c - 1))
                    for k in range(2):
                        ins = pe.transpose(bank(4 + j)[:, k * P:(k + 1) * P], mact[j][:, k * P:(k + 1) * P], ident[:, :])
                    ins.then_inc(at_done.sem, 1)

                def down(c, j, first=False):
                    pe.wait_ge(at_ready.sem, done + (c + 1))
                    pe.wait_ge(mw_lo2.sem, b * 2 + (c + 1))
                    if not first:
                        pe.wait_ge(my_ready.sem, done + c)
                    for half in range(2):
                        for k in range(2):
                            w = slice(k * D + 512 * half, k * D + 512 * half + 512)
                            ins = passes(pe, bank(6 + half), athi[j][:, k, :], atlo[j][:, k, :], mwhi[3 * j + 2][:, w],
                                         mwlo[3 * j + 2][:, w], k == 0, k == 1)
                    ins.then_inc(my_done.sem, 1)

                turn_rows(0, 0, 0, True)
                gate_up(0, 0, True)
                turn_rows(1, 1, 0)
                turn_act(0, 0, True)
                with pe.Fori(0, m) as i:
                    for n in range(2):
                        c, j = i * 2 + (1 + n), 1 - n
                        gate_up(c, j)
                        turn_rows(i * 2 + (2 + n), n, i + 1)
                        down(i * 2 + n, n)
                        turn_act(c, j)
                down(m * 2, 0)
                for tile in range(TILES):
                    pe.wait_ge(*comb_ready(l, tile + 1))
                    if tile >= 2:
                        pe.wait_ge(*x2_ready(l, tile - 1))
                    for k in range(KC):
                        ins = pe.transpose(PS[:, tile % 2, k * P:(k + 1) * P], ybuf[tile % 2][:, k * P:(k + 1) * P],
                                           ident[:, :])
                    ins.then_inc(yt_done.sem, 1)
            pe.wait_ge(*x2_ready(LAYERS - 1, TILES))
            for k in range(KC):
                sum_up(LAYERS, 0, k)
            for k in range(KC):
                pe.wait_ge(*fin_ready(0, k + 1))
                if k >= 2:
                    pe.wait_ge(*fin_out(0, k - 1))
                for tile in range(TILES):
                    ins = pe.transpose(pr(k % 2)[:, tile * P:(tile + 1) * P], tmp[:, k % 2, tile * P:(tile + 1) * P],
                                       ident[:, :])
                ins.then_inc(fin_t.sem, 1)

        @block.scalar
        def _(act):
            for tile in (0, 2, 4):
                act.wait_ge(*xt_done(0, tile + 1))
                ins = act.copy(xT[:, :, tile * P:(tile + 1) * P], PS[:, tile % 4, :].rearrange("p (k n) -> p k n", k=KC))
                ins.then_inc(x_even.sem, 1)
            act.wait_ge(*cond_t(0, 1))
            act.activation(scf[:, :, :], PS[:, 1, 0:2 * KC].rearrange("p (s k) -> p k s", s=2), ACT.Silu
                           ).then_inc(cond_f.sem, 1)
            act.wait_ge(*cond_f(0, 1))
            act.copy(schi[:, :, :], scf[:, :, :]).then_inc(cond_f.sem, 1)
            act.wait_ge(*x_odd(0, 2))

            def square(l, n, k):
                if n:
                    act.wait_ge(*x1_ready(l, k + 1))
                if k >= 2:
                    act.wait_ge(*sq_used(l, KC * n + k - 1))
                act.activation((xsq if n else xsq1)[:, k % 2, :], xT[:, k, :], ACT.Square).then_inc(sq_ready.sem, 1)

            def stds(l, n):
                act.wait_ge(*var_ready(l, n + 1))
                act.activation(rsb[:, :], rsb[:, :], ACT.Sqrt).then_inc(std_ready.sem, 1)

            def modulate(l, n):
                for k in range(KC):
                    act.wait_ge(*tmp_ready(l, KC * n + k + 1))
                    if k >= 2:
                        act.wait_ge(*(hf_used if n else h_ready)(l, k - 1))
                    for s, (a, b) in enumerate(SEG):
                        ins = act.activation(hf[:, k % 2, a:b], tmp[:, k % 2, a:b], ACT.Identity,
                                             bias=ada[:, 24 * n + k, s:s + 1])
                    ins.then_inc(hf_ready.sem, 1)

            with act.Fori(0, LAYERS) as l:
                def high(v, j, dst=None, n=2048):
                    act.wait_ge(w_in[j].sem, l * (V_ALL // 2 * 16) + (v // 2 + 1) * 16)
                    act.copy(whi[j][:, 0:n] if dst is None else dst, wf[j][:, 0:n]).then_inc(w_hi.sem, 1)

                def high_at(i, v, j, step=2):
                    act.wait_ge(w_in[j].sem, l * (V_ALL // 2 * 16) + i * (8 * step) + (v // 2 + 1) * 16)
                    act.copy(whi[j][:, :], wf[j][:, :]).then_inc(w_hi.sem, 1)

                def ada_high(u, loaded, j):
                    act.wait_ge(*ada_used(l, u - 1))
                    act.wait_ge(*a_in[j](l, loaded))
                    act.copy(awhi[j % 2], awf[j]).then_inc(a_hi.sem, 1)

                for j in range(ADA_SLOTS):
                    ada_high(j, 16, j)
                act.wait_ge(*x2_ready(l, 0))
                for k in range(KC):
                    square(l, 0, k)
                stds(l, 0)
                act.wait_ge(*params_in(l, 21 * 16))
                act.copy(wuhi[:, :], wuf[:, :]).then_inc(wu_hi.sem, 1)
                act.wait_ge(*lam_sum(l, 1))
                act.activation(lamt[:, 66:68], lamt[:, 64:66], ACT.Exp).then_inc(lam_exp.sem, 1)
                with act.Fori(0, ADA_UNITS // ADA_SLOTS - 1) as i:
                    for j in range(ADA_SLOTS):
                        ada_high(i * ADA_SLOTS + (ADA_SLOTS + j), i * 16 + 32, j)
                act.wait_ge(*ada_ready(l, 1))
                for u in range(2):
                    high(V_IN + u, u)
                modulate(l, 0)
                act.wait_ge(*du_done(l, 2))
                high(V_IN + 2, 0)
                for c in range(2):
                    act.wait_ge(*du_done(l, 3 + c))
                    act.activation(zsg[:, c, :], pr(2 + c), ACT.Sigmoid).then_inc(sig_ready.sem, 1)
                high(V_IN + 3, 1)
                for u in range(2, IN_UNITS):
                    n = 256 if u < IN_UNITS - 1 else 160
                    for tile in range(TILES):
                        g = (u - 2) * TILES + tile
                        if g == LN_VAR - 1:
                            for c in range(2):
                                act.wait_ge(*zc_ready(l, c + 1))
                                act.activation(zsg[:, c, :], zc[:, c, :], ACT.Square).then_inc(zsq_ready.sem, 1)
                        if g == LN_VAR + 2:
                            act.wait_ge(*zvar_ready(l, 1))
                            act.activation(rsb[:, :], rsb[:, :], ACT.Sqrt).then_inc(zstd_ready.sem, 1)
                        if g == LN_VAR + 4:
                            for c in range(2):
                                act.wait_ge(*zn_ready(l, c + 1))
                                act.activation(zs[:, c, :], zc[:, c, :], ACT.Silu, bias=pcol[:, PC_LB + c:PC_LB + c + 1],
                                               scale=pcol[:, PC_LG + c:PC_LG + c + 1]).then_inc(zs_ready.sem, 1)
                        act.wait_ge(*proj_done(l, g + 1))
                        act.copy(proj[:, tile, 256 * (u - 2):256 * (u - 2) + n], bank(g % 8, n)
                                 ).then_inc(proj_ready.sem, 1)
                    if u + 2 < IN_UNITS:
                        high(V_IN + u + 2, u % 2, n=2048 if u + 2 < IN_UNITS - 1 else KC * 160)
                act.wait_ge(*cache_in(l, 9 * 16))
                act.wait_ge(*proj_ready(l, 40))
                for br, col in enumerate((C_AV, C_BV)):
                    act.copy(vhi[:, 1:5, 256 * br:256 * br + 256], proj[:, 1:5, col:col + 256])
                    act.copy(vhi[:, 5, 256 * br:256 * br + 256], proj[:, 0, col:col + 256])
                act.copy(vhi[:, 0, 0:512], cache[:, 512:1024]).then_inc(v_hi.sem, 1)
                act.wait_ge(*cv_var(l, 1))
                act.activation(cstat[:, 1, :], cstat[:, 0, :], ACT.Sqrt).then_inc(cv_std.sem, 1)
                SCALE = (32 ** -0.5, 64 ** -0.5, 64 ** -0.5)

                def cols(n):
                    kt = 0 if n == TILES else keytile(n)
                    return slice(kt * P, (kt + 1) * P)

                def turned(n, br, src, ready):
                    tk = slice(n * P, (n + 1) * P)
                    act.mul(qThi[:, 2 * br:2 * br + 2, tk], src[:, 0:256].rearrange("p (c n) -> p c n", c=2), SCALE[br])
                    act.copy(kThi[:, 2 * br:2 * br + 2, cols(n)], src[:, 256:512].rearrange("p (c n) -> p c n", c=2)
                             ).then_inc(ready.sem, 1)

                for n in range(TILES + 2):
                    own = n < TILES
                    if n <= TILES:
                        act.wait_ge(*cn_t(l, n + 1))
                        if n:
                            act.wait_ge(*up_done(l, n))
                        lo = 0 if own else 256
                        act.copy(cThi[:, lo:384], bank(0)[:, lo:384]).then_inc(cT_hi.sem, 1)
                    if own:
                        for br in range(2):
                            act.wait_ge(*ab_t(l, 2 * n + br + 1))
                            turned(n, br, bank(4 + br + 2 * (n % 2)), ab_hi)
                    elif n == TILES:
                        act.wait_ge(*ab_t(l, 11))
                        act.copy(kThi[:, 0:4, cols(n)], bank(6).rearrange("p (c n) -> p c n", c=4)
                                 ).then_inc(ab_hi.sem, 1)
                    if n:
                        act.wait_ge(*c_t(l, n))
                        if n <= TILES:
                            turned(n - 1, 2, bank(3), c_hi)
                        else:
                            act.copy(kThi[:, 4:6, cols(n - 1)], bank(3)[:, 256:512].rearrange("p (c n) -> p c n", c=2)
                                     ).then_inc(c_hi.sem, 1)
                    if n <= TILES:
                        act.wait_ge(*up_done(l, n + 1))
                        kt = keytile(n) if own else 0
                        kv = bank(2, 384).rearrange("p (h n) -> p h n", h=4)
                        if own:
                            act.copy(qkc[:, 0:256], bank(1, 256))
                        krope = proj[:, n, C_CKR:C_CKR + 32] if own else cache[:, 1152:1184]
                        qk = qkc[:, 256:512].rearrange("p (h n) -> p h n", h=4)
                        act.copy(qk[:, :, 0:32], kv[:, :, 0:32])
                        act.copy(qk[:, :, 32:64], krope.rearrange("p (o n) -> p o n", o=1).to_broadcast([P, 4, 32]))
                        act.copy(vhi[:, kt, 512:768].rearrange("p (h n) -> p h n", h=4), kv[:, :, 32:96]
                                 ).then_inc(qkc_raw.sem, 1)
                for g in range(0, HEADS_ALL + 4):
                    if head(g):
                        ti, tile, hd, ms = head(g)
                        nk = TOK if tile else P
                        for m in ms:
                            old = (m - 4) % MAPS
                            oti = ti - (m < 4)
                            if oti >= 0:
                                if old < 8:
                                    act.wait_ge(*mix_ready(l, oti * 4 + old // 2 + 1))
                                else:
                                    act.wait_ge(*pt_done(l, oti * HDS + old - 4 + 1))
                            act.wait_ge(*mx_ready(l, ti * MAPS + m + 1))
                            act.activation(ex[:, m % 4, 0:nk], pr(m % 2)[:, 0:nk], ACT.Exp,
                                           bias=stat[:, 0, m:m + 1], accum_out=stat[:, 1, m:m + 1]
                                           ).then_inc(ex_ready.sem, 1)
                    if head(g - 3):
                        ti, tile, hd, ms = head(g - 3)
                        act.wait_ge(*pv_done(l, g - 2))
                        act.wait_ge(*rec_ready(l, g - 2))
                        if ti >= 2 and hd == 0:
                            act.wait_ge(*ot_done(l, ti - 1))
                        act.mul(otok[:, ti % 2, hd * 64:(hd + 1) * 64], bank(6 + hd % 2, 64), stat[:, 2, ms[0]:ms[0] + 1]
                                ).then_inc(o_ready.sem, 1)
                    if head(g - 2) and head(g - 2)[2] == 6:
                        act.wait_ge(*ovar_ready(l, head(g - 2)[0] + 1))
                        act.activation(ostat[:, 1, :], ostat[:, 0, :], ACT.Sqrt).then_inc(ostd_ready.sem, 1)
                    if head(g - 4) and head(g - 4)[2] == HDS - 1:
                        ti, tile = head(g - 4)[:2]
                        act.wait_ge(*ot_done(l, ti + 1))
                        if ti == 0:
                            act.wait_ge(*own_out(l, 6 * 16))
                        act.copy(oThi[:, :, tile * P:(tile + 1) * P], PS[:, 2, 0:768].rearrange("p (c n) -> p c n", c=6)
                                 ).then_inc(ot_hi.sem, 1)
                    if head(g - 1):
                        ti, tile, hd, ms = head(g - 1)
                        nk = TOK if tile else P
                        act.wait_ge(*pt_done(l, g))
                        if g >= 3:
                            act.wait_ge(*pv_done(l, g - 2))
                        act.copy(pthi[:, hd % 2, 0:nk], pr(2)[:, 0:nk]).then_inc(pt_hi.sem, 1)
                for b in range(2):
                    high(V_WO + b, b, dst=wohi[:, b, :, :].rearrange("p k n -> p (k n)"))
                for b in range(2):
                    act.wait_ge(*x_in[b](l, 16))
                    act.copy(wohi[:, 2 + b, :, :].rearrange("p k n -> p (k n)"), wox[b]).then_inc(x_hi.sem, 1)
                for j in range(2):
                    high(V_GATE + j, j)
                with act.Fori(0, KC // 2) as d2:
                    for b in range(4):
                        for c in range(2):
                            act.wait_ge(*g_done(l, d2 * 8 + (2 * b + c + 1)))
                            act.wait_ge(*m_used(l, d2 * 8 + (2 * b + c - 1)))
                            act.activation(sg[:, c, :], pr(c), ACT.Sigmoid,
                                           bias=pcol[:, ds(d2 * 2 + (PC_BG + 8 * b + c), 1)]).then_inc(g_ready.sem, 1)
                        high_at(d2, V_GATE + 2 + b, b % 2, 4)
                    for c in range(2):
                        act.wait_ge(*m_ready(l, d2 * 2 + (c + 1)))
                        act.copy(mhi[:, ds(d2 * 2 + c, 1), :].rearrange("p o n -> p (o n)"), macc[:, c, :]
                                 ).then_inc(m_hi.sem, 1)
                for j in range(2):
                    act.wait_ge(*y_done(l, 2 * j + 2))
                    high(V_OUT + 2 + j, j)
                    for k in range(3 * j, 3 + 5 * j):
                        square(l, 1, k)
                stds(l, 1)
                modulate(l, 1)
                act.wait_ge(started.sem, 1)
                act.wait_ge(*base_ready(l, 1))
                b, ran, done = ran_before(act)

                def part_high(c, j, ci, q, first=False):
                    act.wait_ge(m_in[3 * j + q].sem, b * 16 + (ci * 16 + 16))
                    if not first:
                        act.wait_ge((my_done if q == 2 else mgu_done).sem, done + (c - 1))
                    act.copy(mwhi[3 * j + q], mwf[3 * j + q]).then_inc(mw_hi.sem, 1)

                for c in range(2):
                    for q in range(3):
                        part_high(c, c, 0, q, True)
                act.wait_ge(*rmax_ready(l, 1))
                act.activation(ex5[:, :, :], ex5[:, :, :], ACT.Exp).then_inc(rexp_ready.sem, 1)
                act.wait_ge(started.sem, 1)
                act.wait_ge(*route_ready(l, 1))
                m = pairs_now(act)

                def rows_high(c, j, first=False):
                    act.wait_ge(ht_done.sem, b * 2 + (c + 1))
                    if not first:
                        act.wait_ge(mgu_done.sem, done + (c - 1))
                    act.copy(hshi[j], PS[:, 0, :].rearrange("p (k n) -> p k n", k=KC)).then_inc(hs_hi.sem, 1)

                def silu(c, j, first=False):
                    act.wait_ge(mgu_done.sem, done + (c + 1))
                    if not first:
                        act.wait_ge(mact_ready.sem, done + (c - 1))
                    act.activation(msg[j], bank(2 + j, 256), ACT.Silu).then_inc(msilu_ready.sem, 1)

                def act_high(c, j, first=False):
                    act.wait_ge(at_done.sem, done + (c + 1))
                    if not first:
                        act.wait_ge(my_done.sem, done + (c - 1))
                    act.mul(athi[j], bank(4 + j, 256).rearrange("p (c n) -> p c n", c=2), A_SCALE
                            ).then_inc(at_hi.sem, 1)

                def rows_back(c, j, par, row):
                    act.wait_ge(my_done.sem, done + (c + 1))
                    if par is not None:
                        act.wait_ge(y_out[j].sem, par)
                    act.copy(ybuf[j], PS[:, 3, :]).then_inc(my_ready.sem, 1)
                    act.wait_ge(my_ready.sem, done + (c + 1))
                    act.dma_start(t["y_rows"][ds(row, P), :], ybuf[j]).then_inc(y_out[j].sem, 16)

                act.wait_ge(*filled(l, FILLS * 16))
                rows_high(0, 0, True)
                silu(0, 0, True)
                rows_high(1, 1, True)
                act_high(0, 0, True)
                with act.Fori(0, m) as i:
                    for n in range(2):
                        c, j = i * 2 + (1 + n), 1 - n
                        for q in range(2):
                            part_high(i * 2 + (2 + n), n, i + 1, q)
                        silu(c, j)
                        rows_high(i * 2 + (2 + n), n)
                        rows_back(i * 2 + n, n, (ran if n else b) * 16 + (i * 16 + 16), i * (2 * P) + n * P)
                        part_high(i * 2 + (2 + n), n, i + 1, 2)
                        act_high(c, j)
                rows_back(m * 2, 0, b * 16 + (m * 16 + 16), m * (2 * P))
            act.wait_ge(*x2_ready(LAYERS - 1, TILES))
            for k in range(KC):
                square(LAYERS, 0, k)
            stds(LAYERS, 0)
            for k in range(KC):
                act.wait_ge(*fin_t(0, k + 1))
                act.copy(ytok[:, :, k * P:(k + 1) * P], pr(k % 2).rearrange("p (t n) -> p t n", t=TILES)
                         ).then_inc(fin_out.sem, 1)

        @block.gpsimd
        def _(pool):
            with pool.Fori(0, LAYERS) as l:
                def low(count, j, dst=None, n=2048):
                    pool.wait_ge(w_hi.sem, count)
                    hi = (whi[j] if dst is None else dst[0])[:, 0:n]
                    lo = (wlo[j] if dst is None else dst[1])[:, 0:n]
                    pool.tensor_tensor(lo, wf[j][:, 0:n], hi, ALU.subtract).then_inc(w_lo.sem, 1)

                with pool.Fori(0, ADA_UNITS // ADA_SLOTS) as i:
                    for j in range(ADA_SLOTS):
                        pool.wait_ge(*a_hi(l, i * ADA_SLOTS + (j + 1)))
                        pool.tensor_tensor(awlo[j % 2][:, 0:ADA_POOL], awf[j][:, 0:ADA_POOL], awhi[j % 2][:, 0:ADA_POOL], ALU.subtract
                                           ).then_inc(a_lo.sem, 1)
                for u in range(IN_UNITS):
                    low(l * V_ALL + (V_IN + u + 1), u % 2, n=2048 if u < IN_UNITS - 1 else KC * 160)
                for n in range(1, TILES):
                    if n == 1:
                        pool.wait_ge(*proj_ready(l, 40))
                        pool.wait_ge(*cv_var(l, 1))
                    else:
                        pool.wait_ge(*ab_t(l, 2 * n - 1))
                    v = proj[:, n, 0:512].rearrange("p (h n) -> p h n", n=32)
                    r2 = rope2.rearrange("p (h n) -> p h n", n=32)
                    for o, i in ((0, 8), (8, 0), (16, 24), (24, 16)):
                        pool.tensor_tensor(r2[:, :, o:o + 8], v[:, :, i:i + 8],
                                           sinb[:, n - 1:n, o:o + 8].to_broadcast([P, 16, 8]), ALU.mult)
                    pool.drain()
                    pool.tensor_tensor(v, v, cosb[:, n - 1:n, :].to_broadcast([P, 16, 32]), ALU.mult)
                    pool.drain()
                    pool.tensor_tensor(roped.rearrange("p (h n) -> p h n", n=32), v, r2, ALU.add).then_inc(roped_ready.sem, 1)
                for b in range(WO_UNITS):
                    flat = [w[:, b, :, :].rearrange("p k n -> p (k n)") for w in (wohi, wolo)]
                    if b < 2:
                        low(l * V_ALL + (V_WO + b + 1), b, flat, 640)
                    else:
                        pool.wait_ge(*x_hi(l, b - 1))
                        pool.tensor_tensor(flat[1][:, 0:640], wox[b - 2][:, 0:640], flat[0][:, 0:640], ALU.subtract
                                           ).then_inc(x_lo.sem, 1)
                with pool.Fori(0, (V_ALL - V_GATE) // 2) as i:
                    for j in range(2):
                        low(l * V_ALL + i * 2 + (V_GATE + j + 1), j)
                pool.wait_ge(*base_ready(l, 1))
                pool.tensor_tensor(zero1[:, :], zero1[:, :], zero1[:, :], ALU.add)
                pool.drain()
                b, ran, done = ran_before(pool)

                def gather(c, j):
                    pool.tensor_tensor(idxi[:, j:j + 1], idxall[:, ds(c, 1)] if not isinstance(c, int) else
                                       idxall[:, c:c + 1], zero1[:, :], ALU.add)
                    pool.drain()
                    pool.indirect_dma_start(out=xg[j], out_offset=None, in_=t["h2_rows"],
                                            in_offset=bass.IndirectOffsetOnAxis(ap=idxi[:, j:j + 1], axis=0)
                                            ).then_inc(xg_in[j].sem, 16)

                def part_low(c, j):
                    pool.wait_ge(mw_hi.sem, b * 6 + (c * 3 + 3))
                    pool.tensor_tensor(mwlo[3 * j + 2], mwf[3 * j + 2], mwhi[3 * j + 2], ALU.subtract
                                       ).then_inc(mw_lo2.sem, 1)

                for c in range(2):
                    part_low(c, c)
                pool.wait_ge(*route_ready(l, 1))
                pool.tensor_tensor(zero1[:, :], zero1[:, :], zero1[:, :], ALU.add)
                pool.drain()
                m = pairs_now(pool)
                pool.wait_ge(*rows_out(l, 16))
                pool.tensor_tensor(zero1[:, :], zero1[:, :], zero1[:, :], ALU.add)
                pool.drain()
                for c in range(2):
                    gather(c, c)
                pool.wait_ge(ht_done.sem, b * 2 + 1)
                pool.tensor_tensor(zero1[:, :], zero1[:, :], zero1[:, :], ALU.add)
                pool.drain()
                gather(2, 0)
                with pool.Fori(0, m) as i:
                    for n in range(2):
                        pool.wait_ge(ht_done.sem, b * 2 + (i * 2 + (2 + n)))
                        pool.tensor_tensor(zero1[:, :], zero1[:, :], zero1[:, :], ALU.add)
                        pool.drain()
                        gather(i * 2 + (3 + n), 1 - n)
                        part_low(i * 2 + (2 + n), n)
                pool.wait_ge(hs_ready.sem, b * 2 + m * 2 + 2)
                pool.wait_ge(xg_in[0].sem, l * 16 + b * 16 + (m * 16 + 32))
                pool.wait_ge(y_out[0].sem, b * 16 + (m * 16 + 32))
                pool.wait_ge(y_out[1].sem, ran * 16 + (m * 16 + 16))
                pool.tensor_tensor(sloti[:, :], slotf[:, :], zero1[:, :].to_broadcast([P, 10]), ALU.add)
                pool.drain()
                for tile in range(TILES):
                    for ch, dst in enumerate((cga, cgb)):
                        n = ch * TILES + tile
                        pool.indirect_dma_start(out=dst[:, tile, :], out_offset=None, in_=t["y_rows"],
                                                in_offset=bass.IndirectOffsetOnAxis(ap=sloti[:, n:n + 1], axis=0)
                                                ).then_inc(cg_in[tile].sem, 16)

        @block.vector
        def _(dve):
            dve.memset(ones[:, :], 1.0).then_inc(set_ready.sem, 1)
            dve.wait_ge(*consts_in(0, 7 * 16))
            dve.tensor_copy(band[:, :], bandf[:, :]).then_inc(set_ready.sem, 1)
            for s in (w_lo, wo_lo, a_lo, a_lo_dve, pt_ready, ot_ready, mgu_done, msilu_ready, mact_ready, at_done, at_hi, at_ready,
                      my_done, my_ready):
                dve.nop().then_inc(s.sem, 1)
            for s in y_out:
                dve.nop().then_inc(s.sem, 16)
            dve.nop().then_inc(ada_used.sem, 2)
            dve.nop().then_inc(comb_ready.sem, TILES)
            dve.nop().then_inc(g_ready.sem, 2)
            dve.nop().then_inc(m_used.sem, 2)
            dve.nop().then_inc(x1_ready.sem, 2)
            dve.nop().then_inc(x2_ready.sem, 1)
            dve.nop().then_inc(started.sem, 1)
            dve.memset(zero1[:, :], 0).then_inc(set_ready.sem, 1)
            dve.memset(loopf[:, 0:1], 0.0)
            dve.memset(loopf[:, 1:2], -1.0)
            dve.memset(loopf[:, 2:3], 1.0)
            for tile in (1, 3):
                dve.wait_ge(*xt_done(0, tile + 1))
                dve.tensor_copy(xT[:, :, tile * P:(tile + 1) * P], PS[:, tile, :].rearrange("p (k n) -> p k n", k=KC)
                                ).then_inc(x_odd.sem, 1)
            dve.wait_ge(*cond_f(0, 2))
            dve.tensor_tensor(sclo[:, :, :], scf[:, :, :], schi[:, :, :], ALU.subtract)
            dve.tensor_copy(gfin[:, :], PS[:, 1, 2 * KC:3 * KC]).then_inc(cond_ready.sem, 1)

            def root(l, n):
                dve.wait_ge(*sq_used(l, KC * (n + 1)))
                dve.tensor_scalar(rsb[:, :], pr(2), 1.0 / D, EPS, ALU.mult, ALU.add).then_inc(var_ready.sem, 1)
                dve.wait_ge(*std_ready(l, n + 1))
                dve.reciprocal(rsb[:, :], rsb[:, :])
                dve.drain()

            def norm(l, n):

                def scaled(k):
                    if k >= 2:
                        dve.wait_ge(*hf_ready(l, KC * n + k - 1))
                    for s, (a, b) in enumerate(SEG):
                        ins = dve.scalar_tensor_tensor(out=tmp[:, k % 2, a:b], in0=xT[:, k, a:b],
                                                       scalar=gs[:, n, k, s:s + 1], in1=rsb[:, a:b],
                                                       op0=ALU.mult, op1=ALU.mult)
                    ins.then_inc(tmp_ready.sem, 1)

                scaled(0)
                for k in range(KC):
                    if k + 1 < KC:
                        scaled(k + 1)
                    if n:
                        dve.wait_ge(*hf_used(l, k + 1))
                        dve.tensor_copy(htok[:, :, k * P:(k + 1) * P], pr(k % 2).rearrange("p (t n) -> p t n", t=TILES)
                                        ).then_inc(htk_ready.sem, 1)
                        continue
                    dve.wait_ge(*hf_ready(l, KC * n + k + 1))
                    dve.tensor_copy(hhi[:, k, :], hf[:, k % 2, :])
                    dve.drain()
                    dve.tensor_tensor(hlo[:, k, :], hf[:, k % 2, :], hhi[:, k, :], ALU.subtract
                                      ).then_inc(h_ready.sem, 1)

            def bc(ap, shape):
                return ap.to_broadcast(shape)

            with dve.Fori(0, LAYERS) as l:
                dve.drain()
                dve.scalar_tensor_tensor(out=lamt[:, 70:71], in0=loopf[:, 0:1], scalar=1.0, in1=loopf[:, 1:2],
                                         op0=ALU.add, op1=ALU.add)
                dve.tensor_tensor(lamt[:, 71:72], loopf[:, 2:3], loopf[:, 1:2], ALU.add)
                dve.drain()
                dve.tensor_copy(loopf[:, 0:1], lamt[:, 70:71])
                dve.tensor_copy(loopf[:, 2:3], lamt[:, 71:72])
                dve.tensor_copy(loopi[:, 0:1], lamt[:, 70:71])
                dve.tensor_copy(loopi[:, 2:3], lamt[:, 71:72]).then_inc(base_ready.sem, 1)

                def ada_low(u, j):
                    dve.wait_ge(*a_hi(l, u + 1))
                    dve.tensor_tensor(awlo[j % 2][:, ADA_POOL:2048], awf[j][:, ADA_POOL:2048], awhi[j % 2][:, ADA_POOL:2048],
                                      ALU.subtract).then_inc(a_lo_dve.sem, 1)

                for j in range(ADA_SLOTS):
                    ada_low(j, j)
                root(l, 0)
                dve.wait_ge(*par_t(l, 1))
                dve.tensor_copy(pcol[:, :], bank(6)[:, 0:PC_N])
                dve.tensor_copy(cw[:, :, :], bank(6)[:, 104:168].rearrange("p (c n) -> p c n", c=2)[:, :, 0:CONV_K])
                dve.tensor_copy(rpf[:, :], bank(6)[0:31, 168:228])
                dve.drain()
                dve.tensor_copy(rp[:, 0, :], rpf[:, :])
                dve.drain()
                dve.tensor_tensor(rpd[:, :], rpf[:, :], rp[:, 0, :], ALU.subtract)
                dve.drain()
                dve.tensor_copy(rp[:, 1, :], rpd[:, :])
                dve.drain()
                dve.tensor_tensor(rpf[:, :], rpd[:, :], rp[:, 1, :], ALU.subtract)
                dve.drain()
                dve.tensor_copy(rp[:, 2, :], rpf[:, :]).then_inc(rp_ready.sem, 1)
                dve.wait_ge(*params_in(l, 21 * 16))
                dve.tensor_tensor(lamt[:, 0:64].rearrange("p (a n) -> p a n", a=2), lamv[:, 0:4:2, :], lamv[:, 1:4:2, :],
                                  ALU.mult)
                dve.drain()
                dve.tensor_reduce(lamt[:, 64:66], lamt[:, 0:64].rearrange("p (a n) -> p a n", a=2), AX_X, ALU.add
                                  ).then_inc(lam_sum.sem, 1)
                dve.tensor_scalar(rowg[:, 0:64], rowg[:, 0:64], lamc[:, 1:2], None, ALU.mult)
                dve.wait_ge(*wu_hi(l, 1))
                dve.tensor_tensor(wulo[:, :], wuf[:, :], wuhi[:, :], ALU.subtract).then_inc(wu_ready.sem, 1)
                dve.wait_ge(*lam_exp(l, 1))
                dve.tensor_tensor(lamt[:, 68:69], lamt[:, 67:68], lamt[:, 66:67], ALU.subtract)
                dve.drain()
                dve.tensor_tensor(lamt[:, 69:70], lamt[:, 68:69], lamc[:, 0:1], ALU.subtract)
                nlam = lamt[:, 69:70]
                for g in range(8):
                    dve.wait_ge(*band_done(l, g + 1))
                    for half in range(2):
                        ps = slice(64 * half, 64 * half + 64)
                        src = bank(g % 4, 480)[ps, :].rearrange("p (k h r) -> p h r k", k=8, h=4)
                        m = maskb[ps, 8 * g:8 * g + 8].rearrange("p (a b k) -> p a b k", a=1, b=1)
                        ins = dve.tensor_tensor(bias[ps, :, :, 8 * g:8 * g + 8], src[:, :, 1 - half:15 - half, :],
                                                bc(m, [64, 4, 14, 8]), ALU.add)
                    ins.then_inc(bias_ready.sem, 1)
                with dve.Fori(0, ADA_UNITS // ADA_SLOTS - 1) as i:
                    for j in range(ADA_SLOTS):
                        ada_low(i * ADA_SLOTS + (ADA_SLOTS + j), j)
                dve.wait_ge(*ada_used(l, ADA_UNITS))
                dve.tensor_tensor(ada[:, :, :], PS[:, 3, 512:608].rearrange("p (k s) -> p k s", s=2),
                                  bc(pcol[:, PC_ADA:PC_G1].rearrange("p (k o) -> p k o", o=1), [P, 48, 2]), ALU.add)
                dve.drain()
                for n, g in enumerate((PC_G1, PC_G2)):
                    ins = dve.scalar_tensor_tensor(out=gs[:, n, :, :], in0=ada[:, 24 * n + 8:24 * n + 16, :], scalar=1.0,
                                                   in1=bc(pcol[:, g:g + 8].rearrange("p (k o) -> p k o", o=1), [P, 8, 2]),
                                                   op0=ALU.add, op1=ALU.mult)
                ins.then_inc(ada_ready.sem, 1)
                dve.drain()
                norm(l, 0)
                dve.wait_ge(*sig_ready(l, 1))
                for a, b in ((0, PAD), (PAD + CTX, 2 * PAD + CTX), (2 * PAD + TOK, 3 * PAD + TOK)):
                    dve.memset(zpad[:, :, a:b], 0.0)
                for c in range(2):
                    dve.wait_ge(*sig_ready(l, c + 1))
                    for (a, b), z0 in zip(SEG, (PAD, 2 * PAD)):
                        ins = dve.tensor_tensor(zpad[:, c, z0 + a:z0 + b], pr(c)[:, a:b], zsg[:, c, a:b], ALU.mult)
                    ins.then_inc(z_ready.sem, 1)
                NZ = TOK + PAD
                for k in range(CONV_K):
                    dve.drain()
                    for c in range(2):
                        if k == 0:
                            dve.tensor_scalar(zacc[:, c, :], zpad[:, c, 0:NZ], cw[:, c, 0:1],
                                              pcol[:, PC_CB + c:PC_CB + c + 1], ALU.mult, ALU.add)
                        else:
                            ins = dve.scalar_tensor_tensor(out=zacc[:, c, :], in0=zpad[:, c, k:k + NZ],
                                                           scalar=cw[:, c, k:k + 1], in1=zacc[:, c, :],
                                                           op0=ALU.mult, op1=ALU.add)
                ins.then_inc(cv_ready.sem, 1)
                dve.wait_ge(*mu_done(l, 1))
                dve.tensor_scalar(rsb[:, :], pr(0), 1.0 / CONV_CH, None, ALU.mult)
                dve.drain()
                for c in range(2):
                    for (a, b), z0 in zip(SEG, (0, PAD)):
                        ins = dve.tensor_tensor(zc[:, c, a:b], zacc[:, c, z0 + a:z0 + b], rsb[:, a:b], ALU.subtract)
                    ins.then_inc(zc_ready.sem, 1)
                dve.drain()
                dve.wait_ge(*zv_done(l, 1))
                dve.tensor_scalar(rsb[:, :], pr(1), 1.0 / CONV_CH, EPS, ALU.mult, ALU.add).then_inc(zvar_ready.sem, 1)
                dve.wait_ge(*zstd_ready(l, 1))
                dve.reciprocal(rsb[:, :], rsb[:, :])
                dve.drain()
                for c in range(2):
                    dve.tensor_tensor(zc[:, c, :], zc[:, c, :], rsb[:, :], ALU.mult).then_inc(zn_ready.sem, 1)
                dve.drain()
                for c in range(2):
                    dve.wait_ge(*zs_ready(l, c + 1))
                    dve.tensor_copy(zhi[:, c, :], zs[:, c, :])
                dve.drain()
                ins = dve.tensor_tensor(zlo[:, :, :], zs[:, :, :], zhi[:, :, :], ALU.subtract).then_inc(z_split.sem, 1)
                dve.drain()
                dve.wait_ge(*proj_ready(l, 40))
                cq2 = csq[:, 0:1280].rearrange("p (t n) -> p t n", t=TILES)
                ck2 = csq[:, 1280:1920].rearrange("p (t n) -> p t n", t=TILES)
                dve.tensor_tensor(cq2, proj[:, :, C_CQ:C_CKV], proj[:, :, C_CQ:C_CKV], ALU.mult)
                dve.tensor_tensor(ck2, proj[:, :, C_CKV:C_CKR], proj[:, :, C_CKV:C_CKR], ALU.mult)
                dve.drain()
                dve.tensor_reduce(cstat[:, 2, 0:5], cq2, AX_X, ALU.add)
                dve.tensor_reduce(cstat[:, 2, 5:10], ck2, AX_X, ALU.add)
                dve.drain()
                dve.tensor_scalar(cstat[:, 0, 0:5], cstat[:, 2, 0:5], 1.0 / 256, EPS, ALU.mult, ALU.add)
                dve.tensor_scalar(cstat[:, 0, 5:10], cstat[:, 2, 5:10], 1.0 / 128, EPS, ALU.mult, ALU.add
                                  ).then_inc(cv_var.sem, 1)
                dve.wait_ge(*cv_std(l, 1))
                dve.reciprocal(cstat[:, 2, :], cstat[:, 1, :])
                dve.wait_ge(*v_hi(l, 1))
                for br, col in enumerate((C_AV, C_BV)):
                    w = slice(256 * br, 256 * br + 256)
                    dve.tensor_tensor(vlo[:, 1:5, w], proj[:, 1:5, col:col + 256], vhi[:, 1:5, w], ALU.subtract)
                    dve.tensor_tensor(vlo[:, 5, w], proj[:, 0, col:col + 256], vhi[:, 5, w], ALU.subtract)
                dve.tensor_tensor(vlo[:, 0, 0:512], cache[:, 512:1024], vhi[:, 0, 0:512], ALU.subtract
                                  ).then_inc(v_ready.sem, 1)
                SCALE = (32 ** -0.5, 64 ** -0.5, 64 ** -0.5)

                def rotate(v, tile):
                    c = cosb[:, tile - 1:tile, :]
                    r1 = rope1[:, 0:256].rearrange("p (h n) -> p h n", n=32)
                    r2 = rope1[:, 256:512].rearrange("p (h n) -> p h n", n=32)
                    dve.tensor_tensor(r1, v, bc(c, [P, 8, 32]), ALU.mult)
                    for half in range(2):
                        for a in range(2):
                            o = 16 * a + 8 * half
                            i = 16 * a + 8 * (1 - half)
                            dve.tensor_tensor(r2[:, :, o:o + 8], v[:, :, i:i + 8],
                                              bc(sinb[:, tile - 1:tile, o:o + 8], [P, 8, 8]), ALU.mult)
                    dve.drain()
                    return dve.tensor_tensor(v, r1, r2, ALU.add)

                def cols(n):
                    kt = 0 if n == TILES else keytile(n)
                    return slice(kt * P, (kt + 1) * P)

                def turned(n, br, src, ready):
                    tk = slice(n * P, (n + 1) * P)
                    b2 = slice(2 * br, 2 * br + 2)
                    dve.scalar_tensor_tensor(out=qTlo[:, b2, tk], in0=src[:, 0:256].rearrange("p (c n) -> p c n", c=2),
                                             scalar=SCALE[br], in1=qThi[:, b2, tk], op0=ALU.mult, op1=ALU.subtract)
                    dve.tensor_tensor(kTlo[:, b2, cols(n)], src[:, 256:512].rearrange("p (c n) -> p c n", c=2),
                                      kThi[:, b2, cols(n)], ALU.subtract).then_inc(ready.sem, 1)

                def normed(n):
                    if n:
                        dve.wait_ge(*cn_t(l, n))
                    for a, b, q, g in ((0, 256, n, 64), (256, 384, 5 + n, 320)):
                        ins = dve.scalar_tensor_tensor(out=cn[:, a:b], in0=proj[:, n, C_CQ + a:C_CQ + b],
                                                       scalar=cstat[:, 2, q:q + 1], in1=rowg[:, g:g + b - a],
                                                       op0=ALU.mult, op1=ALU.mult)
                    if n == 0:
                        dve.drain()
                        ins = dve.scalar_tensor_tensor(out=proj[:, 0, C_CKV:C_CKR], in0=proj[:, 0, C_CKV:C_CKR],
                                                       scalar=cstat[:, 2, 5:6], in1=rowg[:, 320:448],
                                                       op0=ALU.mult, op1=ALU.mult)
                    ins.then_inc(cn_ready.sem, 1)

                dve.drain()
                normed(0)
                for n in range(TILES + 2):
                    own = n < TILES
                    if n <= TILES:
                        dve.wait_ge(*cT_hi(l, n + 1))
                        lo = 0 if own else 256
                        dve.tensor_tensor(cTlo[:, lo:384], bank(0)[:, lo:384], cThi[:, lo:384], ALU.subtract
                                          ).then_inc(cT_ready.sem, 1)
                    if own:
                        for br in range(2):
                            dve.wait_ge(*ab_hi(l, 2 * n + br + 1))
                            turned(n, br, bank(4 + br + 2 * (n % 2)), ab_ready)
                    elif n == TILES:
                        dve.wait_ge(*ab_hi(l, 11))
                        dve.tensor_tensor(kTlo[:, 0:4, cols(n)], bank(6).rearrange("p (c n) -> p c n", c=4),
                                          kThi[:, 0:4, cols(n)], ALU.subtract).then_inc(ab_ready.sem, 1)
                    if n:
                        dve.wait_ge(*c_hi(l, n))
                        if n <= TILES:
                            turned(n - 1, 2, bank(3), c_ready)
                        else:
                            dve.tensor_tensor(kTlo[:, 4:6, cols(n - 1)], bank(3)[:, 256:512].rearrange("p (c n) -> p c n", c=2),
                                              kThi[:, 4:6, cols(n - 1)], ALU.subtract).then_inc(c_ready.sem, 1)
                    if n <= TILES:
                        dve.wait_ge(*qkc_raw(l, n + 1))
                        kt = keytile(n) if own else 0
                        dve.tensor_tensor(vlo[:, kt, 512:768].rearrange("p (h n) -> p h n", h=4),
                                          bank(2, 384).rearrange("p (h n) -> p h n", h=4)[:, :, 32:96],
                                          vhi[:, kt, 512:768].rearrange("p (h n) -> p h n", h=4), ALU.subtract
                                          ).then_inc(up_free.sem, 1)
                        if own and n:
                            v = qkc.rearrange("p (h n) -> p h n", h=8)[:, :, 32:64]
                            rotate(v, n).then_inc(qkc_ready.sem, 1)
                        else:
                            dve.nop().then_inc(qkc_ready.sem, 1)
                    if n + 1 < TILES:
                        normed(n + 1)
                    elif n + 1 == TILES:
                        dve.nop().then_inc(cn_ready.sem, 1)
                for g in range(-1, HEADS_ALL + 4):
                    if head(g - 2):
                        ti, tile, hd, ms = head(g - 2)
                        nk = TOK if tile else P
                        dve.wait_ge(*pt_hi(l, g - 1))
                        dve.tensor_tensor(ptlo[:, hd % 2, 0:nk], pr(2)[:, 0:nk], pthi[:, hd % 2, 0:nk], ALU.subtract
                                          ).then_inc(pt_ready.sem, 1)
                    if head(g + 1):
                        ti, tile, hd, ms = head(g + 1)
                        nk = TOK if tile else P
                        for m in ms:
                            dve.wait_ge(*s_done(l, ti * MAPS + m + 1))
                            if 8 <= m < 12 and tile:
                                s0 = 6 - 2 * (tile - 1)
                                dve.tensor_tensor(pr(m % 2)[:, CTX:TOK], pr(m % 2)[:, CTX:TOK],
                                                  bias[:, m - 8, s0:s0 + 8, :].rearrange("p r c -> p (r c)"), ALU.add)
                                dve.drain()
                            dve.tensor_reduce(stat[:, 0, m:m + 1], pr(m % 2)[:, 0:nk], AX_X, ALU.max, negate=True
                                              ).then_inc(mx_ready.sem, 1)
                    if head(g - 4) and head(g - 4)[2] == HDS - 1:
                        ti, tile = head(g - 4)[:2]
                        dve.wait_ge(*ot_hi(l, ti + 1))
                        if ti == 0:
                            dve.wait_ge(*own_out(l, 6 * 16))
                        dve.tensor_tensor(oTlo[:, :, tile * P:(tile + 1) * P],
                                          PS[:, 2, 0:768].rearrange("p (c n) -> p c n", c=6),
                                          oThi[:, :, tile * P:(tile + 1) * P], ALU.subtract).then_inc(ot_ready.sem, 1)
                    if head(g):
                        ti, tile, hd, ms = head(g)
                        nk = TOK if tile else P
                        m, nm = ms[0], len(ms)
                        dve.wait_ge(*ex_ready(l, ti * MAPS + m + nm))
                        dve.reciprocal(stat[:, 2, m:m + nm], stat[:, 1, m:m + nm]).then_inc(rec_ready.sem, 1)
                        if hd < 4:
                            dve.drain()
                            dve.scalar_tensor_tensor(out=cfa[:, 0, hd:hd + 1], in0=stat[:, 1, m:m + 1],
                                                     scalar=nlam, in1=stat[:, 2, m + 1:m + 2],
                                                     op0=ALU.mult, op1=ALU.mult)
                            dve.drain()
                            if hd >= 2:
                                dve.wait_ge(*pt_done(l, ti * HDS + hd - 1))
                            dve.scalar_tensor_tensor(out=wmix[:, hd % 2, 0:nk], in0=ex[:, (m + 1) % 4, 0:nk],
                                                     scalar=cfa[:, 0, hd:hd + 1], in1=ex[:, m % 4, 0:nk],
                                                     op0=ALU.mult, op1=ALU.add).then_inc(mix_ready.sem, 1)
                    if head(g - 2) and head(g - 2)[2] in (5, 7):
                        ti, _, hd, _ = head(g - 2)
                        oa = otok[:, ti % 2, 0:256].rearrange("p (h n) -> p h n", h=4)
                        if hd == 5:
                            dve.wait_ge(*o_ready(l, ti * HDS + 4))
                            dve.tensor_tensor(osq, otok[:, ti % 2, 0:256], otok[:, ti % 2, 0:256], ALU.mult)
                            dve.drain()
                            dve.tensor_reduce(ostat[:, 2, :], osq.rearrange("p (h n) -> p h n", h=4), AX_X, ALU.add)
                            dve.drain()
                            dve.tensor_scalar(ostat[:, 0, :], ostat[:, 2, :], 1.0 / 64, EPS, ALU.mult, ALU.add
                                              ).then_inc(ovar_ready.sem, 1)
                        else:
                            dve.wait_ge(*ostd_ready(l, ti + 1))
                            dve.reciprocal(ostat[:, 2, :], ostat[:, 1, :])
                            dve.drain()
                            dve.tensor_tensor(oa, oa, bc(ostat[:, 2, :].rearrange("p (h o) -> p h o", o=1), [P, 4, 64]),
                                              ALU.mult)
                            dve.drain()
                            dve.tensor_tensor(oa, oa, bc(rowg[:, 0:64].rearrange("p (o n) -> p o n", o=1), [P, 4, 64]),
                                              ALU.mult).then_inc(on_ready.sem, 1)
                for b in range(WO_UNITS):
                    if b < 2:
                        dve.wait_ge(w_hi.sem, l * V_ALL + (V_WO + b + 1))
                    else:
                        dve.wait_ge(*x_hi(l, b - 1))
                    whole = [w[:, b, :, :].rearrange("p k n -> p (k n)") for w in (wohi, wolo)]
                    src = wf[b] if b < 2 else wox[b - 2]
                    dve.tensor_tensor(whole[1][:, 640:2048], src[:, 640:2048], whole[0][:, 640:2048], ALU.subtract
                                      ).then_inc(wo_lo.sem, 1)
                with dve.Fori(0, KC // 2) as d2:
                    for b in range(4):
                        for c in range(2):
                            dve.drain()
                            dve.wait_ge(*b_done(l, d2 * 8 + (2 * b + c + 1)))
                            dve.wait_ge(*g_ready(l, d2 * 8 + (2 * b + c + 1)))
                            dst = mt[:, c, :] if b else macc[:, c, :]
                            dve.tensor_tensor(dst, pr(2 + c), sg[:, c, :], ALU.mult).then_inc(m_used.sem, 1)
                            if b:
                                dve.drain()
                                ins = dve.tensor_tensor(macc[:, c, :], macc[:, c, :], mt[:, c, :], ALU.add)
                            if b == 3:
                                ins.then_inc(m_ready.sem, 1)
                    for c in range(2):
                        dve.wait_ge(*m_hi(l, d2 * 2 + (c + 1)))
                        dve.tensor_tensor(mlo[:, ds(d2 * 2 + c, 1), :].rearrange("p o n -> p (o n)"), macc[:, c, :],
                                          mhi[:, ds(d2 * 2 + c, 1), :].rearrange("p o n -> p (o n)"), ALU.subtract
                                          ).then_inc(m_split.sem, 1)

                def residual(k, pair, gate, ready):
                    for s, (a, b) in enumerate(SEG):
                        xk = xT[:, k, a:b]
                        ins = dve.scalar_tensor_tensor(out=xk, in0=pr(pair)[:, a:b],
                                                       scalar=ada[:, k + gate, s:s + 1],
                                                       in1=xk, op0=ALU.mult, op1=ALU.add)
                    ins.then_inc(ready.sem, 1)

                for k in range(KC):
                    dve.wait_ge(*y_done(l, k + 1))
                    residual(k, k % 2, 16, x1_ready)
                root(l, 1)
                norm(l, 1)
                dve.wait_ge(started.sem, 1)
                dve.wait_ge(*base_ready(l, 1))
                b, ran, done = ran_before(dve)

                def part_low(c, j, q):
                    dve.wait_ge(mw_hi.sem, b * 6 + (c * 3 + (q + 1)))
                    dve.tensor_tensor(mwlo[3 * j + q], mwf[3 * j + q], mwhi[3 * j + q], ALU.subtract).then_inc(mw_lo.sem, 1)

                dve.drain()
                dve.wait_ge(*hf_used(l, KC))
                dve.tensor_scalar(lgT, pr(3)[0:20, :], rbias[:, 0:1], None, ALU.add).then_inc(lg_ready.sem, 1)
                dve.wait_ge(*lgt_done(l, 1))
                dve.tensor_copy(route[:, :, :], bank(4, 100).rearrange("p (t n) -> p t n", t=TILES))
                dve.drain()

                def col(n, shape):
                    return bc(rcol[:, n, :].rearrange("p (t o) -> p t o", o=1), shape)

                T4 = [P, TILES, 4]

                def first_max(src, out, n):
                    dve.tensor_reduce(rcol[:, n, :], src, AX_X, ALU.max)
                    dve.drain()
                    dve.tensor_tensor(out, src, col(n, T4), ALU.is_equal)
                    dve.drain()
                    dve.tensor_tensor(out, out, bc(tie[:, :].rearrange("p (o n) -> p o n", o=1), T4), ALU.mult)
                    dve.drain()
                    dve.tensor_reduce(rcol[:, 7, :], out, AX_X, ALU.max)
                    dve.drain()
                    dve.tensor_tensor(out, out, col(7, T4), ALU.is_equal)
                    dve.drain()

                lg = route[:, :, 0:4]
                oh, oh1, oh2, sel, sel2 = (rw[:, :, 16 + 4 * q:20 + 4 * q] for q in range(5))
                first_max(lg, oh, 0)
                dve.tensor_tensor(ex5[:, :, 0:4], lg, col(0, T4), ALU.subtract)
                w16 = rw[:, :, 0:16].rearrange("p t (g e) -> p t g e", g=4)
                for g in range(4):
                    dve.tensor_tensor(rw[:, :, 4 * g:4 * g + 4], route[:, :, 4 + 4 * g:8 + 4 * g],
                                      bc(oh[:, :, g:g + 1], T4), ALU.mult)
                dve.drain()
                dve.tensor_reduce(sel, rw[:, :, 0:16].rearrange("p t (g e) -> p t e g", g=4), AX_X, ALU.add)
                dve.drain()
                first_max(sel, oh1, 1)
                dve.scalar_tensor_tensor(out=sel2, in0=oh1, scalar=NEG, in1=sel, op0=ALU.mult, op1=ALU.add)
                dve.drain()
                first_max(sel2, oh2, 2)
                dve.tensor_tensor(ex5[:, :, 4], rcol[:, 2, :], rcol[:, 1, :], ALU.subtract).then_inc(rmax_ready.sem, 1)
                dve.wait_ge(*rexp_ready(l, 1))
                dve.tensor_reduce(rcol[:, 3, :], ex5[:, :, 0:4], AX_X, ALU.add)
                dve.tensor_scalar(rcol[:, 4, :], ex5[:, :, 4], 1.0, None, ALU.add)
                dve.drain()
                dve.tensor_tensor(rcol[:, 5, :], rcol[:, 3, :], rcol[:, 4, :], ALU.mult)
                dve.drain()
                dve.reciprocal(rcol[:, 3, :], rcol[:, 5, :])
                dve.drain()
                dve.tensor_tensor(rcol[:, 4, :], rcol[:, 3, :], ex5[:, :, 4], ALU.mult)
                dve.drain()
                for n in (3, 4):
                    dve.tensor_scalar(rcol[:, n + 2, :], rcol[:, n, :], 1.0 / A_SCALE, None, ALU.mult)
                for ch, o in enumerate((oh1, oh2)):
                    for g in range(4):
                        dve.tensor_tensor(ohm[:, 5 * ch:5 * ch + 5, 4 * g:4 * g + 4], o, bc(oh[:, :, g:g + 1], T4), ALU.mult)
                dve.drain()
                dve.tensor_tensor(cum, ohm[:, 0:5, :], ohm[:, 5:10, :], ALU.add).then_inc(hot_ready.sem, 1)
                dve.wait_ge(*cnt_done(l, 1))
                dve.wait_ge(*route_in(l, 16))
                dve.memset(acc[:, 0, :], 0.0)
                for cs in csum:
                    dve.memset(cs[:, 0:8], 0.0)
                dve.drain()
                for tile in range(TILES):
                    dve.tensor_tensor(acc[:, tile + 1, :], acc[:, tile, :], bank(4)[:, 256 + 16 * tile:272 + 16 * tile],
                                      ALU.add)
                    dve.drain()
                dve.tensor_tensor(cum, bank(4)[:, 128:208].rearrange("p (t e) -> p t e", t=TILES), acc[:, 0:5, :], ALU.add)

                def flat(ap):
                    return ap.rearrange("p a b -> p (a b)")

                def count(out, left, right, op, a, b):
                    tb = tbl[:, 0:a * b].rearrange("p (a b) -> p a b", a=a)
                    dve.tensor_tensor(tb, bc(left.rearrange("p (a o) -> p a o", o=1), [P, a, b]),
                                      bc(right.rearrange("p (o b) -> p o b", o=1), [P, a, b]), op)
                    dve.drain()
                    dve.tensor_reduce(out, tb, AX_X, ALU.add)
                    dve.drain()

                count(nch, acc[:, 5, :], steps[:, 1:5], ALU.is_gt, EXPERTS, 4)
                dve.tensor_copy(csum[0][:, 8:24], nch)
                dve.drain()
                for n, sh in enumerate((1, 2, 4, 8)):
                    a, o = csum[n % 2], csum[1 - n % 2]
                    dve.tensor_tensor(o[:, 8:24], a[:, 8:24], a[:, 8 - sh:24 - sh], ALU.add)
                    dve.drain()
                incl = csum[0][:, 8:24]
                dve.tensor_tensor(first, incl, nch, ALU.subtract)
                dve.drain()
                dve.tensor_scalar(incl, incl, float(EXPERTS), None, ALU.add)
                for n, (ch, by) in enumerate((ch, by) for by in range(3) for ch in range(2)):
                    tb = tbl[:, 80 * n:80 * n + 80].rearrange("p (t e) -> p t e", t=TILES)
                    row16 = (None, first, iota[:, 0:EXPERTS])[by]
                    by16 = cum if by == 0 else bc(row16.rearrange("p (o e) -> p o e", o=1), [P, TILES, EXPERTS])
                    dve.tensor_tensor(tb, ohm[:, 5 * ch:5 * ch + 5, :], by16, ALU.mult)
                dve.drain()
                dve.tensor_reduce(rsel[:, 0:3, :].rearrange("p a b -> p (a b)"), tbl[:, 0:480].rearrange("p (n e) -> p n e", n=30),
                                  AX_X, ALU.add)
                dve.drain()
                rank, extra, expert = rsel[:, 0, :], rsel[:, 1, :], rsel[:, 2, :]
                whole, row, chunk = rsel[:, 4, :], rsel[:, 5, :], rsel[:, 6, :]
                count(whole, rank, steps[:, 1:5], ALU.is_ge, 10, 4)
                dve.scalar_tensor_tensor(out=row, in0=whole, scalar=-float(P), in1=rank, op0=ALU.mult, op1=ALU.add)
                dve.tensor_scalar(rsel[:, 3, :], whole, 0.0, None, ALU.is_equal)
                dve.tensor_tensor(extra, whole, extra, ALU.add)
                dve.drain()
                dve.tensor_scalar(extra, extra, float(EXPERTS - 1), None, ALU.add)
                dve.drain()
                dve.tensor_tensor(expert, expert, extra, ALU.subtract)
                dve.drain()
                dve.tensor_tensor(expert, expert, rsel[:, 3, :], ALU.mult)
                dve.drain()
                dve.tensor_tensor(chunk, expert, extra, ALU.add)
                dve.drain()
                dve.scalar_tensor_tensor(out=slotf[:, :], in0=chunk, scalar=float(P), in1=row, op0=ALU.mult, op1=ALU.add)
                for n in range(10):
                    dve.tensor_scalar(rowhot[:, n, :], iota, row[:, n:n + 1], None, ALU.is_equal)
                    ins = dve.tensor_scalar(chhot[:, n, :], iota[:, 0:CHUNKS + 2], chunk[:, n:n + 1],
                                            tokid[:, n % 5:n % 5 + 1], ALU.is_equal, ALU.mult)
                ins.then_inc(place_ready.sem, 1)
                count(cef, iota[:, 0:CHUNKS + 1], incl, ALU.is_ge, CHUNKS + 1, EXPERTS)
                dve.tensor_scalar(cexp[:, :], cef, float(EXPERTS - 1), None, ALU.min)
                dve.drain()
                dve.tensor_copy(cexp[:, 0:EXPERTS], iota[:, 0:EXPERTS])
                count(loopf[:, 1:2], incl[:, 15:16], iota[:, 1:CHUNKS + 1:2], ALU.is_gt, 1, PAIRS + 1)
                dve.tensor_copy(loopi[:, 1:2], loopf[:, 1:2])
                dve.wait_ge(*list_done(l, 1))
                dve.tensor_copy(idxall, bank(5, CHUNKS + 2)).then_inc(route_ready.sem, 1)
                dve.wait_ge(started.sem, 1)
                dve.wait_ge(*route_ready(l, 1))
                m = pairs_now(dve)

                def rows_low(c, j):
                    dve.wait_ge(hs_hi.sem, b * 2 + (c + 1))
                    dve.tensor_tensor(hslo[j], PS[:, 0, :].rearrange("p (k n) -> p k n", k=KC), hshi[j], ALU.subtract
                                      ).then_inc(hs_ready.sem, 1)

                def multiply(c, j, first=False):
                    dve.wait_ge(msilu_ready.sem, done + (c + 1))
                    if not first:
                        dve.wait_ge(at_done.sem, done + (c - 1))
                    dve.tensor_tensor(mact[j], msg[j], bank(2 + j)[:, 256:512], ALU.mult).then_inc(mact_ready.sem, 1)

                def act_low(c, j):
                    dve.wait_ge(at_hi.sem, done + (c + 1))
                    dve.scalar_tensor_tensor(out=atlo[j], in0=bank(4 + j, 256).rearrange("p (c n) -> p c n", c=2),
                                             scalar=A_SCALE, in1=athi[j], op0=ALU.mult, op1=ALU.subtract
                                             ).then_inc(at_ready.sem, 1)

                for q in range(2):
                    part_low(0, 0, q)
                rows_low(0, 0)
                for q in range(2):
                    part_low(1, 1, q)
                multiply(0, 0, True)
                rows_low(1, 1)
                act_low(0, 0)
                with dve.Fori(0, m) as i:
                    for n in range(2):
                        c, j = i * 2 + (1 + n), 1 - n
                        for q in range(2):
                            part_low(i * 2 + (2 + n), n, q)
                        multiply(c, j)
                        rows_low(i * 2 + (2 + n), n)
                        act_low(c, j)
                for tile in range(TILES):
                    dve.drain()
                    dve.wait_ge(*cg_in[tile](l, 32))
                    if tile >= 2:
                        dve.wait_ge(*yt_done(l, tile - 1))
                    dve.tensor_scalar(cga[:, tile, :], cga[:, tile, :], rcol[:, 5, tile:tile + 1], None, ALU.mult)
                    dve.drain()
                    dve.scalar_tensor_tensor(out=ybuf[tile % 2], in0=cgb[:, tile, :], scalar=rcol[:, 6, tile:tile + 1],
                                             in1=cga[:, tile, :], op0=ALU.mult, op1=ALU.add).then_inc(comb_ready.sem, 1)
                    dve.wait_ge(*yt_done(l, tile + 1))
                    s = 0 if tile == 0 else 1
                    xk = xT[:, :, tile * P:(tile + 1) * P]
                    yk = PS[:, tile % 2, :].rearrange("p (k n) -> p k n", k=KC)
                    dve.tensor_tensor(cga[:, tile, :].rearrange("p (k n) -> p k n", k=KC), yk,
                                      bc(ada[:, 40:48, s:s + 1], [P, KC, P]), ALU.mult)
                    dve.drain()
                    dve.tensor_tensor(xk, xk, cga[:, tile, :].rearrange("p (k n) -> p k n", k=KC), ALU.add
                                      ).then_inc(x2_ready.sem, 1)
            root(LAYERS, 0)
            for k in range(KC):
                if k >= 2:
                    dve.wait_ge(*fin_t(0, k - 1))
                dve.scalar_tensor_tensor(out=tmp[:, k % 2, :], in0=xT[:, k, :], scalar=gfin[:, k:k + 1], in1=rsb[:, :],
                                         op0=ALU.mult, op1=ALU.mult).then_inc(fin_ready.sem, 1)


_INS = ['x_prompt', 'x_sample', 'cache_a_k', 'cache_a_v', 'cache_b_k', 'cache_b_v', 'cache_c_kv', 'cache_c_krope',
        'c', 'c_ctx', 'norm1_g', 'norm2_g', 'w_ada', 'b_ada', 'w_in', 'a_lambda', 'a_subln_g', 'a_wo', 'b_rpb', 'b_wo',
        'c_q_norm_g', 'c_kv_norm_g', 'c_wuq', 'c_wukv', 'c_wo', 'd_conv_w', 'd_conv_b', 'd_ln_g', 'd_ln_b', 'd_wo',
        'w_gate', 'b_gate', 'w_out', 'moe_w_group', 'moe_b_group', 'moe_w_expert', 'moe_b_expert', 'moe_w1', 'moe_w2',
        'final_norm_g']
_OUTS = [('y_prompt', (1, 128, 1024)), ('y_sample', (1, 512, 1024)), ('new_a_k', (1, 2, 128, 4, 64)),
         ('new_a_v', (1, 2, 128, 4, 64)), ('new_b_k', (1, 2, 128, 4, 64)), ('new_b_v', (1, 2, 128, 4, 64)),
         ('new_c_kv', (1, 2, 128, 128)), ('new_c_krope', (1, 2, 128, 32))]


def shape_constants():
    f = np.float32
    h = 8
    tok = np.arange(LAT)
    inv = (f(10000.0) ** (-np.arange(h, dtype=f) / f(h))).astype(f)
    ar = (tok // GRID_W).astype(f)[:, None] * inv[None, :]
    ac = (tok % GRID_W).astype(f)[:, None] * inv[None, :]
    ang = np.concatenate([ar, ar, ac, ac], axis=-1)
    sign = np.repeat(np.array([-1, 1, -1, 1], dtype=f), h)
    cos = np.cos(ang).astype(f).reshape(4, P, 32).transpose(1, 0, 2)
    sin = (np.sin(ang).astype(f) * sign).reshape(4, P, 32).transpose(1, 0, 2)
    q = np.arange(P) % GRID_W
    start = np.clip(q - 8, 0, GRID_W - 16)[:, None]
    k = np.arange(GRID_W)[None, :]
    mask = np.where((k >= start) & (k < start + 16), 0.0, NEG).astype(f)
    j, w = np.arange(31)[:, None], np.arange(207)[None, :]
    band = ((w + j == 94) | (w + j == 94 + 64)).astype(f)
    init = [0.8 - 0.6 * math.exp(-0.3 * layer) for layer in range(LAYERS)]
    return {
        'k_ident': np.eye(P, dtype=f), 'k_cos': np.ascontiguousarray(cos), 'k_sin': np.ascontiguousarray(sin),
        'k_mask': mask, 'k_band': band, 'k_tie': np.tile(np.array([4, 3, 2, 1], dtype=f), (P, 1)),
        'k_route': np.concatenate([np.tile(np.arange(P), (P, 1)), np.triu(np.ones((P, P)), 1),
                                   np.arange(P)[:, None] + P * np.arange(TILES)[None, :],
                                   np.tile(P * np.arange(5), (P, 1))], axis=1).astype(f),
        'k_lam': np.array([[x, 1.0 - x] for x in init], dtype=f),
    }


def kernel(**inputs):
    import numpy as _np
    import concourse.bacc as _bacc
    from concourse.bass_utils import run_bass_kernel_spmd as _run

    nc = _bacc.Bacc("TRN2", target_bir_lowering=False, num_devices=1)
    arrays, aps = {}, {}
    given = {name: _np.ascontiguousarray(inputs[name]) for name in _INS}
    for name, a in {**given, **shape_constants()}.items():
        arrays[f"in_{name}"] = a
        aps[name] = nc.dram_tensor(f"in_{name}", a.shape, mybir.dt.from_np(a.dtype), kind="ExternalInput").ap()
    for name, shape in _OUTS:
        aps[name] = nc.dram_tensor(f"out_{name}", shape, F32, kind="ExternalOutput").ap()
    aps["h2_rows"] = nc.dram_tensor("h2_rows", [TOK, D], F32, kind="Internal").ap()
    aps["y_rows"] = nc.dram_tensor("y_rows", [CHUNKS * P, D], F32, kind="Internal").ap()
    build(nc, aps)
    r = _run(nc, [arrays], core_ids=[0])
    return tuple(r.results[0][f"out_{name}"] for name, _ in _OUTS)
```
